# Optimizing a Trainium2 kernel written in Bass

```python
import math
import jax
import jax.numpy as jnp
from jax import lax
import numpy as np

D_MODEL = 1024
BATCH = 1
SEQ = 256
DEPTH = 2

CHUNK = 64
D_FF = 4096
LN_EPS = 1e-5
NORM_EPS = 1e-6
H_A = 4
DK_A = 128
DV_A = 128
CONV_K = 4
A_QK = H_A * DK_A
A_V = H_A * DV_A
H_B = 4
D_B = 128
B_PREV = 8
REL_CLIP = 128
B_W = H_B * D_B
H_C = 8
HKV_C = 2
G_C = H_C // HKV_C
D_C = 64
WINDOW = 128
C_PREV = WINDOW // CHUNK
C_Q = H_C * D_C
C_KV = HKV_C * D_C
N_BRANCH = 3
IN_SPLITS = (A_QK, A_QK, A_V, H_A, H_A, A_V, B_W, B_W, B_W, C_Q, C_KV, C_KV)
D_IN = sum(IN_SPLITS)


def layer_norm(x, g, b):
    xf = x.astype(jnp.float32)
    mu = jnp.mean(xf, -1, keepdims=True)
    xc = xf - mu
    var = jnp.mean(xc * xc, -1, keepdims=True)
    return (xc * lax.rsqrt(var + LN_EPS) * g.astype(jnp.float32) + b.astype(jnp.float32)).astype(x.dtype)

def swiglu(x, w_in, w_out):
    gate, up = jnp.split(x @ w_in, 2, axis=-1)
    return (jax.nn.silu(gate) * up) @ w_out

def causal_depthwise_conv(x, w):
    k = w.shape[0]
    return lax.conv_general_dilated(x, w[:, None, :], window_strides=(1,), padding=[(k - 1, 0)],
                                    dimension_numbers=('NWC', 'WIO', 'NWC'),
                                    feature_group_count=x.shape[-1])

def l2_normalize(x):
    return x * lax.rsqrt(jnp.sum(x * x, -1, keepdims=True) + NORM_EPS)

def to_chunks(a):
    b, t, h = a.shape[:3]
    a = a.reshape(b, t // CHUNK, CHUNK, h, *a.shape[3:])
    return jnp.moveaxis(a, (1, 3), (0, 2))

def chunk_gated_delta_rule(q, k, v, g, beta):
    b, t, h, dk = q.shape
    dv = v.shape[-1]
    q = to_chunks(q) * (dk ** -0.5)
    k = to_chunks(k)
    v = to_chunks(v)
    g = to_chunks(g)
    beta = to_chunks(beta)
    g_cum = jnp.cumsum(g, axis=-1)
    idx = jnp.arange(CHUNK)
    causal = idx[:, None] >= idx[None, :]
    strict = idx[:, None] > idx[None, :]
    decay = jnp.exp(jnp.where(causal, g_cum[..., :, None] - g_cum[..., None, :], -jnp.inf))
    k_beta = k * beta[..., None]
    lower = jnp.where(strict, jnp.einsum('nbhid,nbhjd->nbhij', k_beta, k) * decay, 0.0)
    eye = jnp.eye(CHUNK, dtype=jnp.float32)
    rhs = jnp.concatenate([v * beta[..., None], k_beta * jnp.exp(g_cum)[..., None]], axis=-1)
    uw = lax.linalg.triangular_solve(eye + lower, rhs, left_side=True, lower=True, unit_diagonal=True)
    u, w = uw[..., :dv], uw[..., dv:]
    attn = jnp.einsum('nbhid,nbhjd->nbhij', q, k) * decay
    q_dec = q * jnp.exp(g_cum)[..., None]
    g_last = g_cum[..., -1]
    k_dec = k * jnp.exp(g_last[..., None] - g_cum)[..., None]

    def step(state, inp):
        q_c, k_c, u_c, w_c, a_c, gl_c = inp
        v_new = u_c - jnp.einsum('bhcd,bhdv->bhcv', w_c, state)
        o_c = jnp.einsum('bhcd,bhdv->bhcv', q_c, state) + jnp.einsum('bhij,bhjv->bhiv', a_c, v_new)
        state = state * jnp.exp(gl_c)[..., None, None] + jnp.einsum('bhcd,bhcv->bhdv', k_c, v_new)
        return state, o_c

    s0 = jnp.zeros((b, h, dk, dv), jnp.float32)
    _, o = lax.scan(step, s0, (q_dec, k_dec, u, w, attn, g_last))
    o = jnp.moveaxis(o, (0, 2), (1, 3))
    return o.reshape(b, t, h, dv)

def gated_deltanet(qa, ka, va, beta_raw, a_raw, za, conv_w, a_log, dt_bias, norm_g):
    b, t, _ = qa.shape
    f32 = jnp.float32
    qkv = jax.nn.silu(causal_depthwise_conv(jnp.concatenate([qa, ka, va], -1), conv_w)).astype(f32)
    q, k, v = jnp.split(qkv, [A_QK, 2 * A_QK], axis=-1)
    q = l2_normalize(q.reshape(b, t, H_A, DK_A))
    k = l2_normalize(k.reshape(b, t, H_A, DK_A))
    v = v.reshape(b, t, H_A, DV_A)
    beta = jax.nn.sigmoid(beta_raw.astype(f32))
    g = -jnp.exp(a_log.astype(f32)) * jax.nn.softplus(a_raw.astype(f32) + dt_bias.astype(f32))
    o = chunk_gated_delta_rule(q, k, v, g, beta)
    z = za.reshape(b, t, H_A, DV_A).astype(f32)
    o = o * lax.rsqrt(jnp.mean(o * o, -1, keepdims=True) + NORM_EPS) * norm_g.astype(f32) * jax.nn.silu(z)
    return o.reshape(b, t, A_V).astype(qa.dtype)

def chunk_band(a, n_prev):
    b, t = a.shape[:2]
    n = t // CHUNK
    pad = [(0, 0), (n_prev * CHUNK, 0)] + [(0, 0)] * (a.ndim - 2)
    ap = jnp.pad(a, pad).reshape(b, n + n_prev, CHUNK, *a.shape[2:])
    band = jnp.stack([ap[:, j:j + n] for j in range(n_prev + 1)], axis=2)
    return band.reshape(b, n, (n_prev + 1) * CHUNK, *a.shape[2:])

def band_geometry(n, n_prev):
    i = jnp.arange(CHUNK)
    j = jnp.arange((n_prev + 1) * CHUNK)
    dist = n_prev * CHUNK + i[:, None] - j[None, :]
    valid = (jnp.arange(n)[:, None] - n_prev + j[None, :] // CHUNK) >= 0
    return dist, valid

def alibi_slopes(n):
    return 2.0 ** (-8.0 * jnp.arange(1, n + 1, dtype=jnp.float32) / n)

def chunk_relpos_attention(q, k, v, rel_bias):
    b, t, _ = q.shape
    n = t // CHUNK
    q = q.reshape(b, n, CHUNK, H_B, D_B)
    kb = chunk_band(k.reshape(b, t, H_B, D_B), B_PREV)
    vb = chunk_band(v.reshape(b, t, H_B, D_B), B_PREV)
    s = jnp.einsum('bnqhd,bnkhd->bnhqk', q, kb).astype(jnp.float32) * (D_B ** -0.5)
    dist, valid = band_geometry(n, B_PREV)
    rel_idx = jnp.clip(dist, -(CHUNK - 1), REL_CLIP) + (CHUNK - 1)
    bias = rel_bias.astype(jnp.float32)[:, rel_idx]
    s = jnp.where(valid[None, :, None, None, :], s + bias, -jnp.inf)
    p = jax.nn.softmax(s, axis=-1).astype(v.dtype)
    o = jnp.einsum('bnhqk,bnkhd->bnqhd', p, vb)
    return o.reshape(b, t, B_W)

def swa_sink_attention(q, k, v, sinks):
    b, t, _ = q.shape
    n = t // CHUNK
    q = q.reshape(b, n, CHUNK, HKV_C, G_C, D_C)
    kb = chunk_band(k.reshape(b, t, HKV_C, D_C), C_PREV)
    vb = chunk_band(v.reshape(b, t, HKV_C, D_C), C_PREV)
    s = jnp.einsum('bnqhgd,bnkhd->bnhgqk', q, kb).astype(jnp.float32) * (D_C ** -0.5)
    dist, valid = band_geometry(n, C_PREV)
    slopes = alibi_slopes(H_C).reshape(HKV_C, G_C)
    s = s - slopes[:, :, None, None] * jnp.abs(dist).astype(jnp.float32)
    s = jnp.where(valid[None, :, None, None, None, :], s, -jnp.inf)
    sink = jnp.broadcast_to(sinks.astype(jnp.float32).reshape(HKV_C, G_C)[:, :, None, None], s.shape[:-1] + (1,))
    p = jax.nn.softmax(jnp.concatenate([s, sink], axis=-1), axis=-1)[..., :-1].astype(v.dtype)
    o = jnp.einsum('bnhgqk,bnkhd->bnqhgd', p, vb)
    return o.reshape(b, t, C_Q)

def hybrid_mixer(x, w_in, b_in, conv_w, a_log, dt_bias, gdn_norm_g, rel_bias, sinks,
                 w_gate, b_gate, w_br_a, w_br_b, w_br_c, w_out):
    b, t, d = x.shape
    proj = x @ w_in + b_in
    split_at = np.cumsum(IN_SPLITS)[:-1].tolist()
    (qa, ka, va, beta_raw, a_raw, za, qb, kb, vb, qc, kc, vc) = jnp.split(proj, split_at, axis=-1)
    o_a = gated_deltanet(qa, ka, va, beta_raw, a_raw, za, conv_w, a_log, dt_bias, gdn_norm_g)
    o_b = chunk_relpos_attention(qb, kb, vb, rel_bias)
    o_c = swa_sink_attention(qc, kc, vc, sinks)
    gates = jax.nn.sigmoid(x @ w_gate + b_gate).reshape(b, t, N_BRANCH, d)
    merged = (gates[:, :, 0] * (o_a @ w_br_a) + gates[:, :, 1] * (o_b @ w_br_b)
              + gates[:, :, 2] * (o_c @ w_br_c))
    return merged @ w_out

def first_inputs(seed: int = 0) -> dict:
    key = jax.random.key(seed)
    keys = list(jax.random.split(key, 32))
    f32 = jnp.float32
    L, D = DEPTH, D_MODEL
    sub_scale = (8.0 * DEPTH) ** -0.25

    def nrm(shape, scale):
        return jax.random.normal(keys.pop(), shape, f32) * scale

    def gain(shape):
        return 1.0 + nrm(shape, 0.02)

    x = nrm((BATCH, SEQ, D), 1.0)
    ln1_g = gain((L, D))
    ln1_b = nrm((L, D), 0.02)
    w_ff1_in = nrm((L, D, 2 * D_FF), D ** -0.5)
    w_ff1_out = nrm((L, D_FF, D), D_FF ** -0.5 * sub_scale)
    w_in = nrm((L, D, D_IN), D ** -0.5)
    b_in = nrm((L, D_IN), 0.02)
    conv_w = nrm((L, CONV_K, 2 * A_QK + A_V), CONV_K ** -0.5)
    a_log = jnp.log(jax.random.uniform(keys.pop(), (L, H_A), f32, 1.0, 16.0))
    dt = jnp.exp(jax.random.uniform(keys.pop(), (L, H_A), f32, math.log(1e-3), math.log(1e-1)))
    dt_bias = dt + jnp.log(-jnp.expm1(-dt))
    gdn_norm_g = gain((L, DV_A))
    rel_bias = nrm((L, H_B, CHUNK + REL_CLIP), 0.1)
    sinks = nrm((L, H_C), 0.5)
    w_gate = nrm((L, D, N_BRANCH * D), D ** -0.5)
    b_gate = nrm((L, N_BRANCH * D), 0.02)
    w_br_a = nrm((L, A_V, D), A_V ** -0.5 * sub_scale)
    w_br_b = nrm((L, B_W, D), B_W ** -0.5 * sub_scale)
    w_br_c = nrm((L, C_Q, D), C_Q ** -0.5 * sub_scale)
    w_out = nrm((L, D, D), D ** -0.5 * sub_scale)
    ln2_g = gain((L, D))
    ln2_b = nrm((L, D), 0.02)
    w_ff2_in = nrm((L, D, 2 * D_FF), D ** -0.5)
    w_ff2_out = nrm((L, D_FF, D), D_FF ** -0.5 * sub_scale)
    ln3_g = gain((L, D))
    ln3_b = nrm((L, D), 0.02)
    return {'x': x, 'ln1_g': ln1_g, 'ln1_b': ln1_b, 'w_ff1_in': w_ff1_in, 'w_ff1_out': w_ff1_out,
            'w_in': w_in, 'b_in': b_in, 'conv_w': conv_w, 'a_log': a_log, 'dt_bias': dt_bias,
            'gdn_norm_g': gdn_norm_g, 'rel_bias': rel_bias, 'sinks': sinks, 'w_gate': w_gate,
            'b_gate': b_gate, 'w_br_a': w_br_a, 'w_br_b': w_br_b, 'w_br_c': w_br_c, 'w_out': w_out,
            'ln2_g': ln2_g, 'ln2_b': ln2_b, 'w_ff2_in': w_ff2_in, 'w_ff2_out': w_ff2_out,
            'ln3_g': ln3_g, 'ln3_b': ln3_b}

def first_block(x, ln1_g, ln1_b, w_ff1_in, w_ff1_out, w_in, b_in, conv_w, a_log, dt_bias,
              gdn_norm_g, rel_bias, sinks, w_gate, b_gate, w_br_a, w_br_b, w_br_c, w_out,
              ln2_g, ln2_b, w_ff2_in, w_ff2_out, ln3_g, ln3_b):
    alpha = (2.0 * DEPTH) ** 0.25
    for l in range(DEPTH):
        x = layer_norm(alpha * x + 0.5 * swiglu(x, w_ff1_in[l], w_ff1_out[l]), ln1_g[l], ln1_b[l])
        mix = hybrid_mixer(x, w_in[l], b_in[l], conv_w[l], a_log[l], dt_bias[l], gdn_norm_g[l],
                           rel_bias[l], sinks[l], w_gate[l], b_gate[l], w_br_a[l], w_br_b[l],
                           w_br_c[l], w_out[l])
        x = layer_norm(alpha * x + mix, ln2_g[l], ln2_b[l])
        x = layer_norm(alpha * x + 0.5 * swiglu(x, w_ff2_in[l], w_ff2_out[l]), ln3_g[l], ln3_b[l])
    return x


N_EVEN = (DEPTH + 1) // 2
N_ODD = DEPTH // 2
EPS = 1e-6
ROPE_THETA = 10000.0

D_FF_2 = -(-(8 * D_MODEL) // (3 * 256)) * 256

CONV_WIDTH = D_MODEL // 2
POOL_WIDTH = D_MODEL - CONV_WIDTH
POOL_WINDOWS = (2, 4, 8, 16)
POOL_GROUP = POOL_WIDTH // len(POOL_WINDOWS)
SHORT_CONV_K = 3
EVEN_IN = 3 * CONV_WIDTH + POOL_WIDTH

HEAD_DIM = 64
NSA_WIDTH = D_MODEL // 2
NSA_HEADS = NSA_WIDTH // HEAD_DIM
NSA_KV_GROUPS = 2
GROUP_SIZE = NSA_HEADS // NSA_KV_GROUPS
KV_WIDTH = NSA_KV_GROUPS * HEAD_DIM
CMP_BLOCK = 32
CMP_STRIDE = 16
CMP_HIDDEN = 4 * HEAD_DIM
SEL_BLOCK = 64
N_SELECT = 8
WINDOW_2 = 512
Q_BLOCK = 128
FORCE_SCORE = 1e4
NEG = -1e30
TINY = 1e-30
CONF_WIDTH = D_MODEL - NSA_WIDTH
CONF_K = 31
ODD_PARTS = (NSA_WIDTH, KV_WIDTH, KV_WIDTH, KV_WIDTH, KV_WIDTH, KV_WIDTH, KV_WIDTH,
             3 * NSA_HEADS, 2 * CONF_WIDTH)
ODD_IN = sum(ODD_PARTS)


def rms_norm(x, g):
    xf = x.astype(jnp.float32)
    y = xf * lax.rsqrt(jnp.mean(xf * xf, axis=-1, keepdims=True) + EPS)
    return (y * g.astype(jnp.float32)).astype(x.dtype)

def layer_norm_2(x, g, b):
    xf = x.astype(jnp.float32)
    mu = jnp.mean(xf, axis=-1, keepdims=True)
    var = jnp.mean(jnp.square(xf - mu), axis=-1, keepdims=True)
    y = (xf - mu) * lax.rsqrt(var + EPS)
    return (y * g.astype(jnp.float32) + b.astype(jnp.float32)).astype(x.dtype)

def rope_tables(seq_len):
    inv = 1.0 / (ROPE_THETA ** (jnp.arange(0, HEAD_DIM, 2, dtype=jnp.float32) / HEAD_DIM))
    ang = jnp.arange(seq_len, dtype=jnp.float32)[:, None] * inv[None, :]
    return jnp.cos(ang), jnp.sin(ang)

def apply_rope(x, cos, sin):
    xf = x.astype(jnp.float32)
    x1, x2 = jnp.split(xf, 2, axis=-1)
    c = cos[None, :, None, :]
    s = sin[None, :, None, :]
    return jnp.concatenate([x1 * c - x2 * s, x2 * c + x1 * s], axis=-1).astype(x.dtype)

def causal_dwconv(x, w):
    k, c = w.shape
    return lax.conv_general_dilated(
        x, w[:, None, :].astype(x.dtype), window_strides=(1,), padding=[(k - 1, 0)],
        dimension_numbers=('NWC', 'WIO', 'NWC'), feature_group_count=c)

def masked_softmax(s, mask):
    s = jnp.where(mask, s.astype(jnp.float32), NEG)
    m = jnp.max(s, axis=-1, keepdims=True)
    e = jnp.where(mask, jnp.exp(s - m), 0.0)
    return e / jnp.maximum(jnp.sum(e, axis=-1, keepdims=True), TINY)

def swiglu_2(h, wg, wu, wd):
    return (jax.nn.silu(h @ wg) * (h @ wu)) @ wd

def multiscale_pool(v, pool_w, pool_scale):
    bsz, t, _ = v.shape
    vg = v.reshape(bsz, t, len(POOL_WINDOWS), POOL_GROUP)
    cs = jnp.cumsum(vg.astype(jnp.float32), axis=1)
    pos = jnp.arange(t)
    means = []
    for gi, w in enumerate(POOL_WINDOWS):
        c = cs[:, :, gi]
        prev = jnp.pad(c, ((0, 0), (w, 0), (0, 0)))[:, :t]
        cnt = jnp.minimum(pos + 1, w).astype(jnp.float32)[None, :, None]
        means.append((c - prev) / cnt)
    pooled = jnp.stack(means, axis=2).astype(v.dtype) - vg
    y = jnp.einsum('btgc,gcd->btgd', pooled, pool_w)
    return y.reshape(bsz, t, POOL_WIDTH) * pool_scale

def short_conv_pool_mixer(h, w_in, conv_w, pool_w, pool_scale, w_out):
    u = h @ w_in
    b_gate, c_gate, v_conv, v_pool = jnp.split(
        u, [CONV_WIDTH, 2 * CONV_WIDTH, 3 * CONV_WIDTH], axis=-1)
    y_conv = b_gate * causal_dwconv(c_gate * v_conv, conv_w)
    y_pool = multiscale_pool(v_pool, pool_w, pool_scale)
    return jnp.concatenate([y_conv, y_pool], axis=-1) @ w_out

def compress_blocks(tok, pos_emb, w1, w2):
    bsz, g, t, dh = tok.shape
    n_cmp = (t - CMP_BLOCK) // CMP_STRIDE + 1
    idx = jnp.arange(n_cmp)[:, None] * CMP_STRIDE + jnp.arange(CMP_BLOCK)[None, :]
    blocks = tok[:, :, idx] + pos_emb
    flat = blocks.reshape(bsz, g, n_cmp, CMP_BLOCK * dh)
    return jax.nn.gelu(flat @ w1) @ w2

def native_sparse_attention(q, k_cmp, v_cmp, k_slc, v_slc, k_win, v_win, gates,
                            q_norm, k_norm, cmp_pos, cmp_w1, cmp_w2, cos, sin):
    bsz, t = q.shape[0], q.shape[1]
    q = apply_rope(rms_norm(q, q_norm), cos, sin)
    ks = apply_rope(rms_norm(k_slc, k_norm[0]), cos, sin)
    kw = apply_rope(rms_norm(k_win, k_norm[1]), cos, sin)
    kc_tok = apply_rope(k_cmp, cos, sin)
    to_bgtd = lambda a: a.transpose(0, 2, 1, 3)
    kc = rms_norm(compress_blocks(to_bgtd(kc_tok), cmp_pos[0], cmp_w1[0], cmp_w2[0]), k_norm[2])
    vc = compress_blocks(to_bgtd(v_cmp), cmp_pos[1], cmp_w1[1], cmp_w2[1])
    ks, vs, kw, vw = to_bgtd(ks), to_bgtd(v_slc), to_bgtd(kw), to_bgtd(v_win)

    q5 = q.reshape(bsz, t, NSA_KV_GROUPS, GROUP_SIZE, HEAD_DIM).transpose(0, 2, 3, 1, 4)
    g5 = gates.reshape(bsz, t, NSA_KV_GROUPS, GROUP_SIZE, 3).transpose(0, 2, 3, 1, 4)

    n_cmp = kc.shape[2]
    n_sb = t // SEL_BLOCK
    n_sel = min(N_SELECT, n_sb)
    cmp_start = jnp.arange(n_cmp) * CMP_STRIDE
    cmp_end = cmp_start + CMP_BLOCK - 1
    sb_start = jnp.arange(n_sb) * SEL_BLOCK
    overlap = ((cmp_start[:, None] < sb_start[None, :] + SEL_BLOCK)
               & (cmp_end[:, None] >= sb_start[None, :])).astype(jnp.float32)
    ks_blocks = ks.reshape(bsz, NSA_KV_GROUPS, n_sb, SEL_BLOCK, HEAD_DIM)
    vs_blocks = vs.reshape(bsz, NSA_KV_GROUPS, n_sb, SEL_BLOCK, HEAD_DIM)
    kw_pad = jnp.pad(kw, ((0, 0), (0, 0), (WINDOW_2, 0), (0, 0)))
    vw_pad = jnp.pad(vw, ((0, 0), (0, 0), (WINDOW_2, 0), (0, 0)))
    bi = jnp.arange(bsz)[:, None, None, None]
    gi = jnp.arange(NSA_KV_GROUPS)[None, :, None, None]
    scale = HEAD_DIM ** -0.5

    def query_block(qb):
        q0 = qb * Q_BLOCK
        qblk = lax.dynamic_slice_in_dim(q5, q0, Q_BLOCK, axis=3)
        gblk = lax.dynamic_slice_in_dim(g5, q0, Q_BLOCK, axis=3)
        pos = q0 + jnp.arange(Q_BLOCK)
        s_c = jnp.einsum('bgrqd,bgnd->bgrqn', qblk, kc).astype(jnp.float32) * scale
        p_cmp = masked_softmax(s_c, cmp_end[None, :] <= pos[:, None])
        o_cmp = jnp.einsum('bgrqn,bgnd->bgrqd', p_cmp.astype(vc.dtype), vc)
        imp = jnp.einsum('bgrqn,nj->bgqj', p_cmp, overlap)
        cur = pos // SEL_BLOCK
        jj = jnp.arange(n_sb)[None, :]
        forced = (jj == 0) | (jj == cur[:, None]) | (jj == cur[:, None] - 1)
        valid = sb_start[None, :] <= pos[:, None]
        score = jnp.where(valid, jnp.where(forced, FORCE_SCORE, imp), -1.0)
        _, top_idx = lax.top_k(score, n_sel)
        k_sel = ks_blocks[bi, gi, top_idx].reshape(bsz, NSA_KV_GROUPS, Q_BLOCK, n_sel * SEL_BLOCK, HEAD_DIM)
        v_sel = vs_blocks[bi, gi, top_idx].reshape(bsz, NSA_KV_GROUPS, Q_BLOCK, n_sel * SEL_BLOCK, HEAD_DIM)
        tok_pos = (top_idx[..., None] * SEL_BLOCK + jnp.arange(SEL_BLOCK)).reshape(
            bsz, NSA_KV_GROUPS, Q_BLOCK, n_sel * SEL_BLOCK)
        sel_mask = (tok_pos <= pos[None, None, :, None])[:, :, None]
        s_s = jnp.einsum('bgrqd,bgqkd->bgrqk', qblk, k_sel).astype(jnp.float32) * scale
        p_s = masked_softmax(s_s, sel_mask)
        o_slc = jnp.einsum('bgrqk,bgqkd->bgrqd', p_s.astype(v_sel.dtype), v_sel)
        k_band = lax.dynamic_slice_in_dim(kw_pad, q0, WINDOW_2 + Q_BLOCK, axis=2)
        v_band = lax.dynamic_slice_in_dim(vw_pad, q0, WINDOW_2 + Q_BLOCK, axis=2)
        kpos = q0 - WINDOW_2 + jnp.arange(WINDOW_2 + Q_BLOCK)
        w_mask = ((kpos[None, :] <= pos[:, None]) & (kpos[None, :] > pos[:, None] - WINDOW_2)
                  & (kpos[None, :] >= 0))
        s_w = jnp.einsum('bgrqd,bgkd->bgrqk', qblk, k_band).astype(jnp.float32) * scale
        p_w = masked_softmax(s_w, w_mask)
        o_win = jnp.einsum('bgrqk,bgkd->bgrqd', p_w.astype(v_band.dtype), v_band)
        return gblk[..., 0:1] * o_cmp + gblk[..., 1:2] * o_slc + gblk[..., 2:3] * o_win

    out = lax.map(query_block, jnp.arange(t // Q_BLOCK))
    return out.transpose(1, 0, 4, 2, 3, 5).reshape(bsz, t, NSA_WIDTH)

def sparse_attn_conformer_mixer(h, w_in, q_norm, k_norm, cmp_pos, cmp_w1, cmp_w2,
                                conf_dw, conf_dw_b, conf_ln_g, conf_ln_b, w_out, cos, sin):
    bsz, t, _ = h.shape
    u = h @ w_in
    offs = []
    acc = 0
    for p in ODD_PARTS[:-1]:
        acc += p
        offs.append(acc)
    q, kc, vc, ks, vs, kw, vw, gt, cf = jnp.split(u, offs, axis=-1)
    heads = lambda a: a.reshape(bsz, t, NSA_HEADS, HEAD_DIM)
    kvs = lambda a: a.reshape(bsz, t, NSA_KV_GROUPS, HEAD_DIM)
    gates = jax.nn.sigmoid(gt).reshape(bsz, t, NSA_HEADS, 3)
    o_nsa = native_sparse_attention(heads(q), kvs(kc), kvs(vc), kvs(ks), kvs(vs), kvs(kw), kvs(vw),
                                    gates, q_norm, k_norm, cmp_pos, cmp_w1, cmp_w2, cos, sin)
    a, b = jnp.split(cf, 2, axis=-1)
    z = a * jax.nn.sigmoid(b)
    z = causal_dwconv(z, conf_dw) + conf_dw_b
    z = jax.nn.silu(layer_norm_2(z, conf_ln_g, conf_ln_b))
    return jnp.concatenate([o_nsa, z], axis=-1) @ w_out

def second_inputs(seed: int = 0) -> dict:
    key = jax.random.key(seed)
    ks = jax.random.split(key, 24)
    nrm = lambda k, shape, s: jax.random.normal(k, shape, jnp.float32) * s
    d = D_MODEL
    return {
        'x': nrm(ks[0], (BATCH, SEQ, d), 1.0),
        'norm_mix': 1.0 + nrm(ks[1], (DEPTH, d), 0.05),
        'norm_ffn': 1.0 + nrm(ks[2], (DEPTH, d), 0.05),
        'ffn_gate': nrm(ks[3], (DEPTH, d, D_FF_2), d ** -0.5),
        'ffn_up': nrm(ks[4], (DEPTH, d, D_FF_2), d ** -0.5),
        'ffn_down': nrm(ks[5], (DEPTH, D_FF_2, d), 0.5 * D_FF_2 ** -0.5),
        'w_in_even': nrm(ks[6], (N_EVEN, d, EVEN_IN), d ** -0.5),
        'conv_a': nrm(ks[7], (N_EVEN, SHORT_CONV_K, CONV_WIDTH), SHORT_CONV_K ** -0.5),
        'pool_w': nrm(ks[8], (N_EVEN, len(POOL_WINDOWS), POOL_GROUP, POOL_GROUP), POOL_GROUP ** -0.5),
        'pool_scale': 1.0 + nrm(ks[9], (N_EVEN, POOL_WIDTH), 0.1),
        'w_out_even': nrm(ks[10], (N_EVEN, d, d), 0.5 * d ** -0.5),
        'w_in_odd': nrm(ks[11], (N_ODD, d, ODD_IN), d ** -0.5),
        'q_norm': 1.0 + nrm(ks[12], (N_ODD, HEAD_DIM), 0.05),
        'k_norm': 1.0 + nrm(ks[13], (N_ODD, 3, HEAD_DIM), 0.05),
        'cmp_pos': nrm(ks[14], (N_ODD, 2, CMP_BLOCK, HEAD_DIM), 0.1),
        'cmp_w1': nrm(ks[15], (N_ODD, 2, CMP_BLOCK * HEAD_DIM, CMP_HIDDEN), (CMP_BLOCK * HEAD_DIM) ** -0.5),
        'cmp_w2': nrm(ks[16], (N_ODD, 2, CMP_HIDDEN, HEAD_DIM), CMP_HIDDEN ** -0.5),
        'conf_dw': nrm(ks[17], (N_ODD, CONF_K, CONF_WIDTH), CONF_K ** -0.5),
        'conf_dw_b': nrm(ks[18], (N_ODD, CONF_WIDTH), 0.02),
        'conf_ln_g': 1.0 + nrm(ks[19], (N_ODD, CONF_WIDTH), 0.05),
        'conf_ln_b': nrm(ks[20], (N_ODD, CONF_WIDTH), 0.02),
        'w_out_odd': nrm(ks[21], (N_ODD, d, d), 0.5 * d ** -0.5),
    }

def second_block(x, norm_mix, norm_ffn, ffn_gate, ffn_up, ffn_down,
              w_in_even, conv_a, pool_w, pool_scale, w_out_even,
              w_in_odd, q_norm, k_norm, cmp_pos, cmp_w1, cmp_w2,
              conf_dw, conf_dw_b, conf_ln_g, conf_ln_b, w_out_odd):
    cos, sin = rope_tables(x.shape[1])
    for i in range(DEPTH):
        h = rms_norm(x, norm_mix[i])
        if i % 2 == 0:
            e = i // 2
            x = x + short_conv_pool_mixer(h, w_in_even[e], conv_a[e], pool_w[e],
                                          pool_scale[e], w_out_even[e])
        else:
            o = i // 2
            x = x + sparse_attn_conformer_mixer(h, w_in_odd[o], q_norm[o], k_norm[o], cmp_pos[o],
                                                cmp_w1[o], cmp_w2[o], conf_dw[o], conf_dw_b[o],
                                                conf_ln_g[o], conf_ln_b[o], w_out_odd[o], cos, sin)
        x = x + swiglu_2(rms_norm(x, norm_ffn[i]), ffn_gate[i], ffn_up[i], ffn_down[i])
    return x


def setup_inputs(seed=0):
    out = dict(first_inputs(seed))
    for name, value in second_inputs(seed + 1).items():
        if name != "x":
            out[name + "_2"] = value
    return out


def reference(
    x, ln1_g, ln1_b, w_ff1_in, w_ff1_out, w_in, b_in, conv_w, a_log, dt_bias, gdn_norm_g,
    rel_bias, sinks, w_gate, b_gate, w_br_a, w_br_b, w_br_c, w_out, ln2_g, ln2_b, w_ff2_in,
    w_ff2_out, ln3_g, ln3_b, norm_mix_2, norm_ffn_2, ffn_gate_2, ffn_up_2, ffn_down_2,
    w_in_even_2, conv_a_2, pool_w_2, pool_scale_2, w_out_even_2, w_in_odd_2, q_norm_2, k_norm_2,
    cmp_pos_2, cmp_w1_2, cmp_w2_2, conf_dw_2, conf_dw_b_2, conf_ln_g_2, conf_ln_b_2,
    w_out_odd_2,
):
    x = first_block(
        x, ln1_g, ln1_b, w_ff1_in, w_ff1_out, w_in, b_in, conv_w, a_log, dt_bias, gdn_norm_g,
        rel_bias, sinks, w_gate, b_gate, w_br_a, w_br_b, w_br_c, w_out, ln2_g, ln2_b, w_ff2_in,
        w_ff2_out, ln3_g, ln3_b,
    )
    return second_block(
        x, norm_mix_2, norm_ffn_2, ffn_gate_2, ffn_up_2, ffn_down_2, w_in_even_2, conv_a_2,
        pool_w_2, pool_scale_2, w_out_even_2, w_in_odd_2, q_norm_2, k_norm_2, cmp_pos_2,
        cmp_w1_2, cmp_w2_2, conf_dw_2, conf_dw_b_2, conf_ln_g_2, conf_ln_b_2, w_out_odd_2,
    )


_drawn_inputs = setup_inputs


def setup_inputs(seed=0):
    import zlib

    import numpy as np

    out = dict(_drawn_inputs(seed))
    spreads = {}
    factors = {'b_in': 8.0,
     'a_log': 3.249,
     'gdn_norm_g': 8.0,
     'rel_bias': 8.0,
     'sinks': 8.0,
     'b_gate': 8.0,
     'q_norm_2': 8.0,
     'k_norm_2': 8.0,
     'cmp_pos_2': 6.027,
     'conf_dw_b_2': 7.311,
     'conf_ln_g_2': 4.925,
     'conf_ln_b_2': 8.0}
    for name, (base, spread) in spreads.items():
        noise = np.random.default_rng([zlib.crc32(name.encode()), seed]).standard_normal(out[name].shape)
        drawn = base * np.exp(spread * noise) if base else spread * noise
        out[name] = jnp.asarray(drawn.astype(out[name].dtype))
    for name, factor in factors.items():
        out[name] = (out[name] * factor).astype(out[name].dtype)
    return out
```

```python
from contextlib import ExitStack

import numpy as np

import concourse.bass as bass
from concourse import mybir

ALU = mybir.AluOpType
ACT = mybir.ActivationFunctionType
AX = mybir.AxisListType.X
F = mybir.dt.float32
R = mybir.dt.float32r

P = 128
T = 256
D = 1024
NEG = -1e30
ALPHA = 4.0 ** 0.25

KU = 2
UW = 520
RAW = 4
SPL = 6
LEAD = 4

CMAT = ["ident", "flip", "tri", "rev", "strict", "decay", "pair", "causal",
        "m1", "t1", "t2", "t4", "t8", "t16", "t32", "ali1", "ali0"]
C_CM1 = len(CMAT) * P
C_CMB = C_CM1 + 2 * 32
C_COS = C_CMB + 2 * 32
C_SIN = C_COS + 2 * 32
C_CNT = C_SIN + 2 * 32
C_ONE = C_CNT + 4 * 16
NCONST = C_ONE + P


def shape_constants():
    i = np.arange(P)[:, None]
    j = np.arange(P)[None, :]
    same = i // 64 == j // 64
    zero = np.zeros((P, P), np.float32)

    def level(s, a, b):
        return ((a // (2 * s) == b // (2 * s)) & (a % (2 * s) >= s) & (b % (2 * s) < s)).astype(np.float32)

    m = {
        "ident": (i == j).astype(np.float32),
        "flip": (i + j == P - 1).astype(np.float32),
        "tri": (same & (i <= j)).astype(np.float32),
        "rev": (same & (i > j)).astype(np.float32),
        "strict": (same & (i > j)).astype(np.float32),
        "decay": np.where(same & (i >= j), 0.0, NEG),
        "pair": np.where((i < 64) & (j >= 64), NEG, 0.0) + zero,
        "causal": np.where(j <= i, 0.0, NEG) + zero,
        "m1": level(1, i, j),
        "ali0": np.where((i < 64) & (j >= 64), -NEG, abs(i - j)) + zero,
        "ali1": np.where((i >= 64) & (j < 64), -NEG, abs(P + i - j)) + zero,
    }
    for s in (1, 2, 4, 8, 16, 32):
        m[f"t{s}"] = level(s, j, i)
    out = np.zeros((P, NCONST), np.float32)
    for n, name in enumerate(CMAT):
        out[:, n * P:(n + 1) * P] = m[name]
    pos = np.arange(T)
    n = np.arange(32)
    seen = (n[None, :] < 15) & (n[None, :] * 16 + 31 <= pos[:, None])
    inv = 1.0 / (10000.0 ** (np.arange(0, 64, 2, dtype=np.float32) / np.float32(64)))
    ang = pos[:, None].astype(np.float32) * inv[None, :].astype(np.float32)
    for at, table in ((C_CM1, seen.astype(np.float32)), (C_CMB, np.where(seen, 0.0, NEG)),
                      (C_COS, np.cos(ang)), (C_SIN, np.sin(ang))):
        for t in range(2):
            out[:, at + 32 * t:at + 32 * t + 32] = table[t * P:(t + 1) * P]
    for g, w in enumerate((2, 4, 8, 16)):
        out[:, C_CNT + 16 * g:C_CNT + 16 * g + 16] = 1.0 / np.minimum(np.arange(16) + 1, w)
    out[:, C_ONE:C_ONE + P] = 1.0
    return out


class Queues:

    ENGINES = ("pe", "act", "dve", "pool", "sp")

    def __init__(self, sems, starts):
        self.sems = sems
        self.starts = starts
        self.lists = {e: [] for e in self.ENGINES}
        self.count = {n: 0 for n in sems}
        self.seen = {e: {} for e in self.ENGINES}

    def wait(self, eng, *tokens):
        for tok in tokens:
            if tok is None:
                continue
            if isinstance(tok, list) or (isinstance(tok, tuple) and not isinstance(tok[0], str)):
                self.wait(eng, *tok)
                continue
            name, value = tok
            if self.seen[eng].get(name, 0) < value:
                self.seen[eng][name] = value
                self.lists[eng].append((None, None, None, name, value))

    def put(self, eng, fn, args, kw, tokens, sig=True):
        self.wait(eng, tokens)
        if not sig:
            self.lists[eng].append((fn, args, kw, None, 0))
            return None
        self.count[eng] += 1
        self.lists[eng].append((fn, args, kw, eng, 1))
        return (eng, self.count[eng])

    def dma(self, eng, sem, out, src, *tokens):
        self.wait(eng, *tokens)
        self.count[sem] += 16
        self.lists[eng].append((self.starts[eng], (out, src), {}, sem, 16))
        return (sem, self.count[sem])

    def play(self, eng, engine):
        for fn, args, kw, name, value in self.lists[eng]:
            if fn is None:
                engine.wait_ge(self.sems[name], value)
            else:
                ins = fn(*args, **kw)
                if name is not None:
                    ins.then_inc(self.sems[name], value)


def build(nc, a, out):
    with ExitStack() as ctx:
        def sem(name):
            return ctx.enter_context(nc.semaphore(name))

        def sb(name, shape, dt=F):
            return ctx.enter_context(nc.sbuf_tensor(name, shape, dt))

        names = list(Queues.ENGINES) + [f"raw{n}" for n in range(RAW)] + [f"ld{n}" for n in range(24)] + ["st"]
        sems = {n: sem(f"s_{n}") for n in names}

        CO = sb("CO", [P, NCONST])
        VEC = sb("VEC", [P, 336])
        SM = sb("SM", [P, 2 * 144 + 256])
        GB = sb("GB", [P, 2, D])
        X = sb("X", [P, 2, D])
        XTH = sb("XTH", [P, 8, T], R)
        XTL = sb("XTL", [P, 8, T], R)
        RW = [sb(f"RW{n}", [P, KU, UW]) for n in range(RAW)]
        WH = [sb(f"WH{n}", [P, KU, UW], R) for n in range(SPL)]
        WL = [sb(f"WL{n}", [P, KU, UW], R) for n in range(SPL)]
        ST = sb("ST", [P, 64])
        PS = ctx.enter_context(nc.psum_tensor("PS", [P, 8, 512], F))
        room = 229344 - nc.sbuf_base - 96
        room -= room % 64
        base = nc.sbuf_base
        base += -base % 64
        ctx.enter_context(nc.sbuf_tensor("SCR", [P, room // 4], F))
        made = {}

        def at(off, name, shape, dt=F):
            n = 4
            for s in shape[1:]:
                n *= s
            assert off + n <= room, (name, off + n, room)
            if name not in made:
                tile = nc.alloc_sbuf_tensor_at(name, shape, dt, offset=base + off)
                made[name] = tile[tuple(slice(None) for _ in shape)]
            return made[name]

        scratch = nc.dram_tensor("scratch", (4 * 384 + 2 * T * P,), F).ap()

        units = None
        record = []

        def trace(units):
            q = Queues(sems, {"sp": nc.sync.dma_start, "pool": nc.gpsimd.dma_start, "act": nc.scalar.dma_start})
            V, S, G, E = nc.vector, nc.scalar, nc.gpsimd, nc.tensor

            def pe(fn, *args, w=None, sig=False, **kw):
                return q.put("pe", fn, args, kw, w, sig=sig)

            def act(fn, *args, w=None, **kw):
                return q.put("act", fn, args, kw, w)

            def dve(fn, *args, w=None, **kw):
                return q.put("dve", fn, args, kw, w)

            def pool(fn, *args, w=None, **kw):
                return q.put("pool", fn, args, kw, w)

            cm = {n: CO[:, k * P:(k + 1) * P] for k, n in enumerate(CMAT)}
            ident = cm["ident"]
            ones = CO[:, C_ONE:C_ONE + P]

            loaded, split, freed = {}, {}, {}

            def load(n):
                if units is None or n >= len(units) or n in loaded:
                    return
                src = units[n]
                k, w = src.shape[1], src.shape[2]
                loaded[n] = q.dma("sp", f"raw{n % RAW}", RW[n % RAW][:, 0:k, 0:w], src,
                                  split.get(n - RAW))

            def cut(n):
                if units is None or n >= len(units) or n in split:
                    return
                load(n)
                k, w = units[n].shape[1], units[n].shape[2]
                raw, hi, lo = (t[n % m][:, 0:k, 0:w] for t, m in ((RW, RAW), (WH, SPL), (WL, SPL)))
                th = act(S.activation, hi, raw, ACT.Copy, w=[loaded[n], freed.get(n - SPL)])
                tl = dve(V.tensor_tensor, lo, raw, hi.bitcast(F), ALU.subtract,
                         w=[loaded[n], th, freed.get(n - SPL)])
                split[n] = [th, tl]
                load(n + RAW)

            taken = [0]

            class Unit:

                def __init__(self, src):
                    self.n = taken[0]
                    taken[0] += 1
                    self.nk = src.shape[1]
                    if units is None:
                        record.append(src)
                        self.tok = None
                    else:
                        for m in range(RAW):
                            load(self.n + m) if self.n == 0 else None
                        for m in range(LEAD + 1):
                            cut(self.n + m)
                        self.tok = split[self.n]
                    self.h = WH[self.n % SPL]
                    self.l = WL[self.n % SPL]

                def free(self, tok):
                    freed[self.n] = tok

            def wsrc(w, k0, nk, c0, nc_):
                return w[k0 * P:(k0 + nk) * P, c0:c0 + nc_].rearrange("(k p) n -> p k n", p=P)

            free_banks = [(b, None) for b in range(8)]

            def bank():
                return free_banks.pop(0)

            def drop(b, *tok):
                free_banks.append((b, list(tok)))

            def mm3(o, xh, xl, wh, wl, start, stop, *w, sig=False, flip=False):
                a_ = ((xh, wh), (xh, wl), (xl, wh))
                tok = None
                for n, (x_, w_) in enumerate(a_):
                    l_, r_ = (w_, x_) if flip else (x_, w_)
                    tok = pe(E.matmul, o, l_, r_, start=start and n == 0, stop=stop and n == 2,
                             w=list(w) if n == 0 else None, sig=sig and n == 2)
                return tok

            def rows(w, nk, c0, parts, xh, xl, xtok):
                wide = max(off + width for off, width, _ in parts)
                for k0 in range(0, nk, KU):
                    kk = min(KU, nk - k0)
                    u = Unit(wsrc(w, k0, kk, c0, wide))
                    for t in range(2):
                        for k in range(kk):
                            kt = k0 + k
                            ts = slice(t * P, t * P + P)
                            last = kt == nk - 1
                            for n, (off, width, bks) in enumerate(parts):
                                cs = slice(off, off + width)
                                tok = mm3(PS[:, bks[t][0], 0:width], xh[:, kt, ts], xl[:, kt, ts],
                                          u.h[:, k, cs], u.l[:, k, cs], kt == 0, last,
                                          u.tok, bks[t][1], xtok(kt, t),
                                          sig=n == len(parts) - 1 and (last or (k == kk - 1 and t == 1)))
                            if last:
                                done[t] = tok
                    u.free(tok)
                    yield

            done = {}

            def run(gen):
                for _ in gen:
                    pass

            co = q.dma("pool", "ld0", CO[:, :], a["consts"])
            sm = []
            smv = {}
            c = 0

            def small(key, src):
                nonlocal c
                n = src.shape[1]
                smv[key] = SM[:, c:c + n]
                sm.append(q.dma("pool", f"ld{1 + len(sm)}", SM[:, c:c + n], src.to_broadcast([P, n])))
                c += n

            for l in range(2):
                small(("a_log", l), a["a_log"][l:l + 1, :])
                small(("dt_bias", l), a["dt_bias"][l:l + 1, :])
                small(("norm_g", l), a["gdn_norm_g"][l:l + 1, :])
                small(("sinks", l), a["sinks"][l:l + 1, :])
            small("q_norm", a["q_norm_2"])
            small("k_norm", a["k_norm_2"].rearrange("l a b -> l (a b)"))
            sm_tok = sm

            vec = {}
            vn = 0
            vec_tok = []
            STG = [at(k * 512, f"stg{k}", [P, P]) for k in range(3)]

            def flat(v):
                return v.rearrange("(r p) -> r p", p=P)

            groups = [[], [], []]
            for l in range(2):
                for key, c0, n in (("qb", 2056, 4), ("kb", 2568, 4), ("qc", 3592, 4), ("kc", 4104, 1),
                                   ("qkv", 0, 12)):
                    groups[0].append(((key, l), flat(a["b_in"][l, c0:c0 + n * P])))
                for k in range(4):
                    groups[1].append((("conv", l, k), flat(a["conv_w"][l, k, :])))
            for k in range(3):
                groups[0].append((("conva", k), flat(a["conv_a_2"][0, k, :])))
            groups[0].append(("pool_scale", flat(a["pool_scale_2"][0, :])))
            groups[0].append(("conf_b", flat(a["conf_dw_b_2"][0, :])))
            groups[0].append(("conf_lg", flat(a["conf_ln_g_2"][0, :])))
            groups[0].append(("conf_lb", flat(a["conf_ln_b_2"][0, :])))
            groups[0].append(("cmp_pos", a["cmp_pos_2"].rearrange("z k (j b) d -> (z k j) (b d)", b=2)))
            for k in range(31):
                groups[2].append((("dw", k), flat(a["conf_dw_2"][0, k, :])))
            for g, rows_ in enumerate(groups):
                r = 0
                tok = None
                if g == 2:
                    tok = q.dma("pool", "ld12", STG[g][0:124, :],
                                a["conf_dw_2"][0].rearrange("k (r p) -> (k r) p", p=P))
                elif g == 1:
                    tok = q.dma("pool", "ld13", STG[g][0:96, :],
                                a["conv_w"].rearrange("l k (r p) -> (l k r) p", p=P))
                for key, src in rows_:
                    n = src.shape[0]
                    if g == 0:
                        tok = q.dma("pool", "ld14", STG[g][r:r + n, :], src)
                    vec[key] = VEC[:, vn + r:vn + r + n]
                    r += n
                b, w = bank()
                t1 = pe(E.transpose, PS[:, b, 0:r], STG[g][0:r, :], ident[0:r, 0:r], w=[tok, co, w], sig=True)
                t2 = dve(V.tensor_copy, VEC[:, vn:vn + r], PS[:, b, 0:r], w=t1)
                drop(b, t2)
                vec_tok.append(t2)
                vn += r

            s = {"x": [None, None], "xt": {}}

            def to_hl(src, nkt, t, th, tl, kt0, *w):
                toks = {}
                for g0 in range(0, nkt, 4):
                    n = min(4, nkt - g0)
                    b, bw = bank()
                    for k in range(n):
                        tok = pe(E.transpose, PS[:, b, k * P:k * P + P], src(g0 + k), ident,
                                 w=[bw, co, *w], sig=(k == n - 1))
                    hi = th[:, kt0 + g0:kt0 + g0 + n, t * P:t * P + P]
                    lo = tl[:, kt0 + g0:kt0 + g0 + n, t * P:t * P + P]
                    pv = PS[:, b, 0:n * P].rearrange("p (k n) -> p k n", k=n)
                    t1 = act(S.activation, hi, pv, ACT.Copy, w=tok)
                    t2 = dve(V.tensor_tensor, lo, pv, hi.bitcast(F), ALU.subtract, w=[tok, t1])
                    drop(b, t1, t2)
                    for k in range(n):
                        toks[kt0 + g0 + k] = [t1, t2]
                return toks

            def x_in():
                for t in range(2):
                    s["x"][t] = q.dma("pool", f"ld{15 + t}", X[:, t, :], a["x"][0, t * P:(t + 1) * P, :])

            def x_turn(alpha=None):
                for t in range(2):
                    tk = to_hl(lambda k: X[:, t, k * P:k * P + P], 8, t, XTH, XTL, 0, s["x"][t])
                    for k, v in tk.items():
                        s["xt"][k, t] = v
                    if alpha is not None:
                        s["x"][t] = pool(G.tensor_scalar, X[:, t, :], X[:, t, :], alpha, None, ALU.mult,
                                         w=[s["x"][t], tk[3], tk[7]])

            xtok = lambda kt, t: s["xt"][kt, t]

            gbt = [None]

            def load_gb(g, b=None):
                w = gbt[0]
                gbt[0] = [q.dma("pool", "ld17", GB[:, 0, :], g.to_broadcast([P, D]), w)]
                if b is not None:
                    gbt[0].append(q.dma("pool", "ld18", GB[:, 1, :], b.to_broadcast([P, D])))


            def power(dst, src, scale, eps, *w):
                t1 = act(S.activation, dst, src, ACT.Sqrt, bias=epsc[eps], scale=scale, w=w)
                return dve(V.reciprocal, dst, dst, w=t1)

            epst = [dve(V.memset, ST[:, 60:61], 1e-5), dve(V.memset, ST[:, 61:62], 1e-6)]
            epsc = {1e-5: ST[:, 60:61], 1e-6: ST[:, 61:62]}

            def residual(half, t, b, scale, tok):
                xs = X[:, t, half * 512:half * 512 + 512]
                yt = dve(V.scalar_tensor_tensor, out=xs, in0=PS[:, b, :], scalar=scale, in1=xs,
                         op0=ALU.mult, op1=ALU.add, w=[tok, s["x"][t]])
                drop(b, yt)
                return yt

            def stats(half, t, tok):
                return dve(V.bn_stats, ST[:, 12 * t + 6 * half:12 * t + 6 * half + 6],
                           X[:, t, half * 512:half * 512 + 512], w=tok)

            def ln_finish(t, toks):
                o = 24 + 4 * t
                t1 = dve(V.bn_aggr, ST[:, o:o + 2], ST[:, 12 * t:12 * t + 12], w=toks)
                t2 = power(ST[:, o + 2:o + 3], ST[:, o + 1:o + 2], 1.0, 1e-5, t1, epst)
                x_ = X[:, t, :]
                t3 = dve(V.tensor_scalar, x_, x_, ST[:, o:o + 1], ST[:, o + 2:o + 3],
                         ALU.subtract, ALU.mult, w=[t1, t2])
                t4 = dve(V.tensor_tensor, x_, x_, GB[:, 0, :], ALU.mult, w=[t3, gbt[0]])
                t5 = dve(V.tensor_tensor, x_, x_, GB[:, 1, :], ALU.add, w=t4)
                s["x"][t] = t5
                return t5

            def out_rows(w, nk, xh, xl, xt, scale, ln, c_of=None):
                sts = {0: [], 1: []}
                for half in range(2):
                    bks = [bank(), bank()]
                    yield from rows(w, nk, half * 512, [(0, 512, bks)], xh, xl, xt)
                    for t in range(2):
                        tok = residual(half, t, bks[t][0], scale, done[t])
                        if ln:
                            sts[t].append(stats(half, t, tok))
                        else:
                            sts[t].append(tok)
                if ln:
                    last = [ln_finish(t, sts[t]) for t in range(2)]
                    gbt[0] = last
                else:
                    for t in range(2):
                        s["x"][t] = sts[t][1]

            H_OFF = 0

            def ffn(wg, wu, wd, cg, cu, nf, xt, scale, ln, tag):
                nsl = -(-nf // 512)
                nkt = nf // P
                HTH = at(H_OFF, f"HTH{nkt}", [P, nkt, T], R)
                HTL = at(H_OFF + nkt * T * 4, f"HTL{nkt}", [P, nkt, T], R)
                SG = at(H_OFF + nkt * T * 8, f"SG{nkt}", [P, 2, 512])
                HM = at(H_OFF + nkt * T * 8 + 4096, f"HM{nkt}", [P, 2, 512])
                ht = {}
                pend = []

                def finish(sl, wd_, hm):
                    for t in range(2):
                        n = wd_ // P
                        tk = to_hl(lambda k: HM[:, t, k * P:k * P + P], n, t, HTH, HTL, 4 * sl, hm[t])
                        for k, v in tk.items():
                            ht[k, t] = v
                        hm[t] = v

                last = [None, None]
                for sl in range(nsl):
                    wd_ = min(512, nf - 512 * sl)
                    g = [bank(), bank()]
                    run(rows(wg, 8, cg + 512 * sl, [(0, wd_, g)], XTH, XTL, xt))
                    gd = dict(done)
                    if pend:
                        psl, pw, hm = pend.pop()
                        finish(psl, pw, hm)
                        last = hm
                    u = [bank(), bank()]
                    run(rows(wu, 8, cu + 512 * sl, [(0, wd_, u)], XTH, XTL, xt))
                    hm = [None, None]
                    for t in range(2):
                        t1 = act(S.activation, SG[:, t, 0:wd_], PS[:, g[t][0], 0:wd_], ACT.Silu, w=[gd[t], last[t]])
                        drop(g[t][0], t1)
                        t2 = dve(V.tensor_tensor, HM[:, t, 0:wd_], PS[:, u[t][0], 0:wd_], SG[:, t, 0:wd_], ALU.mult,
                                 w=[t1, done[t], last[t]])
                        drop(u[t][0], t2)
                        hm[t] = t2
                    pend.append((sl, wd_, hm))
                y = out_rows(wd, nkt, HTH, HTL, lambda kt, t: ht[kt, t], scale, ln)
                next(y)
                psl, pw, hm = pend.pop()
                finish(psl, pw, hm)
                run(y)


            def evac(kind, dst, src, *w):
                if kind == "act":
                    return act(S.activation, dst, src, ACT.Copy, w=w)
                return dve(V.tensor_copy, dst, src, w=w)

            def cols(w, c0, nt, bks, xt, width=None):
                for k0 in range(0, 8, KU):
                    u = Unit(wsrc(w, k0, KU, c0, nt * P))
                    for k in range(KU):
                        kt = k0 + k
                        for j in range(nt):
                            cs = slice(j * P, j * P + P)
                            tok = mm3(PS[:, bks[j][0], 0:T], XTH[:, kt, :], XTL[:, kt, :],
                                      u.h[:, k, cs], u.l[:, k, cs], kt == 0, kt == 7,
                                      u.tok, bks[j][1], xt(kt, 0), xt(kt, 1),
                                      sig=(kt == 7) or (k == KU - 1 and j == nt - 1), flip=True)
                            if kt == 7:
                                done["c", j] = tok
                    u.free(tok)
                    yield

            def bcast(ap, *shape):
                return ap.to_broadcast(list(shape))

            def over(ap, n):
                return ap.unsqueeze(2).to_broadcast([ap.shape[0], ap.shape[1], n])

            def heads(ap, n):
                return ap.unsqueeze(1).to_broadcast([ap.shape[0], n, ap.shape[1]])

            def softmax_rows(sv, nh, pv, k, scale, w, sink=None):
                o = 32 * (k % 4)
                m, n_, su, rc, es = (SX[:, o + 4 * q_:o + 4 * q_ + nh] for q_ in range(5))
                t1 = dve(V.tensor_reduce, m, sv, AX, ALU.max, w=w)
                if sink is not None:
                    t1 = dve(V.scalar_tensor_tensor, out=m, in0=m, scalar=scale, in1=sink,
                             op0=ALU.mult, op1=ALU.max, w=[t1, sm_tok])
                    t2 = dve(V.tensor_scalar, n_, m, -1.0, None, ALU.mult, w=t1)
                    t3 = dve(V.tensor_tensor, es, sink, m, ALU.subtract, w=t1)
                    t3 = act(S.activation, es, es, ACT.Exp, w=t3)
                else:
                    t2 = dve(V.tensor_scalar, n_, m, -scale, None, ALU.mult, w=t1)
                    t3 = None
                for h in range(nh):
                    t4 = act(S.activation, pv[:, h, :], sv[:, h, :], ACT.Exp, bias=n_[:, h:h + 1], scale=scale,
                             accum_out=su[:, h:h + 1], w=[t2, w])
                if sink is not None:
                    t5 = dve(V.tensor_tensor, su, su, es, ALU.add, w=[t4, t3])
                    t5 = dve(V.reciprocal, rc, su, w=t5)
                else:
                    t5 = dve(V.reciprocal, rc, su, w=t4)
                return rc, t4, t5

            def block_attention(l, q_ap, k_ap, v_ap, qk_tok, v_tok, group, k, toh, tol, res, kind, extra):
                t, hs = group
                nh, nk = len(hs), (t + 1) * P
                pv = PP[k % 2][:, 0:nh * nk].rearrange("p (h n) -> p h n", h=nh)
                b, bw = bank()
                sv = PS[:, b, 0:nh * nk].rearrange("p (h n) -> p h n", h=nh)
                for n, h in enumerate(hs):
                    tok = pe(E.matmul, sv[:, n, :], q_ap(h, t), k_ap(h, nk), start=True, stop=kind == "c",
                             w=[bw, qk_tok, co], sig=True, skip_group_check=True)
                    if kind == "b":
                        for kt in range(t + 1):
                            tok = pe(E.matmul, sv[:, n, kt * P:kt * P + P],
                                     YH[:, h, (t - kt) * P:(t - kt) * P + P], cm["flip"],
                                     start=False, stop=kt < t, w=[extra], sig=True, skip_group_check=True)
                        tok = pe(E.matmul, sv[:, n, t * P:t * P + P], ident, cm["pair"],
                                 start=False, stop=True, sig=True, skip_group_check=True)
                if kind == "c":
                    lv = SC[k % 2][:, 0:nh * nk].rearrange("p (h n) -> p h n", h=nh)
                    a0 = CMAT.index("ali1") * P
                    al = CO[:, a0:a0 + 2 * P] if t else CO[:, a0 + P:a0 + 2 * P]
                    for n, h in enumerate(hs):
                        tok2 = dve(V.scalar_tensor_tensor, out=lv[:, n, :], in0=al, scalar=-8.0 * 2.0 ** -(h + 1),
                                   in1=sv[:, n, :], op0=ALU.mult, op1=ALU.add, w=[tok, co])
                    drop(b, tok2)
                    rc, te, tr = softmax_rows(lv, nh, pv, k, 0.125, tok2, smv["sinks", l][:, hs[0]:hs[0] + 2 * nh - 1:2])
                else:
                    rc, te, tr = softmax_rows(sv, nh, pv, k, 1.0, tok)
                    drop(b, te)
                tn = dve(V.tensor_tensor, pv, pv, over(rc, nk), ALU.mult, w=tr)
                yield
                b, bw = bank()
                tv = PS[:, b, :].rearrange("p (c n) -> p c n", n=P)
                idx = {}
                for n, h in enumerate(hs):
                    for kt in range(t + 1):
                        i = len(idx)
                        idx[h, kt] = i
                        tok = pe(E.transpose, tv[:, i, :], pv[:, n, kt * P:kt * P + P], ident,
                                 w=[tn, bw], sig=True)
                pt = PT[k % 2]
                tp = act(S.activation, pt[:, 0:len(idx) * P], PS[:, b, 0:len(idx) * P], ACT.Copy, w=tok)
                drop(b, tp)
                yield
                b, bw = bank()
                if kind == "b":
                    for n, h in enumerate(hs):
                        for kt in range(t + 1):
                            i = idx[h, kt]
                            tok = pe(E.matmul, PS[:, b, n * P:n * P + P], v_ap(h, kt), pt[:, i * P:i * P + P],
                                     start=kt == 0, stop=kt == t, w=[tp, bw, v_tok], sig=True)
                    nt, t0, r, m = nh, hs[0], 0, P
                else:
                    r, m = 64 * (hs[0] % 2), 64
                    for n, h in enumerate(hs):
                        for kt in range(t + 1):
                            i = idx[h, kt]
                            tok = pe(E.matmul, PS[r:r + 64, b, n * P:n * P + P], v_ap(h, kt),
                                     pt[:, i * P:i * P + P], start=kt == 0, stop=kt == t,
                                     w=[tp, bw, v_tok], sig=True)
                    nt, t0 = nh, hs[0] // 2
                res.append(split_out(b, r, m, nt, t0, t, toh, tol, tok))
                yield

            def split_out(b, r, m, nt, t0, t, toh, tol, tok):
                src = PS[r:r + m, b, 0:nt * P].rearrange("p (k n) -> p k n", k=nt)
                hi, lo = (o[r:r + m, t0:t0 + nt, t * P:t * P + P] for o in (toh, tol))
                t1 = act(S.activation, hi, src, ACT.Copy, w=tok)
                t2 = dve(V.tensor_tensor, lo, src, hi.bitcast(F), ALU.subtract, w=[t1, tok])
                drop(b, t1, t2)
                return [t1, t2]

            def pipeline(gens, fill, each):
                live = []
                gens = list(gens)
                while gens or live:
                    if gens:
                        live.append(gens.pop(0))
                    keep = []
                    for g in live:
                        try:
                            next(g)
                            keep.append(g)
                        except StopIteration:
                            pass
                    live = keep
                    fill(each)

            def load_gb_after(w1, w2, g, b):
                gbt[0] = [w1, w2]
                load_gb(g, b)

            SX = at(int(93.5 * 1024), "SX", [P, 512])

            def mixer1(l):
                K = 1024
                QK = at(0, "QK", [P, 8, T])
                VB = at(8 * K, "VB", [P, 2, 512])
                QC = at(12 * K, "QC", [P, 4, T])
                KC = at(16 * K, "KC", [P, 2, T])
                VC = at(18 * K, "VC", [P, 2, P])
                nonlocal YH, PP, PT, SC
                YH = at(19 * K, "YH", [P, 4, T])
                PP = [at((23 + 2 * n) * K, f"PP{n}", [P, 512]) for n in range(2)]
                PT = [at((27 + 2 * n) * K, f"PT{n}", [P, 512]) for n in range(2)]
                SC = [at((31 + 2 * n) * K, f"SC{n}", [P, 512]) for n in range(2)]
                RBX = at(35 * K, "RBX", [4, 384])
                QP = at(37 * K, "QP", [P, 12, 259])
                MG = at(37 * K, "MG", [P, 2, D])
                GT = [at((45 + 2 * n) * K, f"GT{n}", [P, 512]) for n in range(2)]
                QX = at(49 * K + 512, "QX", [P, 12, T])
                OH = {i: [at(int((61.5 + 8 * n + 4 * m) * K), f"O{i}{m}", [P, 4, T], R)
                          for m in range(2)] for n, i in enumerate("abc")}
                Z = at(int(85.5 * K), "Z", [P, 2, 512])
                SS = at(int(89.5 * K), "SS", [P, 512])
                VN = at(int(91.5 * K), "VN", [P, 512])

                r1 = q.dma("pool", "ld1", RBX[:, 64:256], a["rel_bias"][l])
                r2 = pool(G.tensor_copy, RBX[:, 0:64], bcast(RBX[:, 64:65], 4, 64), w=r1)
                r3 = pool(G.tensor_copy, RBX[:, 256:384], bcast(RBX[:, 255:256], 4, 128), w=r1)
                r4 = q.dma("pool", "ld2", scratch[0:1536].rearrange("(h n) -> h n", h=4), RBX[:, :], r2, r3)
                yh = q.dma("pool", "ld3", YH[:, :, :], bass.AP(scratch.tensor, 0, [[1, P], [384, 4], [1, T]]), r4)
                b_vb = q.dma("pool", "ld4", GB[:, 1, 0:512], bcast(a["b_in"][l:l + 1, 3080:3592], P, 512), gbt[0])
                b_vc = q.dma("pool", "ld5", GB[:, 1, 512:640], bcast(a["b_in"][l:l + 1, 4232:4360], P, 128), gbt[0])
                b_za = q.dma("pool", "ld6", GB[:, 0, 0:520], bcast(a["b_in"][l:l + 1, 1536:2056], P, 520), gbt[0])
                pz = pool(G.memset, QP[:, :, 0:3], 0.0)

                w_in = a["w_in"][l]
                qk = []
                for part, c0 in enumerate((2056, 2568)):
                    bks = [bank() for _ in range(4)]
                    run(cols(w_in, c0, 4, bks, xtok))
                    key = ("qb", "kb")[part]
                    for j in range(4):
                        qk.append(dve(V.tensor_scalar, QK[:, 4 * part + j, :], PS[:, bks[j][0], 0:T],
                                      vec[key, l][:, j:j + 1], 128.0 ** -0.5 if part == 0 else 1.0,
                                      ALU.add, ALU.mult, w=[done["c", j], vec_tok]))
                        drop(bks[j][0], qk[-1])
                bks = [bank(), bank()]
                run(rows(w_in, 8, 3080, [(0, 512, bks)], XTH, XTL, xtok))
                vb = []
                for t in range(2):
                    vb.append(dve(V.tensor_tensor, VB[:, t, :], PS[:, bks[t][0], :], GB[:, 1, 0:512], ALU.add,
                                  w=[done[t], b_vb]))
                    drop(bks[t][0], vb[-1])
                bks = [bank() for _ in range(4)]
                run(cols(w_in, 3592, 4, bks, xtok))
                qc = []
                for j in range(4):
                    qc.append(dve(V.tensor_scalar, QC[:, j, :], PS[:, bks[j][0], 0:T], vec["qc", l][:, j:j + 1],
                                  None, ALU.add, w=[done["c", j], vec_tok]))
                    drop(bks[j][0], qc[-1])
                kb_, v0, v1 = bank(), bank(), bank()
                for k0 in range(0, 8, KU):
                    u = Unit(wsrc(w_in, k0, KU, 4104, 256))
                    for k in range(KU):
                        kt = k0 + k
                        st, sp = kt == 0, kt == 7
                        tk = mm3(PS[:, kb_[0], 0:T], XTH[:, kt, :], XTL[:, kt, :], u.h[:, k, 0:P], u.l[:, k, 0:P],
                                 st, sp, u.tok, kb_[1], xtok(kt, 0), xtok(kt, 1), sig=True, flip=True)
                        for t, v_ in ((0, v0), (1, v1)):
                            ts = slice(t * P, t * P + P)
                            tv_ = mm3(PS[:, v_[0], 0:P], XTH[:, kt, ts], XTL[:, kt, ts],
                                      u.h[:, k, P:2 * P], u.l[:, k, P:2 * P], st, sp, v_[1], sig=True)
                    u.free(tv_)
                k1_ = dve(V.tensor_scalar, KC[:, 0, :], PS[:, kb_[0], 0:T], vec["kc", l], None, ALU.add,
                          w=[tk, vec_tok])
                drop(kb_[0], k1_)
                vc = []
                for t, v_ in ((0, v0), (1, v1)):
                    vc.append(dve(V.tensor_tensor, VC[:, t, :], PS[:, v_[0], 0:P], GB[:, 1, 512:640], ALU.add,
                                  w=[tv_, b_vc]))
                    drop(v_[0], vc[-1])
                b_, bw = bank()
                pe(E.matmul, PS[0:64, b_, 0:T], ident[:, 64:128], KC[:, 0, :], start=True, stop=True, w=[k1_, bw, co])
                tk = pe(E.matmul, PS[64:128, b_, 0:T], ident[:, 0:64], KC[:, 0, :], start=True, stop=True, sig=True)
                k2_ = dve(V.tensor_copy, KC[:, 1, :], PS[:, b_, 0:T], w=tk)
                drop(b_, k2_)

                ready = {"q": []}
                BA = SX[:, 256:272].rearrange("p (t c) -> p t c", t=2)

                def inputs_a():
                    for part in range(3):
                        bks = [bank() for _ in range(4)]
                        yield from cols(w_in, 512 * part, 4, bks, xtok)
                        for j in range(4):
                            tk = act(S.activation, QP[:, 4 * part + j, 3:259], PS[:, bks[j][0], 0:T], ACT.Identity,
                                     bias=vec["qkv", l][:, 4 * part + j:4 * part + j + 1], w=[done["c", j], vec_tok])
                            drop(bks[j][0], tk)
                            ready["q"].append(tk)
                    bks, ob = [bank(), bank()], [bank(), bank()]
                    yield from rows(w_in, 8, 1536, [(0, 8, ob), (8, 512, bks)], XTH, XTL, xtok)
                    for t in range(2):
                        t1 = dve(V.tensor_tensor, Z[:, t, :], PS[:, bks[t][0], :], GB[:, 0, 8:520], ALU.add,
                                 w=[done[t], b_za])
                        drop(bks[t][0], t1)
                        t2 = dve(V.tensor_tensor, BA[:, t, :], PS[:, ob[t][0], 0:8], GB[:, 0, 0:8], ALU.add,
                                 w=[done[t], b_za])
                        drop(ob[t][0], t2)
                        ready["z", t] = [t1, t2]
                    yield

                gen = inputs_a()
                state = {"gen": gen, "spent": False}

                def fill(n):
                    for _ in range(n):
                        if not state["spent"]:
                            try:
                                next(state["gen"])
                            except StopIteration:
                                state["spent"] = True

                res = {"b": [], "c": []}
                gb_ = [(0, [0, 1, 2, 3]), (1, [0, 1]), (1, [2, 3])]
                gc_ = [(0, [0, 2, 4, 6]), (0, [1, 3, 5, 7]), (1, [0, 2]), (1, [4, 6]), (1, [1, 3]), (1, [5, 7])]
                gens = []
                for n, g in enumerate(gb_):
                    gens.append(block_attention(
                        l, lambda h, t: QK[:, h, t * P:t * P + P], lambda h, nk: QK[:, 4 + h, 0:nk],
                        lambda h, kt: VB[:, kt, h * P:h * P + P], qk, vb, g, n, *OH["b"], res["b"], "b", yh))

                def kc_of(h, nk):
                    r = 64 * (h % 2)
                    return KC[r:r + 64, 0 if h // 4 == h % 2 else 1, 0:nk]

                for n, g in enumerate(gc_):
                    gens.append(block_attention(
                        l, lambda h, t: QC[64 * (h % 2):64 * (h % 2) + 64, h // 2, t * P:t * P + P], kc_of,
                        lambda h, kt: VC[:, kt, (h // 4) * 64:(h // 4) * 64 + 64],
                        qc + [k1_, k2_], vc, g, n + 3, *OH["c"], res["c"], "c", None))
                pipeline(gens, fill, 1)
                while not state["spent"]:
                    fill(1)
                att_done = [res["b"], res["c"]]

                bg = {"a": (0, 1), "b": (1, 1), "c": (2, 0)}
                bgt = {}
                first = [True]
                gtw = [None, None]

                def gate_bias(i, w):
                    n, slot = bg[i]
                    bgt[i] = q.dma("pool", "ld4" if slot else "ld6", GB[:, slot, :],
                                   bcast(a["b_gate"][l:l + 1, n * D:(n + 1) * D], P, D), w)

                def branch(i, th, tl, xt):
                    n, slot = bg[i]
                    wb = a[f"w_br_{i}"][l]
                    for half in range(2):
                        hs = slice(half * 512, half * 512 + 512)
                        g = [bank(), bank()]
                        yield from rows(a["w_gate"][l], 8, n * D + half * 512, [(0, 512, g)], XTH, XTL, xtok)
                        tg = []
                        for t in range(2):
                            t1 = dve(V.tensor_tensor, GT[t], PS[:, g[t][0], :], GB[:, slot, hs], ALU.add,
                                     w=[done[t], bgt[i], gtw[t]])
                            drop(g[t][0], t1)
                            tg.append(act(S.activation, GT[t], GT[t], ACT.Sigmoid, w=t1))
                        y = [bank(), bank()]
                        yield from rows(wb, 4, half * 512, [(0, 512, y)], th, tl, xt)
                        for t in range(2):
                            m = MG[:, t, hs]
                            t1 = dve(V.tensor_tensor, m if i == "b" else GT[t], PS[:, y[t][0], :], GT[t], ALU.mult,
                                     w=[done[t], tg[t]])
                            drop(y[t][0], t1)
                            if i != "b":
                                t1 = pool(G.tensor_tensor, m, m, GT[t], ALU.add, w=t1)
                            gtw[t] = t1
                            mgt[t, half] = t1
                    bgt[i] = t1

                mgt = {}
                gate_bias("b", [vb, vc])
                gate_bias("c", [ready["z", 0], ready["z", 1]])

                def others():
                    yield from branch("b", *OH["b"], lambda kt, t: res["b"])
                    yield from branch("c", *OH["c"], lambda kt, t: res["c"])

                TL = ["KBE", "VBT", "KDC", "DD", "LL", "LT", "QKD", "AT", "BB", "BT", "PW", "MS0", "MS1",
                      "EGR", "QDT", "WT", "UU", "GX"]
                W_ = {n: at(2048 * k, f"g{n}", [P, 4, P]) for k, n in enumerate(TL)}
                flat_ = {n: W_[n][:, :, :].rearrange("p h n -> p (h n)") for n in TL}
                sc = {}
                for k, n in enumerate(("BE", "T1", "T2", "T3", "GG", "GC", "RE", "EG", "ER", "Z1", "Z2")):
                    sc[n] = SX[:, 272 + 8 * k:280 + 8 * k]
                s2 = {n: v.rearrange("p (t h) -> p t h", t=2) for n, v in sc.items()}
                EA = SX[:, 368:372]
                zt = [ready["z", 0], ready["z", 1]]
                tb = act(S.activation, s2["BE"], BA[:, :, 0:4], ACT.Exp, scale=-1.0, w=zt)
                te = act(S.activation, EA, smv["a_log", l], ACT.Exp, w=sm_tok)
                tb = dve(V.tensor_scalar, sc["BE"], sc["BE"], 1.0, None, ALU.add, w=tb)
                tb = dve(V.reciprocal, sc["BE"], sc["BE"], w=tb)
                t1 = dve(V.tensor_tensor, s2["T1"], BA[:, :, 4:8], heads(smv["dt_bias", l], 2), ALU.add, w=[zt, sm_tok])
                t1 = dve(V.scalar_tensor_tensor, out=sc["T2"], in0=sc["T1"], scalar=-1.0, in1=sc["T1"],
                         op0=ALU.mult, op1=ALU.max, w=t1)
                t2 = act(S.activation, sc["T2"], sc["T2"], ACT.Exp, scale=-1.0, w=t1)
                t2 = dve(V.tensor_scalar, sc["T3"], sc["T2"], 2.0, None, ALU.add, w=t2)
                t2 = dve(V.reciprocal, sc["T3"], sc["T3"], w=t2)
                t2 = dve(V.tensor_tensor, sc["Z1"], sc["T2"], sc["T3"], ALU.mult, w=t2)
                t2 = dve(V.tensor_tensor, sc["Z2"], sc["Z1"], sc["Z1"], ALU.mult, w=t2)
                t3 = dve(V.tensor_scalar, sc["T2"], sc["Z2"], 1.0 / 15, None, ALU.mult, w=t2)
                for c in (13, 11, 9, 7, 5, 3):
                    t3 = dve(V.scalar_tensor_tensor, out=sc["T2"], in0=sc["T2"], scalar=1.0 / c, in1=sc["Z2"],
                             op0=ALU.add, op1=ALU.mult, w=t3)
                t3 = dve(V.scalar_tensor_tensor, out=sc["T2"], in0=sc["T2"], scalar=1.0, in1=sc["Z1"],
                         op0=ALU.add, op1=ALU.mult, w=t3)
                t4 = dve(V.tensor_scalar, sc["T1"], sc["T1"], 0.0, None, ALU.max, w=t3)
                t4 = dve(V.scalar_tensor_tensor, out=sc["T1"], in0=sc["T2"], scalar=2.0, in1=sc["T1"],
                         op0=ALU.mult, op1=ALU.add, w=t4)
                tg_ = dve(V.scalar_tensor_tensor, out=s2["GG"], in0=s2["T1"], scalar=-1.0, in1=heads(EA, 2),
                          op0=ALU.mult, op1=ALU.mult, w=[t4, te])

                qx = []
                for g3 in range(3):
                    for j in range(4 * g3, 4 * g3 + 4):
                        cw = [vec["conv", l, k][:, j:j + 1] for k in range(4)]
                        tc = dve(V.tensor_scalar, QX[:, j, :], QP[:, j, 3:259], cw[3], None, ALU.mult,
                                 w=[ready["q"], pz, vec_tok])
                        for k in range(3):
                            tc = dve(V.scalar_tensor_tensor, out=QX[:, j, :], in0=QP[:, j, k:k + T], scalar=cw[k],
                                     in1=QX[:, j, :], op0=ALU.mult, op1=ALU.add, w=tc)
                    qx.append(act(S.activation, QX[:, 4 * g3:4 * g3 + 4, :], QX[:, 4 * g3:4 * g3 + 4, :],
                                  ACT.Silu, w=tc))
                for t in range(2):
                    z1 = act(S.activation, Z[:, t, :], Z[:, t, :], ACT.Silu, w=zt)
                    z1 = pool(G.tensor_tensor, Z[:, t, :].rearrange("p (h n) -> p h n", h=4),
                              Z[:, t, :].rearrange("p (h n) -> p h n", h=4), heads(smv["norm_g", l], 4), ALU.mult,
                              w=[z1, sm_tok])
                    ready["z", t] = z1
                state["gen"], state["spent"] = others(), False
                fill(3)
                qn = []
                for pr in range(4):
                    tmp = flat_[("KBE", "VBT", "KDC", "DD")[pr]]
                    src = QX[:, 2 * pr:2 * pr + 2, :].rearrange("p a b -> p (a b)")
                    t1 = act(S.activation, tmp, src, ACT.Square, w=[qx[pr // 2], att_done])
                    b, bw = bank()
                    t1 = pe(E.matmul, PS[:, b, :], ones, tmp, start=True, stop=True, w=[t1, bw, co], sig=True)
                    fill(1)
                    t1 = act(S.activation, tmp, PS[:, b, :], ACT.Sqrt, bias=epsc[1e-6], w=[t1, epst])
                    drop(b, t1)
                    t1 = dve(V.reciprocal, tmp, tmp, w=t1)
                    qn.append(dve(V.scalar_tensor_tensor, out=src, in0=src, scalar=128.0 ** -0.5 if pr < 2 else 1.0,
                                  in1=tmp, op0=ALU.mult, op1=ALU.mult, w=t1))

                oa = []
                sst = None
                for t in range(2):
                    ts = slice(t * P, t * P + P)
                    h4 = slice(4 * t, 4 * t + 4)
                    tx = pool(G.tensor_copy, W_["GX"], over(sc["GG"][:, h4], P), w=[tg_, oa, qn])
                    b, bw = bank()
                    t1 = pe(E.matmul, PS[:, b, 0:4], cm["tri"], sc["GG"][:, h4], start=True, stop=True,
                            w=[tg_, bw, co], sig=True)
                    t2 = pe(E.matmul, PS[:, b, 4:8], cm["rev"], sc["GG"][:, h4], start=True, stop=True, sig=True)
                    t3 = dve(V.tensor_copy, sc["GC"][:, h4], PS[:, b, 0:4], w=t2)
                    t4 = act(S.activation, sc["EG"][:, h4], PS[:, b, 0:4], ACT.Exp, w=[t2, t3])
                    t5 = act(S.activation, sc["ER"][:, h4], PS[:, b, 4:8], ACT.Exp, w=t2)
                    drop(b, t3, t4, t5)
                    t6 = dve(V.tensor_tensor, sc["RE"][:, h4], sc["BE"][:, h4], sc["EG"][:, h4], ALU.mult, w=[t4, tb])
                    b, bw = bank()
                    pv = PS[:, b, :].rearrange("p (h n) -> p h n", h=4)
                    for h in range(4):
                        t1 = pe(E.matmul, pv[:, h, :], W_["GX"][:, h, :], cm["tri"], start=True, stop=True,
                                w=[tx, bw], sig=True)
                    t7 = act(S.activation, W_["EGR"], pv, ACT.Exp, w=t1)
                    t8 = dve(V.scalar_tensor_tensor, out=W_["DD"], in0=pv, scalar=-1.0, in1=heads(cm["decay"], 4),
                             op0=ALU.mult, op1=ALU.add, w=[t1, qn, t7])
                    drop(b, t7, t8)
                    for h in range(4):
                        td = act(S.activation, W_["DD"][:, h, :], W_["DD"][:, h, :], ACT.Exp,
                                 bias=sc["GC"][:, 4 * t + h:4 * t + h + 1], w=[t8, t3])
                    b1, bw1 = bank()
                    b2, bw2 = bank()
                    kv = PS[:, b1, :].rearrange("p (h n) -> p h n", h=4)
                    vv = PS[:, b2, :].rearrange("p (h n) -> p h n", h=4)
                    for h in range(4):
                        t1 = pe(E.transpose, kv[:, h, :], QX[:, 4 + h, ts], ident, w=[qn, bw1], sig=True)
                    for h in range(4):
                        t2 = pe(E.transpose, vv[:, h, :], QX[:, 8 + h, ts], ident, w=[qx, bw2], sig=True)
                    fill(1)
                    t3_ = dve(V.tensor_tensor, W_["KBE"], kv, over(sc["RE"][:, h4], P), ALU.mult, w=[t1, t6])
                    t4_ = dve(V.tensor_tensor, W_["KDC"], kv, over(sc["ER"][:, h4], P), ALU.mult, w=[t1, t5])
                    t5_ = dve(V.tensor_tensor, W_["VBT"], vv, over(sc["BE"][:, h4], P), ALU.mult, w=[t2, tb])
                    drop(b1, t3_, t4_)
                    drop(b2, t5_)
                    t6_ = pool(G.tensor_tensor, W_["QDT"], QX[:, 0:4, ts], W_["EGR"], ALU.mult, w=[qn, t7])
                    b1, bw1 = bank()
                    b2, bw2 = bank()
                    kk = PS[:, b1, :].rearrange("p (h n) -> p h n", h=4)
                    qk_ = PS[:, b2, :].rearrange("p (h n) -> p h n", h=4)
                    for h in range(4):
                        t1 = pe(E.matmul, kk[:, h, :], QX[:, 4 + h, ts], QX[:, 4 + h, ts], start=True, stop=True,
                                w=bw1, sig=True)
                    for h in range(4):
                        t2 = pe(E.matmul, qk_[:, h, :], QX[:, h, ts], QX[:, 4 + h, ts], start=True, stop=True,
                                w=bw2, sig=True)
                    fill(1)
                    t3 = dve(V.tensor_tensor, W_["LL"], kk, W_["DD"], ALU.mult, w=[t1, td])
                    drop(b1, t3)
                    for h in range(4):
                        t4 = dve(V.scalar_tensor_tensor, out=W_["LL"][:, h, :], in0=W_["LL"][:, h, :],
                                 scalar=sc["BE"][:, 4 * t + h:4 * t + h + 1], in1=cm["strict"],
                                 op0=ALU.mult, op1=ALU.mult, w=t3)
                    t5 = dve(V.tensor_tensor, W_["QKD"], qk_, W_["DD"], ALU.mult, w=[t2, td])
                    drop(b2, t5)
                    b1, bw1 = bank()
                    b2, bw2 = bank()
                    lt = PS[:, b1, :].rearrange("p (h n) -> p h n", h=4)
                    av = PS[:, b2, :].rearrange("p (h n) -> p h n", h=4)
                    for h in range(4):
                        t1 = pe(E.transpose, lt[:, h, :], W_["LL"][:, h, :], ident, w=[t4, bw1], sig=True)
                    for h in range(4):
                        t2 = pe(E.transpose, av[:, h, :], W_["QKD"][:, h, :], ident, w=[t5, bw2], sig=True)
                    fill(1)
                    tl_ = act(S.activation, W_["LT"], lt, ACT.Copy, w=t1)
                    drop(b1, tl_)
                    ta = act(S.activation, W_["AT"], av, ACT.Copy, w=t2)
                    drop(b2, ta)
                    t1 = dve(V.tensor_tensor, W_["BB"], W_["LL"], heads(cm["m1"], 4), ALU.mult, w=t4)
                    tB = dve(V.scalar_tensor_tensor, out=W_["BB"], in0=W_["BB"], scalar=-1.0, in1=heads(ident, 4),
                             op0=ALU.mult, op1=ALU.add, w=t1)
                    t2 = dve(V.tensor_tensor, W_["BT"], W_["LT"], heads(cm["t1"], 4), ALU.mult, w=tl_)
                    tT = dve(V.scalar_tensor_tensor, out=W_["BT"], in0=W_["BT"], scalar=-1.0, in1=heads(ident, 4),
                             op0=ALU.mult, op1=ALU.add, w=t2)
                    msr = [None, None]
                    for n, sz in enumerate((2, 4, 8, 16, 32)):
                        ms = W_[f"MS{n % 2}"]
                        t1 = pool(G.tensor_tensor, ms, W_["LT"], heads(cm[f"t{sz}"], 4), ALU.mult, w=[tl_, msr[n % 2]])
                        b, bw = bank()
                        pv = PS[:, b, :].rearrange("p (h n) -> p h n", h=4)
                        for h in range(4):
                            t2 = pe(E.matmul, pv[:, h, :], ms[:, h, :], W_["BB"][:, h, :], start=True, stop=True,
                                    w=[t1, tB, bw], sig=True)
                        msr[n % 2] = t2
                        fill(1)
                        t3 = act(S.activation, W_["PW"], pv, ACT.Copy, w=t2)
                        drop(b, t3)
                        if sz < 32:
                            b1, bw1 = bank()
                            p1 = PS[:, b1, :].rearrange("p (h n) -> p h n", h=4)
                            for h in range(4):
                                t4 = pe(E.matmul, p1[:, h, :], W_["BT"][:, h, :], W_["PW"][:, h, :], start=True,
                                        stop=True, w=[t3, tT, bw1], sig=True)
                        b2, bw2 = bank()
                        p2 = PS[:, b2, :].rearrange("p (h n) -> p h n", h=4)
                        for h in range(4):
                            t5 = pe(E.matmul, p2[:, h, :], W_["PW"][:, h, :], W_["BT"][:, h, :], start=True,
                                    stop=True, w=[t3, tT, bw2], sig=True)
                        if sz < 32:
                            tB = dve(V.scalar_tensor_tensor, out=W_["BB"], in0=p1, scalar=-1.0, in1=W_["BB"],
                                     op0=ALU.mult, op1=ALU.add, w=t4)
                            drop(b1, tB)
                        tT = dve(V.scalar_tensor_tensor, out=W_["BT"], in0=p2, scalar=-1.0, in1=W_["BT"],
                                 op0=ALU.mult, op1=ALU.add, w=t5)
                        drop(b2, tT)
                        fill(1)
                    b1, bw1 = bank()
                    b2, bw2 = bank()
                    uv = PS[:, b1, :].rearrange("p (h n) -> p h n", h=4)
                    wv = PS[:, b2, :].rearrange("p (h n) -> p h n", h=4)
                    for h in range(4):
                        t1 = pe(E.matmul, uv[:, h, :], W_["BT"][:, h, :], W_["VBT"][:, h, :], start=True, stop=True,
                                w=[tT, t5_, bw1], sig=True)
                    for h in range(4):
                        t2 = pe(E.matmul, wv[:, h, :], W_["KBE"][:, h, :], W_["BT"][:, h, :], start=True, stop=True,
                                w=[t3_, bw2], sig=True)
                    fill(1)
                    tu = act(S.activation, W_["UU"], uv, ACT.Copy, w=t1)
                    drop(b1, tu)
                    tw = act(S.activation, W_["WT"], wv, ACT.Copy, w=t2)
                    drop(b2, tw)
                    bo, bow = bank()
                    for c in range(2):
                        r = slice(64 * c, 64 * c + 64)
                        if sst is None:
                            vn_, tv = flat_["UU"], tu
                        else:
                            b, bw = bank()
                            for h in range(4):
                                t1 = pe(E.matmul, PS[r, b, h * P:h * P + P], W_["WT"][:, h, r], SS[:, h * P:h * P + P],
                                        start=True, stop=True, w=[tw, sst, bw], sig=True)
                            fill(1)
                            vn_ = VN
                            tv = dve(V.scalar_tensor_tensor, out=VN[r, :], in0=PS[r, b, :], scalar=-1.0,
                                     in1=flat_["UU"][r, :], op0=ALU.mult, op1=ALU.add, w=[t1, tu])
                            drop(b, tv)
                        if not (t == 1 and c == 1):
                            b, bw = bank()
                            for h in range(4):
                                t3 = pe(E.matmul, PS[:, b, h * P:h * P + P], W_["KDC"][r, h, :], vn_[r, h * P:h * P + P],
                                        start=True, stop=True, w=[tv, t4_, bw], sig=True)
                        for h in range(4):
                            o_ = PS[r, bo, h * P:h * P + P]
                            if sst is not None:
                                pe(E.matmul, o_, W_["QDT"][:, h, r], SS[:, h * P:h * P + P], start=True, stop=False,
                                   w=[t6_, bow])
                            t2 = pe(E.matmul, o_, W_["AT"][r, h, r], vn_[r, h * P:h * P + P], start=sst is None,
                                    stop=True, w=[ta, tv, bow], sig=True)
                        if not (t == 1 and c == 1):
                            fill(1)
                            if sst is None:
                                sn = dve(V.tensor_copy, SS, PS[:, b, :], w=t3)
                            else:
                                for h in range(4):
                                    hs_ = slice(h * P, h * P + P)
                                    sn = dve(V.scalar_tensor_tensor, out=SS[:, hs_], in0=SS[:, hs_],
                                             scalar=W_["EGR"][:, h, 64 * c + 63:64 * c + 64], in1=PS[:, b, hs_],
                                             op0=ALU.mult, op1=ALU.add, w=[t3, t2, t7])
                            drop(b, sn)
                            sst = sn
                    ov = PS[:, bo, :].rearrange("p (h n) -> p h n", h=4)
                    t1 = act(S.activation, W_["GX"], ov, ACT.Square, w=[t2, tx])
                    t1 = dve(V.tensor_reduce, sc["Z1"][:, 0:4], W_["GX"], AX, ALU.add, w=t1)
                    t1 = act(S.activation, sc["Z1"][:, 0:4], sc["Z1"][:, 0:4], ACT.Sqrt, bias=epsc[1e-6],
                             scale=1.0 / 128, w=[t1, epst])
                    t1 = dve(V.reciprocal, sc["Z1"][:, 0:4], sc["Z1"][:, 0:4], w=t1)
                    t1 = dve(V.tensor_tensor, W_["LL"], ov, over(sc["Z1"][:, 0:4], P), ALU.mult, w=t1)
                    drop(bo, t1)
                    t1 = dve(V.tensor_tensor, flat_["LL"], flat_["LL"], Z[:, t, :], ALU.mult, w=[t1, ready["z", t]])
                    fill(1)
                    tk = to_hl(lambda k: W_["LL"][:, k, :], 4, t, *OH["a"], 0, t1)
                    for k, v in tk.items():
                        oa.append(v)
                        ready["o", k, t] = v
                while not state["spent"]:
                    fill(1)


                gate_bias("a", bgt["b"])
                run(branch("a", *OH["a"], lambda kt, t: ready["o", kt, t]))
                load_gb_after(bgt["a"], bgt["c"], a["ln2_g"][l:l + 1, :], a["ln2_b"][l:l + 1, :])
                mt = {}
                for t in range(2):
                    for k, v in to_hl(lambda k: MG[:, t, k * P:k * P + P], 8, t, XTH, XTL, 0,
                                      mgt[t, 0], mgt[t, 1]).items():
                        mt[k, t] = v
                run(out_rows(a["w_out"][l], 8, XTH, XTL, lambda kt, t: mt[kt, t], 1.0, True))


            def rms_turn(g):
                HN = at(80 * 1024, "HN", [P, 2, D])
                load_gb(g)
                for t in range(2):
                    o = 40 + 2 * t
                    t1 = act(S.activation, HN[:, t, :], X[:, t, :], ACT.Square, accum_out=ST[:, o:o + 1], w=s["x"][t])
                    t2 = power(ST[:, o + 1:o + 2], ST[:, o:o + 1], 1.0 / D, 1e-6, t1, epst)
                    t3 = dve(V.scalar_tensor_tensor, out=HN[:, t, :], in0=X[:, t, :], scalar=ST[:, o + 1:o + 2],
                             in1=GB[:, 0, :], op0=ALU.mult, op1=ALU.mult, w=[t1, t2, gbt[0]])
                    for k, v in to_hl(lambda k: HN[:, t, k * P:k * P + P], 8, t, XTH, XTL, 0, t3).items():
                        s["xt"][k, t] = v
                    s["gbr"] = t3
                gbt[0] = s["gbr"]

            def split_sb(src, hi, lo, w):
                t1 = act(S.activation, hi, src, ACT.Copy, w=w)
                return [t1, dve(V.tensor_tensor, lo, src, hi.bitcast(F), ALU.subtract, w=[w, t1])]

            def mixer_even():
                K = 1024
                YTH = at(0, "YTH", [P, 8, T], R)
                YTL = at(8 * K, "YTL", [P, 8, T], R)
                BGt = at(16 * K, "BGt", [P, 4, T])
                CG = at(20 * K, "CG", [P, 4, T])
                CV = at(24 * K, "CV", [P, 4, 2 + T])
                VP = at(29 * K, "VP", [P, 4, 16 + T])
                S0 = at(34 * K, "S0", [P, 16 + T])
                S1 = at(36 * K, "S1", [P, 16 + T])
                PL = at(38 * K, "PL", [P, 4, T])
                YC = at(42 * K, "YC", [P, 4, T])
                PW_ = at(46 * K, "PW_", [P, 4, P])
                w = a["w_in_even_2"][0]
                pw = q.dma("pool", "ld1", PW_, a["pool_w_2"][0].rearrange("g c d -> c g d"))
                pads = [pool(G.memset, CV[:, :, 0:2], 0.0), pool(G.memset, VP[:, :, 0:16], 0.0),
                        pool(G.memset, S0[:, 0:16], 0.0), pool(G.memset, S1[:, 0:16], 0.0)]
                tk = {}
                for part in range(4):
                    bks = [bank() for _ in range(4)]
                    run(cols(w, 512 * part, 4, bks, xtok))
                    for j in range(4):
                        src = PS[:, bks[j][0], 0:T]
                        d_ = done["c", j]
                        if part == 0:
                            t1 = act(S.activation, BGt[:, j, :], src, ACT.Copy, w=d_)
                        elif part == 1:
                            t1 = act(S.activation, CG[:, j, :], src, ACT.Copy, w=d_)
                        elif part == 2:
                            t1 = dve(V.tensor_tensor, CV[:, j, 2:2 + T], src, CG[:, j, :], ALU.mult, w=[d_, tk[1, j]])
                        else:
                            t1 = act(S.activation, VP[:, j, 16:16 + T], src, ACT.Copy, w=d_)
                        tk[part, j] = t1
                        drop(bks[j][0], t1)
                yt = {}
                for j in range(4):
                    cw = [vec["conva", k][:, j:j + 1] for k in range(3)]
                    t1 = dve(V.tensor_scalar, YC[:, j, :], CV[:, j, 2:2 + T], cw[2], None, ALU.mult,
                             w=[tk[2, j], pads, vec_tok])
                    for k in range(2):
                        t1 = dve(V.scalar_tensor_tensor, out=YC[:, j, :], in0=CV[:, j, k:k + T], scalar=cw[k],
                                 in1=YC[:, j, :], op0=ALU.mult, op1=ALU.add, w=t1)
                    t1 = dve(V.tensor_tensor, YC[:, j, :], YC[:, j, :], BGt[:, j, :], ALU.mult, w=[t1, tk[0, j]])
                    yt[j] = split_sb(YC[:, j, :], YTH[:, j, :], YTL[:, j, :], t1)
                for g in range(4):
                    win = 2 ** (g + 1)
                    cur, t1 = VP[:, g, :], [tk[3, g], pads]
                    for n in range(g + 1):
                        st = 2 ** n
                        nx = (S0, S1)[n % 2]
                        t1 = dve(V.tensor_tensor, nx[:, 16:16 + T], cur[:, 16:16 + T], cur[:, 16 - st:16 + T - st],
                                 ALU.add, w=t1)
                        cur = nx
                    c0 = C_CNT + 16 * g
                    t2 = dve(V.scalar_tensor_tensor, out=PL[:, g, 16:T], in0=cur[:, 32:16 + T], scalar=1.0 / win,
                             in1=VP[:, g, 32:16 + T], op0=ALU.mult, op1=ALU.subtract, w=t1)
                    t3 = dve(V.tensor_tensor, PL[:, g, 0:16], cur[:, 16:32], CO[:, c0:c0 + 16], ALU.mult, w=[t1, co])
                    t3 = dve(V.tensor_tensor, PL[:, g, 0:16], PL[:, g, 0:16], VP[:, g, 16:32], ALU.subtract, w=t3)
                    b, bw = bank()
                    t4 = pe(E.matmul, PS[:, b, 0:T], PW_[:, g, :], PL[:, g, :], start=True, stop=True,
                            w=[pw, t2, t3, bw], sig=True)
                    sc_ = vec["pool_scale"][:, g:g + 1]
                    t5 = act(S.activation, YTH[:, 4 + g, :], PS[:, b, 0:T], ACT.Copy, scale=sc_, w=t4)
                    t6 = dve(V.scalar_tensor_tensor, out=YTL[:, 4 + g, :], in0=PS[:, b, 0:T], scalar=sc_,
                             in1=YTH[:, 4 + g, :].bitcast(F), op0=ALU.mult, op1=ALU.subtract, w=[t4, t5])
                    drop(b, t5, t6)
                    yt[4 + g] = [t5, t6]
                run(out_rows(a["w_out_even_2"][0], 8, YTH, YTL, lambda kt, t: yt[kt], 1.0, False))

            def mixer_odd():
                K = 1024
                W1 = [at(16 * K * n, f"W1{n}", [P, 16, 256]) for n in range(2)]
                OTH, OTL = at(32 * K, "OTH", [P, 8, T], R), at(40 * K, "OTL", [P, 8, T], R)
                RT = [at(48 * K + 3584 * n, f"RT{n}", [P, 14, 64]) for n in range(2)]
                FB = [at((48 + 4 * n) * K, f"FB{n}", [P, 16, 2, 32]) for n in range(2)]
                RO = [at(56 * K + 3584 * n, f"RO{n}", [P, 14, 64]) for n in range(2)]
                TM = [at(int(63.5 * K) + 1792 * n, f"TM{n}", [P, 14, 32]) for n in range(2)]
                GH = at(int(63.5 * K), "GH", [P, 2, 2, 2, 4, 32])
                VV = at(int(67.5 * K), "VV", [P, 3, 2, P])
                ZC = at(int(70.5 * K), "ZC", [P, 4, 30 + T])
                ZA = at(int(75.5 * K), "ZA", [P, 4, T])
                SG_ = at(int(79.5 * K), "SGc", [P, 4, T])
                ZN = at(int(83.5 * K), "ZN", [P, 512])
                ZS = at(int(85.5 * K), "ZS", [P, 4, T])
                PRS = at(int(89.5 * K), "PRS", [P, 2, 2, 2, 64])
                W2 = at(int(91.5 * K), "W2", [P, 2, 2, 64])
                VCB = at(int(85.5 * K), "VCB", [P, 4, 2, 64])
                QTT, KTT = at(0, "QTT", [P, 4, T]), at(4 * K, "KTT", [P, 4, T])
                PA = [at((8 + 4 * n) * K, f"PA{n}", [P, 1024]) for n in range(2)]
                PB = [at((16 + 4 * n) * K, f"PB{n}", [P, 1024]) for n in range(2)]
                KD2 = at(24 * K, "KD2", [P, 2, 4, 2, 64])
                KCN = at(28 * K, "KCN", [P, 2, 2, 64])
                KCT = at(29 * K, "KCT", [P, 2, 32])
                PTC = at(int(29.5 * K), "PTC", [P, 4, P])
                PCM = at(int(31.5 * K), "PCM", [P, 4, 32])
                NW = GB[:, 1, 0:768].rearrange("p (h d) -> p h d", d=64)
                GA = SX[:, 256:304].rearrange("p (t h k) -> p t h k", t=2, k=3)
                MS = SX[:, 304:336]
                w = a["w_in_odd_2"][0]
                w1 = [q.dma("pool", f"ld{1 + n}", W1[n], a["cmp_w1_2"][0, n].rearrange("(j p) n -> p j n", p=P), s["xt"][7, 1], s["x"][1])
                      for n in range(2)]
                w2 = q.dma("pool", "ld3", W2, a["cmp_w2_2"][0].rearrange("k (m p) d -> p k m d", p=P), s["x"][1])
                vz = pool(G.memset, VCB, 0.0, w=[s["xt"][7, 0], s["xt"][7, 1]])
                zp = pool(G.memset, ZC[:, :, 0:30], 0.0, w=s["x"][1])
                nw = [pool(G.tensor_copy, NW[:, 0:8, :], heads(smv["q_norm"], 8), w=[sm_tok, gbt[0]]),
                      pool(G.tensor_copy, NW[:, 8:10, :], heads(smv["k_norm"][:, 0:64], 2), w=sm_tok),
                      pool(G.tensor_copy, NW[:, 10:12, :], heads(smv["k_norm"][:, 64:128], 2), w=sm_tok)]
                zc = []
                for part, c0 in ((1, 1816), (0, 1304)):
                    bks = [bank() for _ in range(4)]
                    run(cols(w, c0, 4, bks, xtok))
                    for j in range(4):
                        src = PS[:, bks[j][0], 0:T]
                        if part == 1:
                            t1 = act(S.activation, SG_[:, j, :], src, ACT.Sigmoid, w=done["c", j])
                            sg = t1
                        else:
                            t1 = dve(V.tensor_tensor, ZC[:, j, 30:30 + T], src, SG_[:, j, :], ALU.mult,
                                     w=[done["c", j], sg, zp])
                            zc.append(t1)
                        drop(bks[j][0], t1)
                zt = {}

                def conv():
                    for k in range(31):
                        for j in range(4):
                            cw = vec["dw", k][:, j:j + 1]
                            if k == 0:
                                zt[j] = dve(V.tensor_scalar, ZA[:, j, :], ZC[:, j, 0:T], cw,
                                            vec["conf_b"][:, j:j + 1], ALU.mult, ALU.add, w=[zc, zp, vec_tok])
                            else:
                                zt[j] = dve(V.scalar_tensor_tensor, out=ZA[:, j, :], in0=ZC[:, j, k:k + T], scalar=cw,
                                            in1=ZA[:, j, :], op0=ALU.mult, op1=ALU.add, w=zt[j])
                        if k % 2 == 1:
                            yield

                cg = conv()
                left = [True]

                def fill(n):
                    for _ in range(n):
                        if left[0]:
                            try:
                                next(cg)
                            except StopIteration:
                                left[0] = False

                def project(c0, wd):
                    bks = [bank(), bank()]
                    for _ in rows(w, 8, c0, [(0, wd, bks)], XTH, XTL, xtok):
                        fill(1)
                    return bks

                rt = {0: [], 1: []}
                vt = {0: [], 1: []}
                bks = project(0, 512)
                for t in range(2):
                    t1 = act(S.activation, RT[t][:, 0:8, :], PS[:, bks[t][0], :].rearrange("p (h d) -> p h d", d=64),
                             ACT.Copy, w=done[t])
                    drop(bks[t][0], t1)
                    rt[t].append(t1)
                bks = project(512, 512)
                for t in range(2):
                    pv = PS[:, bks[t][0], :].rearrange("p (x g d) -> p x g d", x=4, d=64)
                    t1 = act(S.activation, RT[t][:, 12:14, :], pv[:, 0], ACT.Copy, w=done[t])
                    t2 = act(S.activation, VV[:, 2, t, :], PS[:, bks[t][0], 128:256], ACT.Copy, w=done[t])
                    t3 = act(S.activation, RT[t][:, 8:10, :], pv[:, 2], ACT.Copy, w=done[t])
                    t4 = act(S.activation, VV[:, 0, t, :], PS[:, bks[t][0], 384:512], ACT.Copy, w=done[t])
                    drop(bks[t][0], t4)
                    rt[t] += [t1, t3]
                    vt[t] += [t2, t4]
                bks = project(1024, 280)
                gt_ = []
                for t in range(2):
                    t1 = act(S.activation, RT[t][:, 10:12, :],
                             PS[:, bks[t][0], 0:128].rearrange("p (g d) -> p g d", d=64), ACT.Copy, w=done[t])
                    t2 = act(S.activation, VV[:, 1, t, :], PS[:, bks[t][0], 128:256], ACT.Copy, w=done[t])
                    t3 = act(S.activation, SX[:, 256 + 24 * t:280 + 24 * t], PS[:, bks[t][0], 256:280], ACT.Sigmoid,
                             w=done[t])
                    drop(bks[t][0], t3)
                    rt[t].append(t1)
                    vt[t].append(t2)
                    gt_.append(t3)
                ro, wr = [], []
                for t in range(2):
                    rm = RO[t][:, 0:12, :]
                    t1 = act(S.activation, rm, RT[t][:, 0:12, :], ACT.Square, w=rt[t])
                    ms = MS[:, 12 * t:12 * t + 12]
                    t1 = dve(V.tensor_reduce, ms, rm, AX, ALU.add, w=t1)
                    t1 = act(S.activation, ms, ms, ACT.Sqrt, bias=epsc[1e-6], scale=1.0 / 64, w=[t1, epst])
                    t1 = dve(V.reciprocal, ms, ms, w=t1)
                    x12 = RT[t][:, 0:12, :]
                    t1 = dve(V.tensor_tensor, x12, x12, over(ms, 64), ALU.mult, w=t1)
                    t1 = dve(V.tensor_tensor, x12, x12, NW, ALU.mult, w=[t1, nw])
                    co_, si_ = (heads(CO[:, c_ + 32 * t:c_ + 32 * t + 32], 14) for c_ in (C_COS, C_SIN))
                    x1, x2 = RT[t][:, :, 0:32], RT[t][:, :, 32:64]
                    y1, y2 = RO[t][:, :, 0:32], RO[t][:, :, 32:64]
                    t2 = pool(G.tensor_tensor, TM[0], x2, si_, ALU.mult, w=[t1, co, ro])
                    t3 = dve(V.tensor_tensor, y1, x1, co_, ALU.mult, w=t1)
                    t4 = dve(V.tensor_tensor, y1, y1, TM[0], ALU.subtract, w=[t2, t3])
                    t5 = pool(G.tensor_tensor, TM[1], x1, si_, ALU.mult, w=[t1, ro])
                    t6 = dve(V.tensor_tensor, y2, x2, co_, ALU.mult, w=t1)
                    t7 = dve(V.tensor_tensor, y2, y2, TM[1], ALU.add, w=[t5, t6])
                    ro.append([t4, t7])
                    for n, src in ((0, RO[t][:, 12:14, :].rearrange("p g d -> p (g d)")), (1, VV[:, 2, t, :])):
                        o = 1536 + n * T * P + t * P * P
                        wr.append(q.dma("pool", f"ld{4 + 2 * t + n}", scratch[o:o + P * P].rearrange("(p n) -> p n", p=P),
                                        src, t4, t7, vt[t]))
                fb = []
                for n in range(2):
                    rd = [q.dma("pool", f"ld{8 + 2 * n + g}", PRS[:, n, g],
                                bass.AP(scratch.tensor, 1536 + n * T * P + 64 * g, [[2 * P, P], [P, 2], [1, 64]]), wr)
                          for g in range(2)]
                    fm = pool(G.memset, FB[n], 0.0, w=ro)
                    b, bw = bank()
                    for g in range(2):
                        t1 = pe(E.transpose, PS[:, b, g * P:g * P + P], PRS[:, n, g].rearrange("p b d -> p (b d)"),
                                ident, w=[rd, bw], sig=True)
                    base_ = PS[:, b, 0:256]
                    src = bass.AP(base_.tensor, base_.offset, [list(base_.ap[0]), [1, 16], [P, 2], [8, 15]])
                    po = vec["cmp_pos"][:, 16 * n:16 * n + 16].unsqueeze(2).unsqueeze(3).to_broadcast([P, 16, 2, 15])
                    t2 = dve(V.tensor_tensor, FB[n][:, :, :, 0:15], src, po, ALU.add, w=[t1, fm, vec_tok])
                    drop(b, t2)
                    fb.append(t2)
                    fill(1)
                gh = []
                for n in range(2):
                    for m in range(2):
                        b, bw = bank()
                        for j in range(16):
                            t1 = pe(E.matmul, PS[:, b, 0:64], W1[n][:, j, m * P:m * P + P],
                                    FB[n][:, j].rearrange("p g n -> p (g n)"), start=j == 0, stop=j == 15,
                                    w=[fb[n], w1[n], bw], sig=j == 15)
                        src = PS[:, b, 0:64].rearrange("p (g n) -> p g n", g=2).unsqueeze(2).to_broadcast([P, 2, 4, 32])
                        t2 = act(S.activation, GH[:, n, m], src, ACT.Gelu_apprx_tanh, w=[t1, ro])
                        drop(b, t2)
                        gh.append(t2)
                        thid = t1
                b, bw = bank()
                for n in range(2):
                    for g in range(2):
                        for m in range(2):
                            t1 = pe(E.matmul, PS[:, b, (2 * n + g) * 64:(2 * n + g) * 64 + 64],
                                    GH[:, n, m, g].rearrange("p c n -> p (c n)"), W2[:, n, m, :], start=m == 0,
                                    stop=m == 1, w=[gh, w2, bw], sig=m == 1)
                vcc = []
                for i in range(4):
                    r = slice(32 * i, 32 * i + 32)
                    t2 = act(S.activation, VCB[r, i], PS[r, b, 128:256].rearrange("p (g d) -> p g d", g=2), ACT.Copy,
                             w=[t1, vz])
                    vcc.append(t2)
                kr = PS[:, b, 0:128].rearrange("p (g d) -> p g d", g=2)
                t3 = act(S.activation, KCN[:, :, 0, :], kr, ACT.Square, w=[t1, thid])
                ms = MS[:, 24:26]
                t3 = dve(V.tensor_reduce, ms, KCN[:, :, 0, :], AX, ALU.add, w=t3)
                t3 = act(S.activation, ms, ms, ACT.Sqrt, bias=epsc[1e-6], scale=1.0 / 64, w=[t3, epst])
                t3 = dve(V.reciprocal, ms, ms, w=t3)
                t4 = dve(V.tensor_tensor, KCN[:, :, 0, :], kr, over(ms, 64), ALU.mult, w=[t3, t1])
                drop(b, t2, t4)
                t4 = dve(V.tensor_tensor, KCN[:, :, 0, :], KCN[:, :, 0, :], heads(smv["k_norm"][:, 128:192], 2),
                         ALU.mult, w=[t4, sm_tok])
                t4 = dve(V.tensor_copy, KCN[:, :, 1, :], KCN[:, :, 0, :], w=t4)
                b, bw = bank()
                for g in range(2):
                    t1 = pe(E.transpose, PS[:, b, g * P:g * P + P], KCN[:, g].rearrange("p c d -> p (c d)"), ident,
                            w=[t4, bw], sig=True)
                kct = act(S.activation, KCT, PS[:, b, 0:256].rearrange("p (g n) -> p g n", g=2)[:, :, 0:32], ACT.Copy,
                          w=t1)
                drop(b, kct)
                qkt = []
                for t in range(2):
                    kd = pool(G.tensor_copy, KD2[:, t], RO[t][:, 8:12, :].unsqueeze(2).to_broadcast([P, 4, 2, 64]),
                              w=[ro[t], thid])
                    for src, dst, wt in ((lambda k: RO[t][:, 2 * k:2 * k + 2, :].rearrange("p h d -> p (h d)"), QTT, ro[t]),
                                         (lambda k: KD2[:, t, k].rearrange("p c d -> p (c d)"), KTT, kd)):
                        b, bw = bank()
                        for k in range(4):
                            t1 = pe(E.transpose, PS[:, b, k * P:k * P + P], src(k), ident, w=[wt, bw], sig=True)
                        t2 = act(S.activation, dst[:, :, t * P:t * P + P], PS[:, b, :].rearrange("p (k n) -> p k n", k=4),
                                 ACT.Copy, w=[t1, thid])
                        drop(b, t2)
                        qkt.append(t2)
                    fill(1)
                ptc = {}
                prev = None
                for n, (t, par) in enumerate(((0, 0), (0, 1), (1, 0), (1, 1))):
                    r = slice(64 * par, 64 * par + 64)
                    b, bw = bank()
                    for i in range(4):
                        t1 = pe(E.matmul, PS[:, b, 32 * i:32 * i + 32], QTT[r, i, t * P:t * P + P],
                                KCT[r, i // 2, :], start=True, stop=True, w=[qkt, kct, bw], sig=True)
                    sv = PS[:, b, 0:128].rearrange("p (h n) -> p h n", h=4)
                    t2 = dve(V.tensor_tensor, PCM, sv, heads(CO[:, C_CMB + 32 * t:C_CMB + 32 * t + 32], 4), ALU.add,
                             w=[t1, prev, thid, co])
                    drop(b, t2)
                    m_, su = SX[:, 128:132], SX[:, 132:136]
                    t3 = dve(V.tensor_reduce, m_, PCM, AX, ALU.max, w=t2)
                    t3 = dve(V.tensor_scalar, m_, m_, -0.125, None, ALU.mult, w=t3)
                    for i in range(4):
                        t4 = act(S.activation, PCM[:, i, :], PCM[:, i, :], ACT.Exp, bias=m_[:, i:i + 1], scale=0.125, w=t3)
                    t4 = dve(V.tensor_tensor, PCM, PCM, heads(CO[:, C_CM1 + 32 * t:C_CM1 + 32 * t + 32], 4), ALU.mult, w=t4)
                    t5 = dve(V.tensor_reduce, su, PCM, AX, ALU.add, w=t4)
                    t5 = dve(V.tensor_scalar, su, su, 1e-30, None, ALU.max, w=t5)
                    t5 = dve(V.reciprocal, su, su, w=t5)
                    t5 = dve(V.tensor_tensor, su, su, GA[:, t, par:8:2, 0], ALU.mult, w=[t5, gt_])
                    t5 = dve(V.tensor_tensor, PCM, PCM, over(su, 32), ALU.mult, w=t5)
                    b, bw = bank()
                    t6 = pe(E.transpose, PS[:, b, 0:P], PCM.rearrange("p h n -> p (h n)"), ident, w=[t5, bw], sig=True)
                    t7 = act(S.activation, PTC[:, n, :], PS[:, b, 0:P], ACT.Copy, w=t6)
                    drop(b, t7)
                    prev = t6
                    ptc[t, par] = (n, t7)
                    fill(1)
                ot = {0: [], 1: []}

                def item(t, hs, k):
                    par = hs[0] % 2
                    r = slice(64 * par, 64 * par + 64)
                    nk = (t + 1) * P
                    pv = PA[k % 2][:, 0:4 * nk].rearrange("p (x h n) -> p x h n", x=2, h=2)
                    rcs = []
                    bb = {}
                    for x in range(2):
                        if t == 1 or x == 0:
                            bb[x] = bank()
                        b, bw = bb[x] if x in bb else bb[0]
                        for n, h in enumerate(hs):
                            c0 = (0 if t else 2 * x * P) + n * nk
                            o_ = PS[:, b, c0:c0 + nk]
                            pe(E.matmul, o_, QTT[r, h // 2, t * P:t * P + P], KTT[r, 2 * x + h // 4, 0:nk],
                               start=True, stop=t == 1, w=[qkt, bw], skip_group_check=True)
                            t1 = pe(E.matmul, o_[:, t * P:t * P + P], ident, cm["causal"], start=False, stop=True,
                                    sig=True, skip_group_check=True)
                        bb["t", x] = t1
                    if t == 0:
                        views = [(PS[:, bb[0][0], :].rearrange("p (h n) -> p h n", h=4),
                                  pv.rearrange("p x h n -> p (x h) n"), 4, [bb["t", 0], bb["t", 1]], 0)]
                    else:
                        views = [(PS[:, bb[x][0], :].rearrange("p (h n) -> p h n", h=2), pv[:, x], 2, bb["t", x], x)
                                 for x in range(2)]
                    tn = []
                    for i, (sv, dst, nh, wt, x) in enumerate(views):
                        rc, te, tr = softmax_rows(sv, nh, dst, 2 * (k % 2) + i, 0.125, wt)
                        drop(bb[x][0], te)
                        g_ = GA[:, t, hs[0]:hs[0] + 3:2, :]
                        for x_ in ((0, 1) if t == 0 else (x,)):
                            rv = rc[:, 2 * x_:2 * x_ + 2] if t == 0 else rc
                            tr = dve(V.tensor_tensor, rv, rv, g_[:, :, 1 + x_], ALU.mult, w=[tr, gt_])
                        tn.append(dve(V.tensor_tensor, dst, dst, over(rc, nk), ALU.mult, w=tr))
                    yield
                    pt = PB[k % 2]
                    tp = []
                    for x in range(2):
                        if t == 1 or x == 0:
                            b, bw = bank()
                            i = 0
                        for n in range(2):
                            for kt in range(t + 1):
                                t1 = pe(E.transpose, PS[:, b, i * P:i * P + P], pv[:, x, n, kt * P:kt * P + P], ident,
                                        w=[tn, bw], sig=True)
                                i += 1
                        if i == 4:
                            x0 = x if t == 1 else 0
                            tp.append(act(S.activation, pt[:, x0 * 512:x0 * 512 + 512], PS[:, b, :], ACT.Copy, w=t1))
                            drop(b, tp[-1])
                    yield
                    nc_, tc = ptc[t, par]
                    b, bw = bank()
                    for n, h in enumerate(hs):
                        o_ = PS[r, b, n * P:n * P + P]
                        g = h // 4
                        for x in range(2):
                            for kt in range(t + 1):
                                c0 = (x * 2 * (t + 1) + n * (t + 1) + kt) * P
                                pe(E.matmul, o_, VV[:, x, kt, 64 * g:64 * g + 64], pt[:, c0:c0 + P],
                                   start=x == 0 and kt == 0, stop=False, w=[tp, vt[0], vt[1], bw])
                        i = h // 2
                        t1 = pe(E.matmul, o_, VCB[:, i, g, :], PTC[:, nc_, :],
                                start=False, stop=True, w=[tc, vcc], sig=True)
                    ot[t].append(split_out(b, 64 * par, 64, 2, hs[0] // 2, t, OTH, OTL, t1))
                    yield

                items = [(t, hs) for t in range(2) for hs in ([0, 2], [4, 6], [1, 3], [5, 7])]
                pipeline([item(t, hs, k) for k, (t, hs) in enumerate(items)], fill, 1)
                while left[0]:
                    fill(1)
                cf = {}
                for t in range(2):
                    b, bw = bank()
                    for j in range(4):
                        t1 = pe(E.transpose, PS[:, b, j * P:j * P + P], ZA[:, j, t * P:t * P + P], ident,
                                w=[zt[j], bw], sig=True)
                    o = 44 + 8 * t
                    t2 = dve(V.bn_stats, ST[:, o:o + 6], PS[:, b, :], w=t1)
                    t2 = dve(V.bn_aggr, ST[:, o + 6:o + 8], ST[:, o:o + 6], w=t2)
                    t3 = power(ST[:, o:o + 1], ST[:, o + 7:o + 8], 1.0, 1e-6, t2, epst)
                    t4 = dve(V.tensor_scalar, ZN, PS[:, b, :], ST[:, o + 6:o + 7], ST[:, o:o + 1],
                             ALU.subtract, ALU.mult, w=[t2, t3, cf.get(0)])
                    drop(b, t4)
                    b, bw = bank()
                    for j in range(4):
                        t1 = pe(E.transpose, PS[:, b, j * P:j * P + P], ZN[:, j * P:j * P + P], ident,
                                w=[t4, bw], sig=True)
                    for j in range(4):
                        t5 = act(S.activation, ZS[:, j, t * P:t * P + P], PS[:, b, j * P:j * P + P], ACT.Silu,
                                 bias=vec["conf_lb"][:, j:j + 1], scale=vec["conf_lg"][:, j:j + 1], w=[t1, vec_tok])
                    drop(b, t5)
                    ts = slice(t * P, t * P + P)
                    cf[t] = split_sb(ZS[:, :, ts], OTH[:, 4:8, ts], OTL[:, 4:8, ts], t5)
                run(out_rows(a["w_out_odd_2"][0], 8, OTH, OTL, lambda kt, t: ot[t] if kt < 4 else cf[t], 1.0, False))
                gbt[0] = [gbt[0], ro]

            YH = PP = PT = SC = None

            def store():
                toks = [q.dma("sp", "st", out[0, t * P:(t + 1) * P, :], X[:, t, :], s["x"][t]) for t in range(2)]
                q.wait("sp", toks[-1])

            x_in()
            for l in range(2):
                load_gb(a["ln1_g"][l:l + 1, :], a["ln1_b"][l:l + 1, :])
                x_turn(ALPHA)
                ffn(a["w_ff1_in"][l], a["w_ff1_in"][l], a["w_ff1_out"][l], 0, 4096, 4096, xtok, 0.5, True, f"a{l}")
                x_turn(ALPHA)
                mixer1(l)
                load_gb(a["ln3_g"][l:l + 1, :], a["ln3_b"][l:l + 1, :])
                x_turn(ALPHA)
                ffn(a["w_ff2_in"][l], a["w_ff2_in"][l], a["w_ff2_out"][l], 0, 4096, 4096, xtok, 0.5, True, f"c{l}")
            for i in range(2):
                rms_turn(a["norm_mix_2"][i:i + 1, :])
                (mixer_even, mixer_odd)[i]()
                rms_turn(a["norm_ffn_2"][i:i + 1, :])
                ffn(a["ffn_gate_2"][i], a["ffn_up_2"][i], a["ffn_down_2"][i], 0, 0, 2816, xtok, 1.0, False, "g")
            store()
            return q

        trace(None)
        made_units = list(record)
        q = trace(made_units)

        block = ctx.enter_context(nc.Block())

        @block.sync
        def _(e):
            q.play("sp", e)

        @block.gpsimd
        def _(e):
            q.play("pool", e)

        @block.scalar
        def _(e):
            q.play("act", e)

        @block.vector
        def _(e):
            q.play("dve", e)

        @block.tensor
        def _(e):
            q.play("pe", e)


_INS = ['x', 'ln1_g', 'ln1_b', 'w_ff1_in', 'w_ff1_out', 'w_in', 'b_in', 'conv_w', 'a_log', 'dt_bias',
        'gdn_norm_g', 'rel_bias', 'sinks', 'w_gate', 'b_gate', 'w_br_a', 'w_br_b', 'w_br_c', 'w_out',
        'ln2_g', 'ln2_b', 'w_ff2_in', 'w_ff2_out', 'ln3_g', 'ln3_b', 'norm_mix_2', 'norm_ffn_2',
        'ffn_gate_2', 'ffn_up_2', 'ffn_down_2', 'w_in_even_2', 'conv_a_2', 'pool_w_2', 'pool_scale_2',
        'w_out_even_2', 'w_in_odd_2', 'q_norm_2', 'k_norm_2', 'cmp_pos_2', 'cmp_w1_2', 'cmp_w2_2',
        'conf_dw_2', 'conf_dw_b_2', 'conf_ln_g_2', 'conf_ln_b_2', 'w_out_odd_2']


def kernel(**inputs):
    import numpy as _np
    import concourse.bacc as _bacc
    from concourse import mybir as _mybir
    from concourse.bass_utils import run_bass_kernel_spmd as _run

    nc = _bacc.Bacc("TRN2", target_bir_lowering=False, num_devices=1)
    arrays, aps = {}, {}
    for name in _INS + ["consts"]:
        v = shape_constants() if name == "consts" else _np.ascontiguousarray(inputs[name])
        arrays[f"in_{name}"] = v
        aps[name] = nc.dram_tensor(f"in_{name}", v.shape, _mybir.dt.from_np(v.dtype), kind="ExternalInput").ap()
    o = nc.dram_tensor("out_0", (1, T, D), _mybir.dt.float32, kind="ExternalOutput").ap()
    build(nc, aps, o)
    r = _run(nc, [arrays], core_ids=[0])
    return r.results[0]["out_0"]
```

```python
from contextlib import ExitStack

import numpy as np

import concourse.bass as bass
from concourse import mybir

ALU = mybir.AluOpType
ACT = mybir.ActivationFunctionType
AX = mybir.AxisListType.X
F = mybir.dt.float32
R = mybir.dt.float32r

P = 128
T = 256
D = 1024
NEG = -1e30
ALPHA = 4.0 ** 0.25

KU = 2
UW = 520
RAW = 4
SPL = 6
LEAD = 4

CMAT = ["ident", "flip", "tri", "rev", "strict", "decay", "pair", "causal",
        "m1", "t1", "t2", "t4", "t8", "t16", "t32", "ali1", "ali0"]
C_CM1 = len(CMAT) * P
C_CMB = C_CM1 + 2 * 32
C_COS = C_CMB + 2 * 32
C_SIN = C_COS + 2 * 32
C_CNT = C_SIN + 2 * 32
C_ONE = C_CNT + 4 * 16
NCONST = C_ONE + P


def shape_constants():
    i = np.arange(P)[:, None]
    j = np.arange(P)[None, :]
    same = i // 64 == j // 64
    zero = np.zeros((P, P), np.float32)

    def level(s, a, b):
        return ((a // (2 * s) == b // (2 * s)) & (a % (2 * s) >= s) & (b % (2 * s) < s)).astype(np.float32)

    m = {
        "ident": (i == j).astype(np.float32),
        "flip": (i + j == P - 1).astype(np.float32),
        "tri": (same & (i <= j)).astype(np.float32),
        "rev": (same & (i > j)).astype(np.float32),
        "strict": (same & (i > j)).astype(np.float32),
        "decay": np.where(same & (i >= j), 0.0, NEG),
        "pair": np.where((i < 64) & (j >= 64), NEG, 0.0) + zero,
        "causal": np.where(j <= i, 0.0, NEG) + zero,
        "m1": level(1, i, j),
        "ali0": np.where((i < 64) & (j >= 64), -NEG, abs(i - j)) + zero,
        "ali1": np.where((i >= 64) & (j < 64), -NEG, abs(P + i - j)) + zero,
    }
    for s in (1, 2, 4, 8, 16, 32):
        m[f"t{s}"] = level(s, j, i)
    out = np.zeros((P, NCONST), np.float32)
    for n, name in enumerate(CMAT):
        out[:, n * P:(n + 1) * P] = m[name]
    pos = np.arange(T)
    n = np.arange(32)
    seen = (n[None, :] < 15) & (n[None, :] * 16 + 31 <= pos[:, None])
    inv = 1.0 / (10000.0 ** (np.arange(0, 64, 2, dtype=np.float32) / np.float32(64)))
    ang = pos[:, None].astype(np.float32) * inv[None, :].astype(np.float32)
    for at, table in ((C_CM1, seen.astype(np.float32)), (C_CMB, np.where(seen, 0.0, NEG)),
                      (C_COS, np.cos(ang)), (C_SIN, np.sin(ang))):
        for t in range(2):
            out[:, at + 32 * t:at + 32 * t + 32] = table[t * P:(t + 1) * P]
    for g, w in enumerate((2, 4, 8, 16)):
        out[:, C_CNT + 16 * g:C_CNT + 16 * g + 16] = 1.0 / np.minimum(np.arange(16) + 1, w)
    out[:, C_ONE:C_ONE + P] = 1.0
    return out


class Queues:

    ENGINES = ("pe", "act", "dve", "pool", "sp")

    def __init__(self, sems, starts):
        self.sems = sems
        self.starts = starts
        self.lists = {e: [] for e in self.ENGINES}
        self.count = {n: 0 for n in sems}
        self.seen = {e: {} for e in self.ENGINES}

    def wait(self, eng, *tokens):
        for tok in tokens:
            if tok is None:
                continue
            if isinstance(tok, list) or (isinstance(tok, tuple) and not isinstance(tok[0], str)):
                self.wait(eng, *tok)
                continue
            name, value = tok
            if self.seen[eng].get(name, 0) < value:
                self.seen[eng][name] = value
                self.lists[eng].append((None, None, None, name, value))

    def put(self, eng, fn, args, kw, tokens, sig=True):
        self.wait(eng, tokens)
        if not sig:
            self.lists[eng].append((fn, args, kw, None, 0))
            return None
        self.count[eng] += 1
        self.lists[eng].append((fn, args, kw, eng, 1))
        return (eng, self.count[eng])

    def dma(self, eng, sem, out, src, *tokens):
        self.wait(eng, *tokens)
        self.count[sem] += 16
        self.lists[eng].append((self.starts[eng], (out, src), {}, sem, 16))
        return (sem, self.count[sem])

    def play(self, eng, engine):
        for fn, args, kw, name, value in self.lists[eng]:
            if fn is None:
                engine.wait_ge(self.sems[name], value)
            else:
                ins = fn(*args, **kw)
                if name is not None:
                    ins.then_inc(self.sems[name], value)


def build(nc, a, out):
    with ExitStack() as ctx:
        def sem(name):
            return ctx.enter_context(nc.semaphore(name))

        def sb(name, shape, dt=F):
            return ctx.enter_context(nc.sbuf_tensor(name, shape, dt))

        names = list(Queues.ENGINES) + [f"raw{n}" for n in range(RAW)] + [f"ld{n}" for n in range(24)] + ["st"]
        sems = {n: sem(f"s_{n}") for n in names}

        CO = sb("CO", [P, NCONST])
        VEC = sb("VEC", [P, 336])
        SM = sb("SM", [P, 2 * 144 + 256])
        GB = sb("GB", [P, 2, D])
        X = sb("X", [P, 2, D])
        XTH = sb("XTH", [P, 8, T], R)
        XTL = sb("XTL", [P, 8, T], R)
        RW = [sb(f"RW{n}", [P, KU, UW]) for n in range(RAW)]
        WH = [sb(f"WH{n}", [P, KU, UW], R) for n in range(SPL)]
        WL = [sb(f"WL{n}", [P, KU, UW], R) for n in range(SPL)]
        ST = sb("ST", [P, 64])
        PS = ctx.enter_context(nc.psum_tensor("PS", [P, 8, 512], F))
        room = 229344 - nc.sbuf_base - 96
        room -= room % 64
        base = nc.sbuf_base
        base += -base % 64
        ctx.enter_context(nc.sbuf_tensor("SCR", [P, room // 4], F))
        made = {}

        def at(off, name, shape, dt=F):
            n = 4
            for s in shape[1:]:
                n *= s
            assert off + n <= room, (name, off + n, room)
            if name not in made:
                tile = nc.alloc_sbuf_tensor_at(name, shape, dt, offset=base + off)
                made[name] = tile[tuple(slice(None) for _ in shape)]
            return made[name]

        scratch = nc.dram_tensor("scratch", (4 * 384 + 2 * T * P,), F).ap()

        units = None
        record = []

        def trace(units):
            q = Queues(sems, {"sp": nc.sync.dma_start, "pool": nc.gpsimd.dma_start, "act": nc.scalar.dma_start})
            V, S, G, E = nc.vector, nc.scalar, nc.gpsimd, nc.tensor

            def pe(fn, *args, w=None, sig=False, **kw):
                return q.put("pe", fn, args, kw, w, sig=sig)

            def act(fn, *args, w=None, **kw):
                return q.put("act", fn, args, kw, w)

            def dve(fn, *args, w=None, **kw):
                return q.put("dve", fn, args, kw, w)

            def pool(fn, *args, w=None, **kw):
                return q.put("pool", fn, args, kw, w)

            cm = {n: CO[:, k * P:(k + 1) * P] for k, n in enumerate(CMAT)}
            ident = cm["ident"]
            ones = CO[:, C_ONE:C_ONE + P]

            loaded, split, freed = {}, {}, {}

            def load(n):
                if units is None or n >= len(units) or n in loaded:
                    return
                src = units[n]
                k, w = src.shape[1], src.shape[2]
                loaded[n] = q.dma("sp", f"raw{n % RAW}", RW[n % RAW][:, 0:k, 0:w], src,
                                  split.get(n - RAW))

            def cut(n, by_pool=False):
                if units is None or n >= len(units) or n in split:
                    return
                load(n)
                k, w = units[n].shape[1], units[n].shape[2]
                raw, hi, lo = (t[n % m][:, 0:k, 0:w] for t, m in ((RW, RAW), (WH, SPL), (WL, SPL)))
                th = act(S.activation, hi, raw, ACT.Copy, w=[loaded[n], freed.get(n - SPL)])
                on, fn = (pool, G.tensor_tensor) if by_pool else (dve, V.tensor_tensor)
                tl = on(fn, lo, raw, hi.bitcast(F), ALU.subtract, w=[loaded[n], th, freed.get(n - SPL)])
                split[n] = [th, tl]
                load(n + RAW)

            taken = [0]
            held_ = set()

            class Unit:

                def __init__(self, src):
                    self.n = taken[0]
                    taken[0] += 1
                    held_.add(self.n)
                    self.nk = src.shape[1]
                    if units is None:
                        record.append(src)
                        self.tok = None
                    else:
                        for m in range(RAW):
                            load(self.n + m) if self.n == 0 else None
                        for m in range(self.n, min(self.n + LEAD + 1, min(held_) + SPL)):
                            cut(m)
                        self.tok = split[self.n]
                    self.h = WH[self.n % SPL]
                    self.l = WL[self.n % SPL]

                def free(self, tok):
                    freed[self.n] = tok
                    held_.discard(self.n)

            def wsrc(w, k0, nk, c0, nc_):
                return w[k0 * P:(k0 + nk) * P, c0:c0 + nc_].rearrange("(k p) n -> p k n", p=P)

            free_banks = [(b, None) for b in range(8)]

            def bank():
                return free_banks.pop(0)

            def drop(b, *tok):
                free_banks.append((b, list(tok)))

            def mm3(o, xh, xl, wh, wl, start, stop, *w, sig=False, flip=False):
                a_ = ((xh, wh), (xh, wl), (xl, wh))
                tok = None
                for n, (x_, w_) in enumerate(a_):
                    l_, r_ = (w_, x_) if flip else (x_, w_)
                    tok = pe(E.matmul, o, l_, r_, start=start and n == 0, stop=stop and n == 2,
                             w=list(w) if n == 0 else None, sig=sig and n == 2)
                return tok

            def late():
                if s["late"] is not None:
                    fn, s["late"] = s["late"], None
                    fn()

            def rows(w, nk, c0, parts, xh, xl, xtok, order=None, first_n=2, last_n=2):
                wide = max(off + width for off, width, _ in parts)
                k0s = order or list(range(0, nk, KU))
                nu, g = len(k0s), 0
                if nu <= max(first_n, last_n):
                    sizes = [nu]
                else:
                    mid = nu - first_n - last_n
                    sizes = [first_n] + [2] * (mid // 2) + [1] * (mid % 2) + [last_n]
                for size in sizes:
                    held = [(k0, Unit(wsrc(w, k0, min(KU, nk - k0), c0, wide))) for k0 in k0s[g:g + size]]
                    for t in range(2):
                        for m, (k0, u) in enumerate(held):
                            if m == len(held) - 1 - t * (len(held) - 1):
                                late()
                            for k in range(u.nk):
                                kt = k0 + k
                                ts = slice(t * P, t * P + P)
                                first = g == 0 and m == 0 and k == 0
                                last = g + m == nu - 1 and k == u.nk - 1
                                for n, (off, width, bks) in enumerate(parts):
                                    cs = slice(off, off + width)
                                    tok = mm3(PS[:, bks[t][0], 0:width], xh[:, kt, ts], xl[:, kt, ts],
                                              u.h[:, k, cs], u.l[:, k, cs], first, last,
                                              u.tok, bks[t][1], xtok(kt, t),
                                              sig=n == len(parts) - 1 and (last or (k == u.nk - 1 and t == 1)))
                                if last:
                                    done[t] = tok
                            if t == 1:
                                u.free(tok)
                            yield
                    g += size

            done = {}

            def run(gen):
                for _ in gen:
                    pass

            s = {"x": [None, None], "xh": [None, None], "xt": {}, "late": None}
            for t in range(2):
                s["x"][t] = q.dma("sp", f"ld{15 + t}", X[:, t, :], a["x"][0, t * P:(t + 1) * P, :])
            co_i = q.dma("sp", "ld20", ident, a["consts"][:, 0:P])
            co = [co_i, q.dma("pool", "ld0", CO[:, P:], a["consts"][:, P:])]
            sm = []
            smv = {}
            c = 0

            def small(key, src):
                nonlocal c
                n = src.shape[1]
                smv[key] = SM[:, c:c + n]
                sm.append(q.dma("pool", f"ld{1 + len(sm)}", SM[:, c:c + n], src.to_broadcast([P, n])))
                c += n

            for l in range(2):
                small(("a_log", l), a["a_log"][l:l + 1, :])
                small(("dt_bias", l), a["dt_bias"][l:l + 1, :])
                small(("norm_g", l), a["gdn_norm_g"][l:l + 1, :])
                small(("sinks", l), a["sinks"][l:l + 1, :])
            small("q_norm", a["q_norm_2"])
            small("k_norm", a["k_norm_2"].rearrange("l a b -> l (a b)"))
            sm_tok = sm

            vec = {}
            vn = 0
            vec_tok = []
            STG = [at(90 * 1024 + k * 512, f"stg{k}", [P, P]) for k in range(3)]

            def flat(v):
                return v.rearrange("(r p) -> r p", p=P)

            groups = [[], [], []]
            for l in range(2):
                for key, c0, n in (("qb", 2056, 4), ("kb", 2568, 4), ("qc", 3592, 4), ("kc", 4104, 1),
                                   ("qkv", 0, 12)):
                    groups[0].append(((key, l), flat(a["b_in"][l, c0:c0 + n * P])))
                for k in range(4):
                    groups[1].append((("conv", l, k), flat(a["conv_w"][l, k, :])))
            for k in range(3):
                groups[0].append((("conva", k), flat(a["conv_a_2"][0, k, :])))
            groups[0].append(("pool_scale", flat(a["pool_scale_2"][0, :])))
            groups[0].append(("conf_b", flat(a["conf_dw_b_2"][0, :])))
            groups[0].append(("conf_lg", flat(a["conf_ln_g_2"][0, :])))
            groups[0].append(("conf_lb", flat(a["conf_ln_b_2"][0, :])))
            groups[0].append(("cmp_pos", a["cmp_pos_2"].rearrange("z k (j b) d -> (z k j) (b d)", b=2)))
            for k in range(31):
                groups[2].append((("dw", k), flat(a["conf_dw_2"][0, k, :])))
            staged = []
            for g, rows_ in enumerate(groups):
                r = 0
                tok = None
                if g == 2:
                    tok = q.dma("pool", "ld12", STG[g][0:124, :],
                                a["conf_dw_2"][0].rearrange("k (r p) -> (k r) p", p=P))
                elif g == 1:
                    tok = q.dma("pool", "ld13", STG[g][0:96, :],
                                a["conv_w"].rearrange("l k (r p) -> (l k r) p", p=P))
                for key, src in rows_:
                    n = src.shape[0]
                    if g == 0:
                        tok = q.dma("pool", "ld14", STG[g][r:r + n, :], src)
                    vec[key] = VEC[:, vn + r:vn + r + n]
                    r += n
                staged.append((g, r, vn, tok))
                vn += r

            def turn_vectors():
                for g, r, c0, tok in staged:
                    b, w = bank()
                    t1 = pe(E.transpose, PS[:, b, 0:r], STG[g][0:r, :], ident[0:r, 0:r], w=[tok, co_i, w], sig=True)
                    t2 = dve(V.tensor_copy, VEC[:, c0:c0 + r], PS[:, b, 0:r], w=t1)
                    drop(b, t2)
                    vec_tok.append(t2)

            def to_hl(src, nkt, t, th, tl, kt0, *w):
                toks = {}
                for g0 in range(0, nkt, 4):
                    n = min(4, nkt - g0)
                    b, bw = bank()
                    for k in range(n):
                        tok = pe(E.transpose, PS[:, b, k * P:k * P + P], src(g0 + k), ident,
                                 w=[bw, co_i, w[g0 // 4] if len(w) > 1 else w], sig=(k == n - 1))
                    hi = th[:, kt0 + g0:kt0 + g0 + n, t * P:t * P + P]
                    lo = tl[:, kt0 + g0:kt0 + g0 + n, t * P:t * P + P]
                    pv = PS[:, b, 0:n * P].rearrange("p (k n) -> p k n", k=n)
                    t1 = act(S.activation, hi, pv, ACT.Copy, w=tok)
                    t2 = dve(V.tensor_tensor, lo, pv, hi.bitcast(F), ALU.subtract, w=[tok, t1])
                    drop(b, t1, t2)
                    for k in range(n):
                        toks[kt0 + g0 + k] = [t1, t2]
                return toks

            def x_turn(t):
                tk = to_hl(lambda k: X[:, t, k * P:k * P + P], 8, t, XTH, XTL, 0, *(s["xh"][t] or [s["x"][t]]))
                for k, v in tk.items():
                    s["xt"][k, t] = v
                for n in ((1, 0) if t == 1 else ()):
                    s["x"][n] = pool(G.tensor_scalar, X[:, n, :], X[:, n, :], ALPHA, None, ALU.mult,
                                     w=[s["x"][n], s["xt"][3, n], s["xt"][7, n]])

            def turn(t):
                if s["next"] == "x":
                    fn = lambda: x_turn(t)
                elif s["next"] == "rms":
                    fn = rms_turn(t)
                else:
                    return
                if t == 0:
                    fn()
                else:
                    s["late"] = fn

            xtok = lambda kt, t: s["xt"][kt, t]

            gbt = [None]

            def load_rg(g, off, *w):
                s["rg"] = at(off * 1024, f"RG{off}", [P, D])
                s["rgt"] = q.dma("pool", "ld19", s["rg"], g.to_broadcast([P, D]), s.get("rgr"), *w)

            def load_gb(g, b=None):
                w = gbt[0]
                gbt[0] = [q.dma("pool", "ld17", GB[:, 0, :], g.to_broadcast([P, D]), w)]
                if b is not None:
                    gbt[0].append(q.dma("pool", "ld18", GB[:, 1, :], b.to_broadcast([P, D])))


            def power(dst, src, scale, eps, *w):
                t1 = act(S.activation, dst, src, ACT.Sqrt, bias=epsc[eps], scale=scale, w=w)
                return dve(V.reciprocal, dst, dst, w=t1)

            epst = [dve(V.memset, ST[:, 60:61], 1e-5), dve(V.memset, ST[:, 61:62], 1e-6)]
            epsc = {1e-5: ST[:, 60:61], 1e-6: ST[:, 61:62]}

            def residual(half, t, b, scale, tok):
                xs = X[:, t, half * 512:half * 512 + 512]
                yt = dve(V.scalar_tensor_tensor, out=xs, in0=PS[:, b, :], scalar=scale, in1=xs,
                         op0=ALU.mult, op1=ALU.add, w=[tok, s["x"][t]])
                drop(b, yt)
                return yt

            def stats(half, t, tok):
                return dve(V.bn_stats, ST[:, 12 * t + 6 * half:12 * t + 6 * half + 6],
                           X[:, t, half * 512:half * 512 + 512], w=tok)

            def ln_finish(t, toks):
                o = 24 + 4 * t
                t1 = dve(V.bn_aggr, ST[:, o:o + 2], ST[:, 12 * t:12 * t + 12], w=toks)
                t2 = power(ST[:, o + 2:o + 3], ST[:, o + 1:o + 2], 1.0, 1e-5, t1, epst)
                res = []
                for half in range(2):
                    hs = slice(half * 512, half * 512 + 512)
                    x_ = X[:, t, hs]
                    t3 = dve(V.scalar_tensor_tensor, out=x_, in0=x_, scalar=ST[:, o:o + 1], in1=GB[:, 0, hs],
                             op0=ALU.subtract, op1=ALU.mult, w=[t1, gbt[0]])
                    res.append(dve(V.scalar_tensor_tensor, out=x_, in0=x_, scalar=ST[:, o + 2:o + 3], in1=GB[:, 1, hs],
                                   op0=ALU.mult, op1=ALU.add, w=[t3, t2]))
                s["x"][t] = res[1]
                s["xh"][t] = res
                return res[1]

            def ahead(t):
                if t == 0:
                    for n in range(taken[0], taken[0] + 4):
                        cut(n, n >= taken[0] + 2)

            def out_rows(w, nk, xh, xl, xt, scale, ln, order=None):
                sts = {0: [], 1: []}
                for half in range(2):
                    bks = [bank(), bank()]
                    yield from rows(w, nk, half * 512, [(0, 512, bks)], xh, xl, xt, order, last_n=4 if half else 2)
                    for t in range(2):
                        tok = residual(half, t, bks[t][0], scale, done[t])
                        sts[t].append(stats(half, t, tok) if ln else tok)
                        if half == 1 and ln:
                            ln_finish(t, sts[t])
                            turn(t)
                            ahead(t)
                if ln:
                    gbt[0] = s["xh"][1]
                else:
                    for t in range(2):
                        s["x"][t] = sts[t][1]
                        s["xh"][t] = sts[t]
                        turn(t)
                        ahead(t)

            H_OFF = 0

            def ffn(wg, wu, wd, cg, cu, nf, xt, scale, ln, tag):
                nsl = -(-nf // 512)
                nkt = nf // P
                HTH = at(H_OFF, f"HTH{nkt}", [P, nkt, T], R)
                HTL = at(H_OFF + nkt * T * 4, f"HTL{nkt}", [P, nkt, T], R)
                SG = at(H_OFF + nkt * T * 8, f"SG{nkt}", [P, 2, 512])
                HM = at(H_OFF + nkt * T * 8 + 4096, f"HM{nkt}", [P, 2, 512])
                ht = {}
                pend = []

                def finish(sl, wd_, hm):
                    for t in range(2):
                        n = wd_ // P
                        tk = to_hl(lambda k: HM[:, t, k * P:k * P + P], n, t, HTH, HTL, 4 * sl, hm[t])
                        for k, v in tk.items():
                            ht[k, t] = v
                        hm[t] = v

                last = [None, None]
                for sl in range(nsl):
                    wd_ = min(512, nf - 512 * sl)
                    g = [bank(), bank()]
                    run(rows(wg, 8, cg + 512 * sl, [(0, wd_, g)], XTH, XTL, xt, first_n=2 if sl else 4))
                    gd = dict(done)
                    if pend:
                        psl, pw, hm = pend.pop()
                        finish(psl, pw, hm)
                        last = hm
                    u = [bank(), bank()]
                    run(rows(wu, 8, cu + 512 * sl, [(0, wd_, u)], XTH, XTL, xt))
                    hm = [None, None]
                    for t in range(2):
                        t1 = act(S.activation, SG[:, t, 0:wd_], PS[:, g[t][0], 0:wd_], ACT.Silu, w=[gd[t], last[t]])
                        drop(g[t][0], t1)
                        t2 = dve(V.tensor_tensor, HM[:, t, 0:wd_], PS[:, u[t][0], 0:wd_], SG[:, t, 0:wd_], ALU.mult,
                                 w=[t1, done[t], last[t]])
                        drop(u[t][0], t2)
                        hm[t] = t2
                    pend.append((sl, wd_, hm))
                    if staged and sl == 3:
                        turn_vectors()
                        staged.clear()
                y = out_rows(wd, nkt, HTH, HTL, lambda kt, t: ht[kt, t], scale, ln)
                next(y)
                psl, pw, hm = pend.pop()
                finish(psl, pw, hm)
                run(y)


            def evac(kind, dst, src, *w):
                if kind == "act":
                    return act(S.activation, dst, src, ACT.Copy, w=w)
                return dve(V.tensor_copy, dst, src, w=w)

            def cols(w, c0, nt, bks, xt, width=None):
                late()
                for k0 in range(0, 8, KU):
                    u = Unit(wsrc(w, k0, KU, c0, nt * P))
                    for k in range(KU):
                        kt = k0 + k
                        for j in range(nt):
                            cs = slice(j * P, j * P + P)
                            tok = mm3(PS[:, bks[j][0], 0:T], XTH[:, kt, :], XTL[:, kt, :],
                                      u.h[:, k, cs], u.l[:, k, cs], kt == 0, kt == 7,
                                      u.tok, bks[j][1], xt(kt, 0), xt(kt, 1),
                                      sig=(kt == 7) or (k == KU - 1 and j == nt - 1), flip=True)
                            if kt == 7:
                                done["c", j] = tok
                    u.free(tok)
                    yield

            def bcast(ap, *shape):
                return ap.to_broadcast(list(shape))

            def over(ap, n):
                return ap.unsqueeze(2).to_broadcast([ap.shape[0], ap.shape[1], n])

            def heads(ap, n):
                return ap.unsqueeze(1).to_broadcast([ap.shape[0], n, ap.shape[1]])

            def softmax_start(sv, nh, pv, k, scale, w, sink=None):
                o = 24 * (k % 6)
                m, n_, su, rc, es = (SX[:, o + 4 * q_:o + 4 * q_ + nh] for q_ in range(5))
                t1 = dve(V.tensor_reduce, m, sv, AX, ALU.max, w=w)
                if sink is not None:
                    t1 = dve(V.scalar_tensor_tensor, out=m, in0=m, scalar=scale, in1=sink,
                             op0=ALU.mult, op1=ALU.max, w=[t1, sm_tok])
                    t2 = dve(V.tensor_scalar, n_, m, -1.0, None, ALU.mult, w=t1)
                    t3 = dve(V.tensor_tensor, es, sink, m, ALU.subtract, w=t1)
                    t3 = act(S.activation, es, es, ACT.Exp, w=t3)
                else:
                    t2 = dve(V.tensor_scalar, n_, m, -scale, None, ALU.mult, w=t1)
                    t3 = None
                for h in range(nh):
                    t4 = act(S.activation, pv[:, h, :], sv[:, h, :], ACT.Exp, bias=n_[:, h:h + 1], scale=scale,
                             accum_out=su[:, h:h + 1], w=[t2, w])
                return su, rc, es, t3, t4

            def softmax_end(state_):
                su, rc, es, t3, t4 = state_
                if t3 is not None:
                    t5 = dve(V.tensor_tensor, su, su, es, ALU.add, w=[t4, t3])
                    t5 = dve(V.reciprocal, rc, su, w=t5)
                else:
                    t5 = dve(V.reciprocal, rc, su, w=t4)
                return rc, t4, t5

            def softmax_rows(*args):
                return softmax_end(softmax_start(*args))

            def block_attention(l, q_ap, k_ap, v_ap, qk_tok, v_tok, group, k, toh, tol, res, kind, extra):
                t, hs = group
                nh, nk = len(hs), (t + 1) * P
                pv = PP[k % 2][:, 0:nh * nk].rearrange("p (h n) -> p h n", h=nh)
                b, bw = bank()
                sv = PS[:, b, 0:nh * nk].rearrange("p (h n) -> p h n", h=nh)
                for n, h in enumerate(hs):
                    tok = pe(E.matmul, sv[:, n, :], q_ap(h, t), k_ap(h, nk), start=True, stop=kind == "c",
                             w=[bw, qk_tok, co], sig=True, skip_group_check=True)
                    if kind == "b":
                        for kt in range(t + 1):
                            tok = pe(E.matmul, sv[:, n, kt * P:kt * P + P],
                                     YH[:, h, (t - kt) * P:(t - kt) * P + P], cm["flip"],
                                     start=False, stop=kt < t, w=[extra], sig=True, skip_group_check=True)
                        tok = pe(E.matmul, sv[:, n, t * P:t * P + P], ident, cm["pair"],
                                 start=False, stop=True, sig=True, skip_group_check=True)
                if kind == "c":
                    lv = SC[k % 2][:, 0:nh * nk].rearrange("p (h n) -> p h n", h=nh)
                    a0 = CMAT.index("ali1") * P
                    al = CO[:, a0:a0 + 2 * P] if t else CO[:, a0 + P:a0 + 2 * P]
                    for n, h in enumerate(hs):
                        tok2 = dve(V.scalar_tensor_tensor, out=lv[:, n, :], in0=al, scalar=-8.0 * 2.0 ** -(h + 1),
                                   in1=sv[:, n, :], op0=ALU.mult, op1=ALU.add, w=[tok, co])
                    drop(b, tok2)
                    rc, te, tr = softmax_rows(lv, nh, pv, k % 5, 0.125, tok2, smv["sinks", l][:, hs[0]:hs[0] + 2 * nh - 1:2])
                else:
                    rc, te, tr = softmax_rows(sv, nh, pv, k % 5, 1.0, tok)
                    drop(b, te)
                tn = dve(V.tensor_tensor, pv, pv, over(rc, nk), ALU.mult, w=tr)
                yield
                b, bw = bank()
                tv = PS[:, b, :].rearrange("p (c n) -> p c n", n=P)
                idx = {}
                for n, h in enumerate(hs):
                    for kt in range(t + 1):
                        i = len(idx)
                        idx[h, kt] = i
                        tok = pe(E.transpose, tv[:, i, :], pv[:, n, kt * P:kt * P + P], ident,
                                 w=[tn, bw], sig=True)
                pt = PT[k % 2]
                tp = act(S.activation, pt[:, 0:len(idx) * P], PS[:, b, 0:len(idx) * P], ACT.Copy, w=tok)
                drop(b, tp)
                yield
                b, bw = bank()
                if kind == "b":
                    for n, h in enumerate(hs):
                        for kt in range(t + 1):
                            i = idx[h, kt]
                            tok = pe(E.matmul, PS[:, b, n * P:n * P + P], v_ap(h, kt), pt[:, i * P:i * P + P],
                                     start=kt == 0, stop=kt == t, w=[tp, bw, v_tok], sig=True)
                    nt, t0, r, m = nh, hs[0], 0, P
                else:
                    r, m = 64 * (hs[0] % 2), 64
                    for n, h in enumerate(hs):
                        for kt in range(t + 1):
                            i = idx[h, kt]
                            tok = pe(E.matmul, PS[r:r + 64, b, n * P:n * P + P], v_ap(h, kt),
                                     pt[:, i * P:i * P + P], start=kt == 0, stop=kt == t,
                                     w=[tp, bw, v_tok], sig=True)
                    nt, t0 = nh, hs[0] // 2
                res.append(split_out(b, r, m, nt, t0, t, toh, tol, tok))
                yield

            def split_out(b, r, m, nt, t0, t, toh, tol, tok):
                src = PS[r:r + m, b, 0:nt * P].rearrange("p (k n) -> p k n", k=nt)
                hi, lo = (o[r:r + m, t0:t0 + nt, t * P:t * P + P] for o in (toh, tol))
                t1 = act(S.activation, hi, src, ACT.Copy, w=tok)
                t2 = dve(V.tensor_tensor, lo, src, hi.bitcast(F), ALU.subtract, w=[t1, tok])
                drop(b, t1, t2)
                return [t1, t2]

            def pipeline(gens, fill, each):
                live = []
                gens = list(gens)
                while gens or live:
                    new = [gens.pop(0)] if gens else []
                    keep = []
                    for n, g in enumerate(new + live):
                        if n == len(new + live) - 1:
                            fill(each)
                        try:
                            next(g)
                            keep.append(g)
                        except StopIteration:
                            pass
                    live = [g for g in keep if g not in new] + new

            def load_gb_after(w1, w2, g, b):
                gbt[0] = [w1, w2]
                load_gb(g, b)

            SX = at(int(93.5 * 1024), "SX", [P, 512])

            def mixer1(l):
                K = 1024
                QK = at(0, "QK", [P, 8, T])
                VB = at(8 * K, "VB", [P, 2, 512])
                QC = at(12 * K, "QC", [P, 4, T])
                KC = at(16 * K, "KC", [P, 2, T])
                VC = at(18 * K, "VC", [P, 2, P])
                nonlocal YH, PP, PT, SC
                YH = at(19 * K, "YH", [P, 4, T])
                PP = [at((23 + 2 * n) * K, f"PP{n}", [P, 512]) for n in range(2)]
                PT = [at((27 + 2 * n) * K, f"PT{n}", [P, 512]) for n in range(2)]
                SC = [at((31 + 2 * n) * K, f"SC{n}", [P, 512]) for n in range(2)]
                RBX = at(35 * K, "RBX", [4, 384])
                QP = at(37 * K, "QP", [P, 12, 259])
                MG = at(37 * K, "MG", [P, 2, D])
                GT = [at((45 + 2 * n) * K, f"GT{n}", [P, 512]) for n in range(2)]
                QX = at(49 * K + 512, "QX", [P, 12, T])
                OH = {i: [at(int((61.5 + 8 * n + 4 * m) * K), f"O{i}{m}", [P, 4, T], R)
                          for m in range(2)] for n, i in enumerate("abc")}
                Z = at(int(85.5 * K), "Z", [P, 2, 512])
                SS = at(int(89.5 * K), "SS", [P, 512])
                VN = at(int(91.5 * K), "VN", [P, 512])

                r1 = q.dma("pool", "ld1", RBX[:, 64:256], a["rel_bias"][l])
                r2 = pool(G.tensor_copy, RBX[:, 0:64], bcast(RBX[:, 64:65], 4, 64), w=r1)
                r3 = pool(G.tensor_copy, RBX[:, 256:384], bcast(RBX[:, 255:256], 4, 128), w=r1)
                r4 = q.dma("pool", "ld2", scratch[0:1536].rearrange("(h n) -> h n", h=4), RBX[:, :], r2, r3)
                yh = q.dma("pool", "ld3", YH[:, :, :], bass.AP(scratch.tensor, 0, [[1, P], [384, 4], [1, T]]), r4)
                b_vb = q.dma("pool", "ld4", GB[:, 1, 0:512], bcast(a["b_in"][l:l + 1, 3080:3592], P, 512), gbt[0])
                b_vc = q.dma("pool", "ld5", GB[:, 1, 512:640], bcast(a["b_in"][l:l + 1, 4232:4360], P, 128), gbt[0])
                b_za = q.dma("pool", "ld6", GB[:, 0, 0:520], bcast(a["b_in"][l:l + 1, 1536:2056], P, 520), gbt[0])
                pz = pool(G.memset, QP[:, :, 0:3], 0.0)

                w_in = a["w_in"][l]
                bks = [bank(), bank()]
                run(rows(w_in, 8, 3080, [(0, 512, bks)], XTH, XTL, xtok, first_n=4))
                vb = []
                for t in range(2):
                    vb.append(dve(V.tensor_tensor, VB[:, t, :], PS[:, bks[t][0], :], GB[:, 1, 0:512], ALU.add,
                                  w=[done[t], b_vb]))
                    drop(bks[t][0], vb[-1])
                qk = []
                for part, c0 in enumerate((2056, 2568)):
                    bks = [bank() for _ in range(4)]
                    run(cols(w_in, c0, 4, bks, xtok))
                    key = ("qb", "kb")[part]
                    for j in range(4):
                        qk.append(dve(V.tensor_scalar, QK[:, 4 * part + j, :], PS[:, bks[j][0], 0:T],
                                      vec[key, l][:, j:j + 1], 128.0 ** -0.5 if part == 0 else 1.0,
                                      ALU.add, ALU.mult, w=[done["c", j], vec_tok]))
                        drop(bks[j][0], qk[-1])
                bks = [bank() for _ in range(4)]
                run(cols(w_in, 3592, 4, bks, xtok))
                qc = []
                for j in range(4):
                    qc.append(dve(V.tensor_scalar, QC[:, j, :], PS[:, bks[j][0], 0:T], vec["qc", l][:, j:j + 1],
                                  None, ALU.add, w=[done["c", j], vec_tok]))
                    drop(bks[j][0], qc[-1])
                kb_, v0, v1 = bank(), bank(), bank()
                for k0 in range(0, 8, KU):
                    u = Unit(wsrc(w_in, k0, KU, 4104, 256))
                    for k in range(KU):
                        kt = k0 + k
                        st, sp = kt == 0, kt == 7
                        tk = mm3(PS[:, kb_[0], 0:T], XTH[:, kt, :], XTL[:, kt, :], u.h[:, k, 0:P], u.l[:, k, 0:P],
                                 st, sp, u.tok, kb_[1], xtok(kt, 0), xtok(kt, 1), sig=True, flip=True)
                        for t, v_ in ((0, v0), (1, v1)):
                            ts = slice(t * P, t * P + P)
                            tv_ = mm3(PS[:, v_[0], 0:P], XTH[:, kt, ts], XTL[:, kt, ts],
                                      u.h[:, k, P:2 * P], u.l[:, k, P:2 * P], st, sp, v_[1], sig=True)
                    u.free(tv_)
                k1_ = dve(V.tensor_scalar, KC[:, 0, :], PS[:, kb_[0], 0:T], vec["kc", l], None, ALU.add,
                          w=[tk, vec_tok])
                drop(kb_[0], k1_)
                vc = []
                for t, v_ in ((0, v0), (1, v1)):
                    vc.append(dve(V.tensor_tensor, VC[:, t, :], PS[:, v_[0], 0:P], GB[:, 1, 512:640], ALU.add,
                                  w=[tv_, b_vc]))
                    drop(v_[0], vc[-1])
                b_, bw = bank()
                pe(E.matmul, PS[0:64, b_, 0:T], ident[:, 64:128], KC[:, 0, :], start=True, stop=True, w=[k1_, bw, co])
                tk = pe(E.matmul, PS[64:128, b_, 0:T], ident[:, 0:64], KC[:, 0, :], start=True, stop=True, sig=True)
                k2_ = dve(V.tensor_copy, KC[:, 1, :], PS[:, b_, 0:T], w=tk)
                drop(b_, k2_)

                ready = {"q": []}
                BA = SX[:, 256:272].rearrange("p (t c) -> p t c", t=2)

                TL = ["KBE", "VBT", "KDC", "DD", "LL", "LT", "QKD", "AT", "BB", "BT", "PW", "MS0", "MS1",
                      "EGR", "QDT", "WT", "UU", "GX"]
                W_ = {n: at(2048 * k, f"g{n}", [P, 4, P]) for k, n in enumerate(TL)}
                flat_ = {n: W_[n][:, :, :].rearrange("p h n -> p (h n)") for n in TL}
                sc = {}
                for k, n in enumerate(("BE", "T1", "T2", "T3", "GG", "GC", "RE", "EG", "ER", "Z1", "Z2")):
                    sc[n] = SX[:, 272 + 8 * k:280 + 8 * k]
                s2 = {n: v.rearrange("p (t h) -> p t h", t=2) for n, v in sc.items()}
                EA = SX[:, 368:372]

                def decays():
                    zt = [ready["z", 0], ready["z", 1]]
                    tb = act(S.activation, s2["BE"], BA[:, :, 0:4], ACT.Exp, scale=-1.0, w=zt)
                    te = act(S.activation, EA, smv["a_log", l], ACT.Exp, w=sm_tok)
                    tb = dve(V.tensor_scalar, sc["BE"], sc["BE"], 1.0, None, ALU.add, w=tb)
                    tb = dve(V.reciprocal, sc["BE"], sc["BE"], w=tb)
                    t1 = dve(V.tensor_tensor, s2["T1"], BA[:, :, 4:8], heads(smv["dt_bias", l], 2), ALU.add, w=[zt, sm_tok])
                    t1 = dve(V.scalar_tensor_tensor, out=sc["T2"], in0=sc["T1"], scalar=-1.0, in1=sc["T1"],
                             op0=ALU.mult, op1=ALU.max, w=t1)
                    t2 = act(S.activation, sc["T2"], sc["T2"], ACT.Exp, scale=-1.0, w=t1)
                    t2 = dve(V.tensor_scalar, sc["T3"], sc["T2"], 2.0, None, ALU.add, w=t2)
                    t2 = dve(V.reciprocal, sc["T3"], sc["T3"], w=t2)
                    t2 = dve(V.tensor_tensor, sc["Z1"], sc["T2"], sc["T3"], ALU.mult, w=t2)
                    t2 = dve(V.tensor_tensor, sc["Z2"], sc["Z1"], sc["Z1"], ALU.mult, w=t2)
                    t3 = dve(V.tensor_scalar, sc["T2"], sc["Z2"], 1.0 / 15, None, ALU.mult, w=t2)
                    for c in (13, 11, 9, 7, 5, 3):
                        t3 = dve(V.scalar_tensor_tensor, out=sc["T2"], in0=sc["T2"], scalar=1.0 / c, in1=sc["Z2"],
                                 op0=ALU.add, op1=ALU.mult, w=t3)
                    t3 = dve(V.scalar_tensor_tensor, out=sc["T2"], in0=sc["T2"], scalar=1.0, in1=sc["Z1"],
                             op0=ALU.add, op1=ALU.mult, w=t3)
                    t4 = dve(V.tensor_scalar, sc["T1"], sc["T1"], 0.0, None, ALU.max, w=t3)
                    t4 = dve(V.scalar_tensor_tensor, out=sc["T1"], in0=sc["T2"], scalar=2.0, in1=sc["T1"],
                             op0=ALU.mult, op1=ALU.add, w=t4)
                    tg_ = dve(V.scalar_tensor_tensor, out=s2["GG"], in0=s2["T1"], scalar=-1.0, in1=heads(EA, 2),
                              op0=ALU.mult, op1=ALU.mult, w=[t4, te])
                    ready["g"], ready["beta"] = tg_, tb

                def z_gate():
                    for t in range(2):
                        z1 = act(S.activation, Z[:, t, :], Z[:, t, :], ACT.Silu, w=ready["z", t])
                        ready["z", t] = pool(G.tensor_tensor, Z[:, t, :].rearrange("p (h n) -> p h n", h=4),
                                             Z[:, t, :].rearrange("p (h n) -> p h n", h=4),
                                             heads(smv["norm_g", l], 4), ALU.mult, w=[z1, sm_tok])

                qx = []

                def conv_silu(j):
                    cw = [vec["conv", l, k][:, j:j + 1] for k in range(4)]
                    tc = dve(V.tensor_scalar, QX[:, j, :], QP[:, j, 3:259], cw[3], None, ALU.mult,
                             w=[ready["q", j], pz, vec_tok])
                    for k in range(3):
                        tc = dve(V.scalar_tensor_tensor, out=QX[:, j, :], in0=QP[:, j, k:k + T], scalar=cw[k],
                                 in1=QX[:, j, :], op0=ALU.mult, op1=ALU.add, w=tc)
                    if j % 4 == 3:
                        qx.append(act(S.activation, QX[:, j - 3:j + 1, :], QX[:, j - 3:j + 1, :], ACT.Silu, w=tc))

                NR = SX[:, 376:392]
                NT = SX[0:16, 128:256]
                nb = {}
                qn = []

                def square(pr):
                    src = QX[:, 2 * pr:2 * pr + 2, :].rearrange("p a b -> p (a b)")
                    nb["sq", pr] = act(S.activation, (SS, VN)[pr % 2], src, ACT.Square,
                                       w=[qx[pr // 2], nb.get(("mm", pr - 2))])

                def sums(pr):
                    if pr == 0:
                        nb["b"] = bank()
                    b, bw = nb["b"]
                    for jj in range(2):
                        for t in range(2):
                            c_ = 8 * t + 2 * pr + jj
                            o_ = (2 * jj + t) * P
                            nb["mm", pr] = pe(E.matmul, PS[:, b, c_:c_ + 1], (SS, VN)[pr % 2][:, o_:o_ + P], ones[:, 0:1],
                                              start=True, stop=True, w=[nb["sq", pr], bw, co], sig=True)

                def roots():
                    b, _ = nb["b"]
                    t1 = act(S.activation, NR, PS[:, b, 0:16], ACT.Sqrt, bias=epsc[1e-6], w=[nb["mm", 3], epst])
                    drop(b, t1)
                    nb["rn"] = dve(V.reciprocal, NR, NR, w=t1)

                def turned():
                    b, bw = bank()
                    t1 = pe(E.transpose, PS[0:16, b, 0:P], NR, ident, w=[nb["rn"], bw], sig=True)
                    nb["rt"] = act(S.activation, NT, PS[0:16, b, 0:P], ACT.Copy, w=t1)
                    drop(b, nb["rt"])

                def norm(pr):
                    src = QX[:, 2 * pr:2 * pr + 2, :].rearrange("p a b -> p (a b)")
                    b, bw = bank()
                    for jj in range(2):
                        for t in range(2):
                            c_ = 8 * t + 2 * pr + jj
                            o_ = (2 * jj + t) * P
                            t1 = pe(E.matmul, PS[:, b, o_:o_ + P], ident[0:16, c_:c_ + 1].to_broadcast([16, P]), NT,
                                    start=True, stop=True, w=[nb["rt"], bw], sig=True)
                    t1 = dve(V.scalar_tensor_tensor, out=src, in0=src, scalar=128.0 ** -0.5 if pr < 2 else 1.0,
                             in1=PS[:, b, :], op0=ALU.mult, op1=ALU.mult, w=[t1, nb["sq", pr]])
                    drop(b, t1)
                    qn.append(t1)

                def norms():
                    return [lambda: square(0), lambda: (sums(0), square(1)), lambda: (sums(1), square(2)),
                            lambda: (sums(2), square(3)), lambda: (sums(3), roots()), turned] + [
                                lambda pr=pr: norm(pr) for pr in range(4)]

                todo = []
                z_in = []

                def inputs_a():
                    for part in (0, None, 1, 2):
                        if part is None:
                            bks, ob = [bank(), bank()], [bank(), bank()]
                            gen = rows(w_in, 8, 1536, [(0, 8, ob), (8, 512, bks)], XTH, XTL, xtok)
                            for n, _ in enumerate(gen):
                                if n % 2:
                                    yield
                            for t in range(2):
                                t1 = dve(V.tensor_tensor, Z[:, t, :], PS[:, bks[t][0], :], GB[:, 0, 8:520], ALU.add,
                                         w=[done[t], b_za])
                                drop(bks[t][0], t1)
                                t2 = dve(V.tensor_tensor, BA[:, t, :], PS[:, ob[t][0], 0:8], GB[:, 0, 0:8], ALU.add,
                                         w=[done[t], b_za])
                                drop(ob[t][0], t2)
                                ready["z", t] = [t1, t2]
                                z_in.append([t1, t2])
                            todo.append(decays)
                            todo.append(z_gate)
                            continue
                        bks = [bank() for _ in range(4)]
                        yield from cols(w_in, 512 * part, 4, bks, xtok)
                        for j in range(4 * part, 4 * part + 4):
                            ready["q", j] = act(S.activation, QP[:, j, 3:259], PS[:, bks[j % 4][0], 0:T], ACT.Identity,
                                                bias=vec["qkv", l][:, j:j + 1], w=[done["c", j % 4], vec_tok])
                            drop(bks[j % 4][0], ready["q", j])
                            if part == 2:
                                todo.insert(2 * (j - 8), lambda j=j: conv_silu(j))
                            else:
                                todo.append(lambda j=j: conv_silu(j))
                        if part == 1:
                            todo.extend(norms())

                gen = inputs_a()
                state = {"gen": gen, "spent": False}

                def fill(n):
                    for _ in range(n):
                        if not state["spent"]:
                            try:
                                next(state["gen"])
                            except StopIteration:
                                state["spent"] = True
                        if todo:
                            todo.pop(0)()

                res = {"b": [], "c": []}
                gb_ = [(0, [0, 1, 2, 3]), (1, [0, 1]), (1, [2, 3])]
                gc_ = [(0, [0, 2, 4, 6]), (0, [1, 3, 5, 7]), (1, [0, 2]), (1, [4, 6]), (1, [1, 3]), (1, [5, 7])]
                gens = []
                for n, g in enumerate(gb_):
                    gens.append(block_attention(
                        l, lambda h, t: QK[:, h, t * P:t * P + P], lambda h, nk: QK[:, 4 + h, 0:nk],
                        lambda h, kt: VB[:, kt, h * P:h * P + P], qk, vb, g, n, *OH["b"], res["b"], "b", yh))

                def kc_of(h, nk):
                    r = 64 * (h % 2)
                    return KC[r:r + 64, 0 if h // 4 == h % 2 else 1, 0:nk]

                for n, g in enumerate(gc_):
                    gens.append(block_attention(
                        l, lambda h, t: QC[64 * (h % 2):64 * (h % 2) + 64, h // 2, t * P:t * P + P], kc_of,
                        lambda h, kt: VC[:, kt, (h // 4) * 64:(h // 4) * 64 + 64],
                        qc + [k1_, k2_], vc, g, n + 3, *OH["c"], res["c"], "c", None))
                pipeline(gens, fill, 1)
                while not state["spent"]:
                    fill(1)
                att_done = [res["b"], res["c"]]

                bg = {"a": (0, 1), "b": (1, 1), "c": (2, 0)}
                bgt = {}
                first = [True]
                gtw = [None, None]

                def gate_bias(i, w):
                    n, slot = bg[i]
                    bgt[i] = q.dma("pool", "ld4" if slot else "ld6", GB[:, slot, :],
                                   bcast(a["b_gate"][l:l + 1, n * D:(n + 1) * D], P, D), w)

                def branch(i, th, tl, xt):
                    n, slot = bg[i]
                    wb = a[f"w_br_{i}"][l]
                    for half in range(2):
                        hs = slice(half * 512, half * 512 + 512)
                        if i == "a":
                            y = [bank(), bank()]
                            yield from rows(wb, 4, half * 512, [(0, 512, y)], th, tl, xt)
                            for t in range(2):
                                ga, m = GTA[:, t, hs], MG[:, t, hs]
                                t1 = dve(V.tensor_tensor, ga, PS[:, y[t][0], :], ga, ALU.mult,
                                         w=[done[t], gta[t, half]])
                                drop(y[t][0], t1)
                                mgt[t, half] = dve(V.tensor_tensor, m, m, ga, ALU.add, w=[t1, mgt[t, half]])
                            continue
                        g = [bank(), bank()]
                        yield from rows(a["w_gate"][l], 8, n * D + half * 512, [(0, 512, g)], XTH, XTL, xtok)
                        tg = []
                        for t in range(2):
                            t1 = dve(V.tensor_tensor, GT[t], PS[:, g[t][0], :], GB[:, slot, hs], ALU.add,
                                     w=[done[t], bgt[i], gtw[t]])
                            drop(g[t][0], t1)
                            tg.append(act(S.activation, GT[t], GT[t], ACT.Sigmoid, w=t1))
                        y = [bank(), bank()]
                        yield from rows(wb, 4, half * 512, [(0, 512, y)], th, tl, xt)
                        for t in range(2):
                            m = MG[:, t, hs]
                            t1 = dve(V.tensor_tensor, m if i == "b" else GT[t], PS[:, y[t][0], :], GT[t], ALU.mult,
                                     w=[done[t], tg[t]])
                            drop(y[t][0], t1)
                            if i != "b":
                                t1 = pool(G.tensor_tensor, m, m, GT[t], ALU.add, w=t1)
                            gtw[t] = t1
                            mgt[t, half] = t1
                    if i != "a":
                        bgt[i] = t1

                GTA = at(int(69.5 * K), "GTA", [P, 2, D])
                gta = {}

                def gate_a():
                    n, slot = bg["a"]
                    for half in range(2):
                        hs = slice(half * 512, half * 512 + 512)
                        g = [bank(), bank()]
                        yield from rows(a["w_gate"][l], 8, n * D + half * 512, [(0, 512, g)], XTH, XTL, xtok)
                        for t in range(2):
                            t1 = dve(V.tensor_tensor, GTA[:, t, hs], PS[:, g[t][0], :], GB[:, slot, hs], ALU.add,
                                     w=[done[t], bgt["a"], mgt[t, 1]])
                            drop(g[t][0], t1)
                            gta[t, half] = act(S.activation, GTA[:, t, hs], GTA[:, t, hs], ACT.Sigmoid, w=t1)
                    bgt["a"] = t1

                mgt = {}
                gate_bias("b", [vb, vc])
                gate_bias("c", z_in)

                def others():
                    yield from branch("b", *OH["b"], lambda kt, t: res["b"])
                    gate_bias("a", bgt["b"])
                    yield from branch("c", *OH["c"], lambda kt, t: res["c"])
                    yield from gate_a()

                state["gen"], state["spent"] = others(), False
                tg_, tb = ready["g"], ready["beta"]

                def spread(t, w):
                    return pool(G.tensor_copy, W_["GX"], over(sc["GG"][:, 4 * t:4 * t + 4], P), w=[tg_, w])

                def gate_sums(t):
                    h4 = slice(4 * t, 4 * t + 4)
                    b, bw = bank()
                    t1 = pe(E.matmul, PS[:, b, 0:4], cm["tri"], sc["GG"][:, h4], start=True, stop=True,
                            w=[tg_, bw, co], sig=True)
                    t2 = pe(E.matmul, PS[:, b, 4:8], cm["rev"], sc["GG"][:, h4], start=True, stop=True, sig=True)
                    t3 = dve(V.tensor_copy, sc["GC"][:, h4], PS[:, b, 0:4], w=t2)
                    t4 = act(S.activation, sc["EG"][:, h4], PS[:, b, 0:4], ACT.Exp, w=[t2, t3])
                    t5 = act(S.activation, sc["ER"][:, h4], PS[:, b, 4:8], ACT.Exp, w=t2)
                    drop(b, t3, t4, t5)
                    t6 = dve(V.tensor_tensor, sc["RE"][:, h4], sc["BE"][:, h4], sc["EG"][:, h4], ALU.mult, w=[t4, tb])
                    return [None, t3, t4, t5, t6]

                fill(1)
                gates = [gate_sums(t) for t in range(2)]
                gates[0][0] = spread(0, att_done)
                while todo:
                    fill(1)
                oa = []
                sst = None
                for t in range(2):
                    ts = slice(t * P, t * P + P)
                    h4 = slice(4 * t, 4 * t + 4)
                    tx, t3, t4, t5, t6 = gates[t]
                    b, bw = bank()
                    pv = PS[:, b, :].rearrange("p (h n) -> p h n", h=4)
                    for h in range(4):
                        t1 = pe(E.matmul, pv[:, h, :], W_["GX"][:, h, :], cm["tri"], start=True, stop=True,
                                w=[tx, bw], sig=True)
                    if t == 0:
                        gates[1][0] = spread(1, t1)
                    t7 = act(S.activation, W_["EGR"], pv, ACT.Exp, w=t1)
                    t8 = dve(V.scalar_tensor_tensor, out=W_["DD"], in0=pv, scalar=-1.0, in1=heads(cm["decay"], 4),
                             op0=ALU.mult, op1=ALU.add, w=[t1, qn, t7])
                    drop(b, t7, t8)
                    for h in range(4):
                        td = act(S.activation, W_["DD"][:, h, :], W_["DD"][:, h, :], ACT.Exp,
                                 bias=sc["GC"][:, 4 * t + h:4 * t + h + 1], w=[t8, t3])
                    b1, bw1 = bank()
                    b2, bw2 = bank()
                    kv = PS[:, b1, :].rearrange("p (h n) -> p h n", h=4)
                    vv = PS[:, b2, :].rearrange("p (h n) -> p h n", h=4)
                    for h in range(4):
                        t1 = pe(E.transpose, kv[:, h, :], QX[:, 4 + h, ts], ident, w=[qn, bw1], sig=True)
                    for h in range(4):
                        t2 = pe(E.transpose, vv[:, h, :], QX[:, 8 + h, ts], ident, w=[qx, bw2], sig=True)
                    fill(1)
                    t3_ = dve(V.tensor_tensor, W_["KBE"], kv, over(sc["RE"][:, h4], P), ALU.mult, w=[t1, t6])
                    t4_ = dve(V.tensor_tensor, W_["KDC"], kv, over(sc["ER"][:, h4], P), ALU.mult, w=[t1, t5])
                    t5_ = dve(V.tensor_tensor, W_["VBT"], vv, over(sc["BE"][:, h4], P), ALU.mult, w=[t2, tb])
                    drop(b1, t3_, t4_)
                    drop(b2, t5_)
                    t6_ = pool(G.tensor_tensor, W_["QDT"], QX[:, 0:4, ts], W_["EGR"], ALU.mult, w=[qn, t7])
                    b1, bw1 = bank()
                    b2, bw2 = bank()
                    kk = PS[:, b1, :].rearrange("p (h n) -> p h n", h=4)
                    qk_ = PS[:, b2, :].rearrange("p (h n) -> p h n", h=4)
                    for h in range(4):
                        t1 = pe(E.matmul, kk[:, h, :], QX[:, 4 + h, ts], QX[:, 4 + h, ts], start=True, stop=True,
                                w=bw1, sig=True)
                    for h in range(4):
                        t2 = pe(E.matmul, qk_[:, h, :], QX[:, h, ts], QX[:, 4 + h, ts], start=True, stop=True,
                                w=bw2, sig=True)
                    fill(2)
                    t3 = dve(V.tensor_tensor, W_["LL"], kk, W_["DD"], ALU.mult, w=[t1, td])
                    drop(b1, t3)
                    for h in range(4):
                        t4 = dve(V.scalar_tensor_tensor, out=W_["LL"][:, h, :], in0=W_["LL"][:, h, :],
                                 scalar=sc["BE"][:, 4 * t + h:4 * t + h + 1], in1=cm["strict"],
                                 op0=ALU.mult, op1=ALU.mult, w=t3)
                    t5 = dve(V.tensor_tensor, W_["QKD"], qk_, W_["DD"], ALU.mult, w=[t2, td])
                    drop(b2, t5)
                    b1, bw1 = bank()
                    b2, bw2 = bank()
                    lt = PS[:, b1, :].rearrange("p (h n) -> p h n", h=4)
                    av = PS[:, b2, :].rearrange("p (h n) -> p h n", h=4)
                    for h in range(4):
                        t1 = pe(E.transpose, lt[:, h, :], W_["LL"][:, h, :], ident, w=[t4, bw1], sig=True)
                    for h in range(4):
                        t2 = pe(E.transpose, av[:, h, :], W_["QKD"][:, h, :], ident, w=[t5, bw2], sig=True)
                    fill(2)
                    tl_ = act(S.activation, W_["LT"], lt, ACT.Copy, w=t1)
                    drop(b1, tl_)
                    ta = act(S.activation, W_["AT"], av, ACT.Copy, w=t2)
                    drop(b2, ta)
                    t1 = dve(V.tensor_tensor, W_["BB"], W_["LL"], heads(cm["m1"], 4), ALU.mult, w=t4)
                    tB = dve(V.scalar_tensor_tensor, out=W_["BB"], in0=W_["BB"], scalar=-1.0, in1=heads(ident, 4),
                             op0=ALU.mult, op1=ALU.add, w=t1)
                    t2 = dve(V.tensor_tensor, W_["BT"], W_["LT"], heads(cm["t1"], 4), ALU.mult, w=tl_)
                    tT = dve(V.scalar_tensor_tensor, out=W_["BT"], in0=W_["BT"], scalar=-1.0, in1=heads(ident, 4),
                             op0=ALU.mult, op1=ALU.add, w=t2)
                    msr = [None, None]
                    for n, sz in enumerate((2, 4, 8, 16, 32)):
                        ms = W_[f"MS{n % 2}"]
                        t1 = pool(G.tensor_tensor, ms, W_["LT"], heads(cm[f"t{sz}"], 4), ALU.mult, w=[tl_, msr[n % 2]])
                        b, bw = bank()
                        pv = PS[:, b, :].rearrange("p (h n) -> p h n", h=4)
                        for h in range(4):
                            t2 = pe(E.matmul, pv[:, h, :], ms[:, h, :], W_["BB"][:, h, :], start=True, stop=True,
                                    w=[t1, tB, bw], sig=True)
                        msr[n % 2] = t2
                        fill(1)
                        t3 = act(S.activation, W_["PW"], pv, ACT.Copy, w=t2)
                        drop(b, t3)
                        if sz < 32:
                            b1, bw1 = bank()
                            p1 = PS[:, b1, :].rearrange("p (h n) -> p h n", h=4)
                            for h in range(4):
                                t4 = pe(E.matmul, p1[:, h, :], W_["BT"][:, h, :], W_["PW"][:, h, :], start=True,
                                        stop=True, w=[t3, tT, bw1], sig=True)
                        b2, bw2 = bank()
                        p2 = PS[:, b2, :].rearrange("p (h n) -> p h n", h=4)
                        for h in range(4):
                            t5 = pe(E.matmul, p2[:, h, :], W_["PW"][:, h, :], W_["BT"][:, h, :], start=True,
                                    stop=True, w=[t3, tT, bw2], sig=True)
                        if sz < 32:
                            tB = dve(V.scalar_tensor_tensor, out=W_["BB"], in0=p1, scalar=-1.0, in1=W_["BB"],
                                     op0=ALU.mult, op1=ALU.add, w=t4)
                            drop(b1, tB)
                        tT = dve(V.scalar_tensor_tensor, out=W_["BT"], in0=p2, scalar=-1.0, in1=W_["BT"],
                                 op0=ALU.mult, op1=ALU.add, w=t5)
                        drop(b2, tT)
                        fill(n % 2)
                    b1, bw1 = bank()
                    b2, bw2 = bank()
                    uv = PS[:, b1, :].rearrange("p (h n) -> p h n", h=4)
                    wv = PS[:, b2, :].rearrange("p (h n) -> p h n", h=4)
                    for h in range(4):
                        t1 = pe(E.matmul, uv[:, h, :], W_["BT"][:, h, :], W_["VBT"][:, h, :], start=True, stop=True,
                                w=[tT, t5_, bw1], sig=True)
                    for h in range(4):
                        t2 = pe(E.matmul, wv[:, h, :], W_["KBE"][:, h, :], W_["BT"][:, h, :], start=True, stop=True,
                                w=[t3_, bw2], sig=True)
                    fill(2)
                    tu = act(S.activation, W_["UU"], uv, ACT.Copy, w=t1)
                    drop(b1, tu)
                    tw = act(S.activation, W_["WT"], wv, ACT.Copy, w=t2)
                    drop(b2, tw)
                    bo, bow = bank()
                    for c in range(2):
                        r = slice(64 * c, 64 * c + 64)
                        if sst is None:
                            vn_, tv = flat_["UU"], tu
                        else:
                            b, bw = bank()
                            for h in range(4):
                                t1 = pe(E.matmul, PS[r, b, h * P:h * P + P], W_["WT"][:, h, r], SS[:, h * P:h * P + P],
                                        start=True, stop=True, w=[tw, sst, bw], sig=True)
                            fill(2)
                            vn_ = VN
                            tv = dve(V.scalar_tensor_tensor, out=VN[r, :], in0=PS[r, b, :], scalar=-1.0,
                                     in1=flat_["UU"][r, :], op0=ALU.mult, op1=ALU.add, w=[t1, tu])
                            drop(b, tv)
                        if not (t == 1 and c == 1):
                            b, bw = bank()
                            for h in range(4):
                                t3 = pe(E.matmul, PS[:, b, h * P:h * P + P], W_["KDC"][r, h, :], vn_[r, h * P:h * P + P],
                                        start=True, stop=True, w=[tv, t4_, bw], sig=True)
                        for h in range(4):
                            o_ = PS[r, bo, h * P:h * P + P]
                            if sst is not None:
                                pe(E.matmul, o_, W_["QDT"][:, h, r], SS[:, h * P:h * P + P], start=True, stop=False,
                                   w=[t6_, bow])
                            t2 = pe(E.matmul, o_, W_["AT"][r, h, r], vn_[r, h * P:h * P + P], start=sst is None,
                                    stop=True, w=[ta, tv, bow], sig=True)
                        if not (t == 1 and c == 1):
                            fill(1)
                            if sst is None:
                                sn = dve(V.tensor_copy, SS, PS[:, b, :], w=t3)
                            else:
                                for h in range(4):
                                    hs_ = slice(h * P, h * P + P)
                                    sn = dve(V.scalar_tensor_tensor, out=SS[:, hs_], in0=SS[:, hs_],
                                             scalar=W_["EGR"][:, h, 64 * c + 63:64 * c + 64], in1=PS[:, b, hs_],
                                             op0=ALU.mult, op1=ALU.add, w=[t3, t2, t7])
                            drop(b, sn)
                            sst = sn
                    ov = PS[:, bo, :].rearrange("p (h n) -> p h n", h=4)
                    t1 = act(S.activation, W_["PW"], ov, ACT.Square, w=t2)
                    t1 = dve(V.tensor_reduce, sc["Z1"][:, 0:4], W_["PW"], AX, ALU.add, w=t1)
                    t1 = act(S.activation, sc["Z1"][:, 0:4], sc["Z1"][:, 0:4], ACT.Sqrt, bias=epsc[1e-6],
                             scale=1.0 / 128, w=[t1, epst])
                    t1 = dve(V.reciprocal, sc["Z1"][:, 0:4], sc["Z1"][:, 0:4], w=t1)
                    t1 = dve(V.tensor_tensor, W_["LL"], ov, over(sc["Z1"][:, 0:4], P), ALU.mult, w=t1)
                    drop(bo, t1)
                    t1 = dve(V.tensor_tensor, flat_["LL"], flat_["LL"], Z[:, t, :], ALU.mult, w=[t1, ready["z", t]])
                    fill(4)
                    tk = to_hl(lambda k: W_["LL"][:, k, :], 4, t, *OH["a"], 0, t1)
                    for k, v in tk.items():
                        oa.append(v)
                        ready["o", k, t] = v
                while not state["spent"]:
                    fill(1)


                run(branch("a", *OH["a"], lambda kt, t: ready["o", kt, t]))
                load_gb_after(bgt["a"], bgt["c"], a["ln2_g"][l:l + 1, :], a["ln2_b"][l:l + 1, :])
                mt = {}
                for t in range(2):
                    for k, v in to_hl(lambda k: MG[:, t, k * P:k * P + P], 8, t, XTH, XTL, 0,
                                      mgt[t, 0], mgt[t, 1]).items():
                        mt[k, t] = v
                run(out_rows(a["w_out"][l], 8, XTH, XTL, lambda kt, t: mt[kt, t], 1.0, True))


            def rms_turn(t):
                HN = at(80 * 1024, "HN", [P, 2, D])
                o = 40 + 2 * t
                t1 = act(S.activation, HN[:, t, :], X[:, t, :], ACT.Square, accum_out=ST[:, o:o + 1], w=s["x"][t])
                t2 = power(ST[:, o + 1:o + 2], ST[:, o:o + 1], 1.0 / D, 1e-6, t1, epst)
                t3 = []
                for half in range(2):
                    hs = slice(half * 512, half * 512 + 512)
                    t3.append(dve(V.scalar_tensor_tensor, out=HN[:, t, hs], in0=X[:, t, hs],
                                  scalar=ST[:, o + 1:o + 2], in1=s["rg"][:, hs], op0=ALU.mult, op1=ALU.mult,
                                  w=[t1, t2, s["rgt"]]))
                s["rgr"] = t3

                def turned():
                    for k, v in to_hl(lambda k: HN[:, t, k * P:k * P + P], 8, t, XTH, XTL, 0, *t3).items():
                        s["xt"][k, t] = v

                return turned

            def split_sb(src, hi, lo, w):
                t1 = act(S.activation, hi, src, ACT.Copy, w=w)
                return [t1, dve(V.tensor_tensor, lo, src, hi.bitcast(F), ALU.subtract, w=[w, t1])]

            def mixer_even():
                K = 1024
                YTH = at(0, "YTH", [P, 8, T], R)
                YTL = at(8 * K, "YTL", [P, 8, T], R)
                CG = at(20 * K, "CG", [P, 4, T])
                CV = at(24 * K, "CV", [P, 4, 2 + T])
                VP = at(29 * K, "VP", [P, 4, 16 + T])
                S0 = at(34 * K, "S0", [P, 16 + T])
                S1 = at(36 * K, "S1", [P, 16 + T])
                PL = at(38 * K, "PL", [P, 4, T])
                YC = at(42 * K, "YC", [P, 4, T])
                PW_ = at(46 * K, "PW_", [P, 4, P])
                w = a["w_in_even_2"][0]
                pw = q.dma("pool", "ld1", PW_, a["pool_w_2"][0].rearrange("g c d -> c g d"))
                pads = [pool(G.memset, CV[:, :, 0:2], 0.0), pool(G.memset, VP[:, :, 0:16], 0.0),
                        pool(G.memset, S0[:, 0:16], 0.0), pool(G.memset, S1[:, 0:16], 0.0)]
                tk, yt, todo = {}, {}, []

                def pooled(g):
                    win = 2 ** (g + 1)
                    cur, t1 = VP[:, g, :], [tk[3, g], pads]
                    for n in range(g + 1):
                        st = 2 ** n
                        nx = (S0, S1)[n % 2]
                        t1 = dve(V.tensor_tensor, nx[:, 16:16 + T], cur[:, 16:16 + T], cur[:, 16 - st:16 + T - st],
                                 ALU.add, w=t1)
                        cur = nx
                    c0 = C_CNT + 16 * g
                    t2 = dve(V.scalar_tensor_tensor, out=PL[:, g, 16:T], in0=cur[:, 32:16 + T], scalar=1.0 / win,
                             in1=VP[:, g, 32:16 + T], op0=ALU.mult, op1=ALU.subtract, w=t1)
                    t3 = dve(V.tensor_tensor, PL[:, g, 0:16], cur[:, 16:32], CO[:, c0:c0 + 16], ALU.mult, w=[t1, co])
                    tk["pl", g] = [t2, dve(V.tensor_tensor, PL[:, g, 0:16], PL[:, g, 0:16], VP[:, g, 16:32],
                                           ALU.subtract, w=t3)]

                def mixed(g):
                    b, bw = bank()
                    t4 = pe(E.matmul, PS[:, b, 0:T], PW_[:, g, :], PL[:, g, :], start=True, stop=True,
                            w=[pw, tk["pl", g], bw], sig=True)
                    sc_ = vec["pool_scale"][:, g:g + 1]
                    t5 = act(S.activation, YTH[:, 4 + g, :], PS[:, b, 0:T], ACT.Copy, scale=sc_, w=t4)
                    t6 = dve(V.scalar_tensor_tensor, out=YTL[:, 4 + g, :], in0=PS[:, b, 0:T], scalar=sc_,
                             in1=YTH[:, 4 + g, :].bitcast(F), op0=ALU.mult, op1=ALU.subtract, w=[t4, t5])
                    drop(b, t5, t6)
                    yt[4 + g] = [t5, t6]

                def convolved(j):
                    cw = [vec["conva", k][:, j:j + 1] for k in range(3)]
                    t1 = dve(V.tensor_scalar, YC[:, j, :], CV[:, j, 2:2 + T], cw[2], None, ALU.mult,
                             w=[tk[2, j], pads, vec_tok])
                    for k in range(2):
                        t1 = dve(V.scalar_tensor_tensor, out=YC[:, j, :], in0=CV[:, j, k:k + T], scalar=cw[k],
                                 in1=YC[:, j, :], op0=ALU.mult, op1=ALU.add, w=t1)
                    tk["yc", j] = t1

                RV = at(16 * K, "RV", [P, 2, 512])
                bks = [bank(), bank()]
                run(rows(w, 8, 1536, [(0, 512, bks)], XTH, XTL, xtok, first_n=4))
                for t in range(2):
                    tk["rv", t] = act(S.activation, RV[:, t, :], PS[:, bks[t][0], :], ACT.Copy, w=done[t])
                    drop(bks[t][0], tk["rv", t])

                def channels(t):
                    b, bw = bank()
                    for j in range(4):
                        t1 = pe(E.transpose, PS[:, b, j * P:j * P + P], RV[:, t, j * P:j * P + P], ident,
                                w=[tk["rv", t], bw], sig=True)
                    t1 = act(S.activation, VP[:, :, 16 + t * P:16 + t * P + P],
                             PS[:, b, :].rearrange("p (k n) -> p k n", k=4), ACT.Copy, w=t1)
                    drop(b, t1)
                    for j in range(4):
                        tk.setdefault((3, j), []).append(t1)

                todo += [lambda: channels(0), lambda: channels(1)]
                for j in range(4):
                    todo.append(lambda j=j: pooled(j))
                    if j:
                        todo.append(lambda j=j: mixed(j - 1))
                todo.append(lambda: mixed(3))
                for part in (1, 2, 0):
                    bks = [bank() for _ in range(4)]
                    for _ in cols(w, 512 * part, 4, bks, xtok):
                        for _ in range(2):
                            if todo:
                                todo.pop(0)()
                    for j in range(4):
                        src = PS[:, bks[j][0], 0:T]
                        d_ = done["c", j]
                        if part == 0:
                            t1 = dve(V.tensor_tensor, YC[:, j, :], src, YC[:, j, :], ALU.mult, w=[d_, tk["yc", j]])
                            yt[j] = split_sb(YC[:, j, :], YTH[:, j, :], YTL[:, j, :], t1)
                        elif part == 1:
                            t1 = act(S.activation, CG[:, j, :], src, ACT.Copy, w=d_)
                        elif part == 2:
                            t1 = dve(V.tensor_tensor, CV[:, j, 2:2 + T], src, CG[:, j, :], ALU.mult, w=[d_, tk[1, j]])
                        tk[part, j] = t1
                        drop(bks[j][0], t1)
                        if part == 2:
                            todo.append(lambda j=j: convolved(j))
                run(out_rows(a["w_out_even_2"][0], 8, YTH, YTL, lambda kt, t: yt[kt], 1.0, False, [4, 6, 0, 2]))

            def mixer_odd():
                K = 1024
                W1 = [at(16 * K * n, f"W1{n}", [P, 16, 256]) for n in range(2)]
                OTH, OTL = at(32 * K, "OTH", [P, 8, T], R), at(40 * K, "OTL", [P, 8, T], R)
                RT = [at(48 * K + 3584 * n, f"RT{n}", [P, 14, 64]) for n in range(2)]
                FB = [at((32 + 4 * n) * K, f"FB{n}", [P, 16, 2, 32]) for n in range(2)]
                RO = [at(56 * K + 3584 * n, f"RO{n}", [P, 14, 64]) for n in range(2)]
                TM = [at(int(63.5 * K) + 1792 * n, f"TM{n}", [P, 14, 32]) for n in range(2)]
                GH = at(40 * K, "GH", [P, 2, 2, 2, 4, 32])
                G1 = at(int(83.5 * K), "G1", [64, 2, 256])
                VV = at(int(67.5 * K), "VV", [P, 3, 2, P])
                ZC = at(int(70.5 * K), "ZC", [P, 4, 30 + T])
                ZA = at(int(75.5 * K), "ZA", [P, 4, T])
                SG_ = at(int(79.5 * K), "SGc", [P, 4, T])
                ZN = [at(int((83.5 + 6 * n) * K), f"ZN{n}", [P, 512]) for n in range(2)]
                ZS = at(int(85.5 * K), "ZS", [P, 4, T])
                PRS = at(int(89.5 * K), "PRS", [P, 2, 2, 2, 64])
                W2 = at(int(91.5 * K), "W2", [P, 2, 2, 64])
                VCB = at(int(79.5 * K), "VCB", [P, 4, 2, 64])
                QTT, KTT = at(0, "QTT", [P, 4, T]), at(4 * K, "KTT", [P, 4, T])
                PA = [at((8, 12, 56)[n] * K, f"PA{n}", [P, 1024]) for n in range(3)]
                PB = [at((16 + 4 * n) * K, f"PB{n}", [P, 1024]) for n in range(2)]
                KD2 = at(44 * K, "KD2", [P, 2, 4, 2, 64])
                KCN = at(28 * K, "KCN", [P, 2, 2, 64])
                KCT = at(29 * K, "KCT", [P, 2, 32])
                PTC = at(int(81.5 * K), "PTC", [P, 4, P])
                PCMS = [at(48 * K + 512 * n, f"PCM{n}", [P, 4, 32]) for n in range(2)]
                NW = GB[:, 1, 0:768].rearrange("p (h d) -> p h d", d=64)
                GA = SX[:, 256:304].rearrange("p (t h k) -> p t h k", t=2, k=3)
                MS = SX[:, 304:336]
                w = a["w_in_odd_2"][0]
                w1 = {}
                parts = [(n, c) for n in range(2) for c in range(4)]

                def load_w1():
                    if parts:
                        n, c = parts.pop(0)
                        w1[n] = q.dma("pool", f"ld{1 + n}", W1[n][:, 4 * c:4 * c + 4],
                                      a["cmp_w1_2"][0, n, 512 * c:512 * c + 512].rearrange("(j p) n -> p j n", p=P),
                                      s["x"][1])

                load_w1()
                w2 = q.dma("pool", "ld3", W2, a["cmp_w2_2"][0].rearrange("k (m p) d -> p k m d", p=P), s["x"][1])
                zp = pool(G.memset, ZC[:, :, 0:30], 0.0, w=s["x"][1])
                nw = [pool(G.tensor_copy, NW[:, 0:8, :], heads(smv["q_norm"], 8), w=[sm_tok]),
                      pool(G.tensor_copy, NW[:, 8:10, :], heads(smv["k_norm"][:, 0:64], 2), w=sm_tok),
                      pool(G.tensor_copy, NW[:, 10:12, :], heads(smv["k_norm"][:, 64:128], 2), w=sm_tok)]
                zc, zt, todo = [], {}, []

                def conv(k, j):
                    cw = vec["dw", k][:, j:j + 1]
                    if k == 0:
                        zt[j] = dve(V.tensor_scalar, ZA[:, j, :], ZC[:, j, 0:T], cw,
                                    vec["conf_b"][:, j:j + 1], ALU.mult, ALU.add, w=[zc, zp, vec_tok])
                    else:
                        zt[j] = dve(V.scalar_tensor_tensor, out=ZA[:, j, :], in0=ZC[:, j, k:k + T], scalar=cw,
                                    in1=ZA[:, j, :], op0=ALU.mult, op1=ALU.add, w=zt[j])

                def taps(n):
                    for k, j in todo[:n]:
                        conv(k, j)
                    del todo[:n]

                DG = [at(24 * K + 512 * n, f"DG{n}", [P, P]) for n in range(8)]
                used = {}

                def conv_pe():
                    b, bw = bank()
                    for j in range(2):
                        for k in range(31):
                            n = 31 * j + k
                            dg = pool(G.tensor_tensor, DG[n % 8], ident, vec["dw", k][:, j:j + 1].to_broadcast([P, P]),
                                      ALU.mult, w=[thid, used.get(n - 8), vec_tok])
                            used[n] = pe(E.matmul, PS[:, b, j * T:j * T + T], DG[n % 8], ZC[:, j, k:k + T],
                                         start=k == 0, stop=k == 30, w=[dg, zc, zp, bw], sig=True)
                            yield
                    for j in range(2):
                        zt[j] = act(S.activation, ZA[:, j, :], PS[:, b, j * T:j * T + T], ACT.Identity,
                                    bias=vec["conf_b"][:, j:j + 1], w=[used[n], zc, vec_tok])
                    drop(b, zt[1])

                cpe = conv_pe()

                def fill(n):
                    for _ in range(n):
                        next(cpe, None)

                def project(c0, wd, first_n=2):
                    bks = [bank(), bank()]
                    run(rows(w, 8, c0, [(0, wd, bks)], XTH, XTL, xtok, first_n=first_n))
                    return bks

                rt = {0: [], 1: []}
                vt = {0: [], 1: []}
                ro = {0: [], 1: []}
                bks = project(512, 512, 4)
                for t in range(2):
                    pv = PS[:, bks[t][0], :].rearrange("p (x g d) -> p x g d", x=4, d=64)
                    t1 = act(S.activation, RT[t][:, 12:14, :], pv[:, 0], ACT.Copy, w=done[t])
                    t2 = act(S.activation, VV[:, 2, t, :], PS[:, bks[t][0], 128:256], ACT.Copy, w=done[t])
                    t3 = act(S.activation, RT[t][:, 8:10, :], pv[:, 2], ACT.Copy, w=done[t])
                    t4 = act(S.activation, VV[:, 0, t, :], PS[:, bks[t][0], 384:512], ACT.Copy, w=done[t])
                    drop(bks[t][0], t4)
                    rt[t] += [t1, t3]
                    vt[t] += [t2, t4]
                load_w1()
                bks = project(1024, 280)
                load_w1()
                gt_ = []
                for t in range(2):
                    t1 = act(S.activation, RT[t][:, 10:12, :],
                             PS[:, bks[t][0], 0:128].rearrange("p (g d) -> p g d", d=64), ACT.Copy, w=done[t])
                    t2 = act(S.activation, VV[:, 1, t, :], PS[:, bks[t][0], 128:256], ACT.Copy, w=done[t])
                    t3 = act(S.activation, SX[:, 256 + 24 * t:280 + 24 * t], PS[:, bks[t][0], 256:280], ACT.Sigmoid,
                             w=done[t])
                    drop(bks[t][0], t3)
                    rt[t].append(t1)
                    vt[t].append(t2)
                    gt_.append(t3)

                def rotate(t, h0, h1, normed, *w):
                    n, m = h1 - h0, normed - h0
                    xn, rm = RT[t][:, h0:normed, :], RO[t][:, h0:normed, :]
                    t1 = act(S.activation, rm, xn, ACT.Square, w=w)
                    ms = MS[:, 12 * t + h0:12 * t + normed]
                    t1 = dve(V.tensor_reduce, ms, rm, AX, ALU.add, w=t1)
                    t1 = act(S.activation, ms, ms, ACT.Sqrt, bias=epsc[1e-6], scale=1.0 / 64, w=[t1, epst])
                    t1 = dve(V.reciprocal, ms, ms, w=t1)
                    t1 = dve(V.tensor_tensor, xn, xn, over(ms, 64), ALU.mult, w=t1)
                    t1 = dve(V.tensor_tensor, xn, xn, NW[:, h0:normed, :], ALU.mult, w=[t1, nw, w])
                    co_, si_ = (heads(CO[:, c_ + 32 * t:c_ + 32 * t + 32], n) for c_ in (C_COS, C_SIN))
                    x1, x2 = RT[t][:, h0:h1, 0:32], RT[t][:, h0:h1, 32:64]
                    y1, y2 = RO[t][:, h0:h1, 0:32], RO[t][:, h0:h1, 32:64]
                    ta, tb = TM[0][:, h0:h1], TM[1][:, h0:h1]
                    t2 = pool(G.tensor_tensor, ta, x2, si_, ALU.mult, w=[t1, co, ro[0]])
                    t3 = dve(V.tensor_tensor, y1, x1, co_, ALU.mult, w=t1)
                    t5 = pool(G.tensor_tensor, tb, x1, si_, ALU.mult, w=[t1, ro[0]])
                    t4 = dve(V.tensor_tensor, y1, y1, ta, ALU.subtract, w=[t2, t3])
                    t6 = dve(V.tensor_tensor, y2, x2, co_, ALU.mult, w=t1)
                    t7 = dve(V.tensor_tensor, y2, y2, tb, ALU.add, w=[t5, t6])
                    ro[t] += [t4, t7]
                    return [t4, t7]

                wr, kd, rd, fm = [], [], [], []

                def keys(t):
                    tr = rotate(t, 8, 14, 12, rt[t])
                    for n, src in ((0, RO[t][:, 12:14, :].rearrange("p g d -> p (g d)")), (1, VV[:, 2, t, :])):
                        o = 1536 + n * T * P + t * P * P
                        wr.append(q.dma("pool", f"ld{4 + 2 * t + n}", scratch[o:o + P * P].rearrange("(p n) -> p n", p=P),
                                        src, tr, vt[t]))

                def windows():
                    for n in range(2):
                        rd.append([q.dma("pool", f"ld{8 + 2 * n + g}", PRS[:, n, g],
                                         bass.AP(scratch.tensor, 1536 + n * T * P + 64 * g, [[2 * P, P], [P, 2], [1, 64]]),
                                         wr)
                                   for g in range(2)])
                    for n in range(2):
                        fm.append(pool(G.memset, FB[n], 0.0, w=s["x"][1]))
                    for t in range(2):
                        kd.append(pool(G.tensor_copy, KD2[:, t],
                                       RO[t][:, 8:12, :].unsqueeze(2).to_broadcast([P, 4, 2, 64]), w=ro[t]))

                early = [lambda: keys(0), lambda: keys(1), windows]
                for part, c0 in ((1, 1816), (0, 1304)):
                    bks = [bank() for _ in range(4)]
                    for _ in cols(w, c0, 4, bks, xtok):
                        load_w1()
                        if early:
                            early.pop(0)()
                    for j in range(4):
                        src = PS[:, bks[j][0], 0:T]
                        if part == 1:
                            t1 = act(S.activation, SG_[:, j, :], src, ACT.Sigmoid, w=done["c", j])
                            sg = t1
                        else:
                            t1 = dve(V.tensor_tensor, ZC[:, j, 30:30 + T], src, SG_[:, j, :], ALU.mult,
                                     w=[done["c", j], sg, zp])
                            zc.append(t1)
                        drop(bks[j][0], t1)
                vz = pool(G.memset, VCB, 0.0, w=zc)
                todo += [(k, j) for k in range(31) for j in (2, 3)]
                fb = []

                def paired(n):
                    b, bw = bank()
                    for g in range(2):
                        t1 = pe(E.transpose, PS[:, b, g * P:g * P + P], PRS[:, n, g].rearrange("p b d -> p (b d)"),
                                ident, w=[rd[n], bw], sig=True)
                    base_ = PS[:, b, 0:256]
                    src = bass.AP(base_.tensor, base_.offset, [list(base_.ap[0]), [1, 16], [P, 2], [8, 15]])
                    po = vec["cmp_pos"][:, 16 * n:16 * n + 16].unsqueeze(2).unsqueeze(3).to_broadcast([P, 16, 2, 15])
                    t2 = dve(V.tensor_tensor, FB[n][:, :, :, 0:15], src, po, ALU.add, w=[t1, fm[n], vec_tok])
                    drop(b, t2)
                    fb.append(t2)

                bks = [bank(), bank()]
                for n, _ in enumerate(rows(w, 8, 0, [(0, 512, bks)], XTH, XTL, xtok)):
                    if n in (4, 6):
                        paired(n // 2 - 2)
                    taps(3)
                rq = []
                for t in range(2):
                    rq.append(act(S.activation, RT[t][:, 0:8, :], PS[:, bks[t][0], :].rearrange("p (h d) -> p h d", d=64),
                                  ACT.Copy, w=done[t]))
                    drop(bks[t][0], rq[t])
                for t in range(2):
                    rotate(t, 0, 8, 8, rq[t])
                    taps(9 - 9 * t)
                g1 = []
                for n in range(2):
                    b, bw = bank()
                    for j in range(16):
                        t1 = pe(E.matmul, PS[0:64, b, 0:256], FB[n][:, j].rearrange("p g n -> p (g n)"),
                                W1[n][:, j, :], start=j == 0, stop=j == 15, w=[fb[n], w1[n], bw], sig=j == 15)
                    g1.append(act(S.activation, G1[:, n, :], PS[0:64, b, 0:256], ACT.Gelu_apprx_tanh, w=t1))
                    drop(b, g1[n])
                thid = t1
                qkt = []

                def features(t, src, dst, wt):
                    b, bw = bank()
                    for k in range(4):
                        t1 = pe(E.transpose, PS[:, b, k * P:k * P + P], src(k), ident, w=[wt, bw], sig=True)
                    t2 = act(S.activation, dst[:, :, t * P:t * P + P], PS[:, b, :].rearrange("p (k n) -> p k n", k=4),
                             ACT.Copy, w=[t1, thid])
                    drop(b, t2)
                    qkt.append(t2)

                b, bw = bank()
                for n in range(2):
                    for m in range(2):
                        c0 = 64 * (2 * n + m)
                        t1 = pe(E.transpose, PS[:, b, c0:c0 + 64], G1[:, n, m * P:m * P + P], ident[0:64, 0:64],
                                w=[g1[n], bw], sig=True)
                gh = [act(S.activation, GH[:, n, m],
                          PS[:, b, 64 * (2 * n + m):64 * (2 * n + m) + 64].rearrange("p (g i) -> p g i", g=2)
                          .unsqueeze(2).to_broadcast([P, 2, 4, 32]), ACT.Copy, w=t1)
                      for n in range(2) for m in range(2)]
                drop(b, gh)
                for t in range(2):
                    features(t, lambda k: KD2[:, t, k].rearrange("p c d -> p (c d)"), KTT, kd[t])
                b, bw = bank()
                for n in range(2):
                    for g in range(2):
                        for m in range(2):
                            t1 = pe(E.matmul, PS[:, b, (2 * n + g) * 64:(2 * n + g) * 64 + 64],
                                    GH[:, n, m, g].rearrange("p c n -> p (c n)"), W2[:, n, m, :], start=m == 0,
                                    stop=m == 1, w=[gh, w2, bw], sig=m == 1)
                load_rg(a["norm_ffn_2"][1:2, :], 52, ro[0], ro[1])
                vcc = []
                for i in range(4):
                    r = slice(32 * i, 32 * i + 32)
                    t2 = act(S.activation, VCB[r, i], PS[r, b, 128:256].rearrange("p (g d) -> p g d", g=2), ACT.Copy,
                             w=[t1, vz])
                    vcc.append(t2)
                kr = PS[:, b, 0:128].rearrange("p (g d) -> p g d", g=2)
                t3 = act(S.activation, KCN[:, :, 0, :], kr, ACT.Square, w=[t1, thid])
                ms = MS[:, 24:26]
                t3 = dve(V.tensor_reduce, ms, KCN[:, :, 0, :], AX, ALU.add, w=t3)
                t3 = act(S.activation, ms, ms, ACT.Sqrt, bias=epsc[1e-6], scale=1.0 / 64, w=[t3, epst])
                t3 = dve(V.reciprocal, ms, ms, w=t3)
                t4 = dve(V.tensor_tensor, KCN[:, :, 0, :], kr, over(ms, 64), ALU.mult, w=[t3, t1])
                drop(b, t2, t4)
                t4 = dve(V.tensor_tensor, KCN[:, :, 0, :], KCN[:, :, 0, :], heads(smv["k_norm"][:, 128:192], 2),
                         ALU.mult, w=[t4, sm_tok])
                t4 = dve(V.tensor_copy, KCN[:, :, 1, :], KCN[:, :, 0, :], w=t4)
                b, bw = bank()
                for g in range(2):
                    t1 = pe(E.transpose, PS[:, b, g * P:g * P + P], KCN[:, g].rearrange("p c d -> p (c d)"), ident,
                            w=[t4, bw], sig=True)
                kct = act(S.activation, KCT, PS[:, b, 0:256].rearrange("p (g n) -> p g n", g=2)[:, :, 0:32], ACT.Copy,
                          w=t1)
                drop(b, kct)
                taps(12)
                for t in range(2):
                    features(t, lambda k: RO[t][:, 2 * k:2 * k + 2, :].rearrange("p h d -> p (h d)"), QTT, ro[t])
                ptc = {}
                pcr = {}

                def compressed(n, t, par):
                    PCM = PCMS[n % 2]
                    r = slice(64 * par, 64 * par + 64)
                    b, bw = bank()
                    for i in range(4):
                        t1 = pe(E.matmul, PS[:, b, 32 * i:32 * i + 32], QTT[r, i, t * P:t * P + P],
                                KCT[r, i // 2, :], start=True, stop=True, w=[qkt, kct, bw], sig=True)
                    sv = PS[:, b, 0:128].rearrange("p (h n) -> p h n", h=4)
                    t2 = dve(V.tensor_tensor, PCM, sv, heads(CO[:, C_CMB + 32 * t:C_CMB + 32 * t + 32], 4), ALU.add,
                             w=[t1, pcr.get(n - 2), ro[0], ro[1], co])
                    drop(b, t2)
                    o = 144 + 8 * (n % 2)
                    m_, su = SX[:, o:o + 4], SX[:, o + 4:o + 8]
                    t3 = dve(V.tensor_reduce, m_, PCM, AX, ALU.max, w=t2)
                    t3 = dve(V.tensor_scalar, m_, m_, -0.125, None, ALU.mult, w=t3)
                    for i in range(4):
                        t4 = act(S.activation, PCM[:, i, :], PCM[:, i, :], ACT.Exp, bias=m_[:, i:i + 1], scale=0.125, w=t3)
                    yield
                    t4 = dve(V.tensor_tensor, PCM, PCM, heads(CO[:, C_CM1 + 32 * t:C_CM1 + 32 * t + 32], 4), ALU.mult, w=t4)
                    t5 = dve(V.tensor_reduce, su, PCM, AX, ALU.add, w=t4)
                    t5 = dve(V.tensor_scalar, su, su, 1e-30, None, ALU.max, w=t5)
                    t5 = dve(V.reciprocal, su, su, w=t5)
                    t5 = dve(V.tensor_tensor, su, su, GA[:, t, par:8:2, 0], ALU.mult, w=[t5, gt_])
                    t5 = dve(V.tensor_tensor, PCM, PCM, over(su, 32), ALU.mult, w=t5)
                    yield
                    b, bw = bank()
                    t6 = pe(E.transpose, PS[:, b, 0:P], PCM.rearrange("p h n -> p (h n)"), ident, w=[t5, bw], sig=True)
                    t7 = act(S.activation, PTC[:, n, :], PS[:, b, 0:P], ACT.Copy, w=t6)
                    drop(b, t7)
                    pcr[n] = t6
                    ptc[t, par] = (n, t7)
                    yield

                ot = {0: [], 1: []}

                def item(t, hs, k):
                    par = hs[0] % 2
                    r = slice(64 * par, 64 * par + 64)
                    nk = (t + 1) * P
                    pv = PA[k % 3][:, 0:4 * nk].rearrange("p (x h n) -> p x h n", x=2, h=2)
                    rcs = []
                    bb = {}
                    for x in range(2):
                        if t == 1 or x == 0:
                            bb[x] = bank()
                        b, bw = bb[x] if x in bb else bb[0]
                        for n, h in enumerate(hs):
                            c0 = (0 if t else 2 * x * P) + n * nk
                            o_ = PS[:, b, c0:c0 + nk]
                            pe(E.matmul, o_, QTT[r, h // 2, t * P:t * P + P], KTT[r, 2 * x + h // 4, 0:nk],
                               start=True, stop=t == 1, w=[qkt, bw], skip_group_check=True)
                            t1 = pe(E.matmul, o_[:, t * P:t * P + P], ident, cm["causal"], start=False, stop=True,
                                    sig=True, skip_group_check=True)
                        bb["t", x] = t1
                    if t == 0:
                        views = [(PS[:, bb[0][0], :].rearrange("p (h n) -> p h n", h=4),
                                  pv.rearrange("p x h n -> p (x h) n"), 4, [bb["t", 0], bb["t", 1]], 0)]
                    else:
                        views = [(PS[:, bb[x][0], :].rearrange("p (h n) -> p h n", h=2), pv[:, x], 2, bb["t", x], x)
                                 for x in range(2)]
                    tn = []
                    sm_ = [softmax_start(sv, nh, dst, 2 * (k % 3) + i, 0.125, wt)
                           for i, (sv, dst, nh, wt, x) in enumerate(views)]
                    taps(3)
                    for i, (sv, dst, nh, wt, x) in enumerate(views):
                        rc, te, tr = softmax_end(sm_[i])
                        drop(bb[x][0], te)
                        g_ = GA[:, t, hs[0]:hs[0] + 3:2, :]
                        for x_ in ((0, 1) if t == 0 else (x,)):
                            rv = rc[:, 2 * x_:2 * x_ + 2] if t == 0 else rc
                            tr = dve(V.tensor_tensor, rv, rv, g_[:, :, 1 + x_], ALU.mult, w=[tr, gt_])
                        tn.append(dve(V.tensor_tensor, dst, dst, over(rc, nk), ALU.mult, w=tr))
                    yield
                    yield
                    pt = PB[k % 2]
                    tp = []
                    for x in range(2):
                        if t == 1 or x == 0:
                            b, bw = bank()
                            i = 0
                        for n in range(2):
                            for kt in range(t + 1):
                                t1 = pe(E.transpose, PS[:, b, i * P:i * P + P], pv[:, x, n, kt * P:kt * P + P], ident,
                                        w=[tn, bw], sig=True)
                                i += 1
                        if i == 4:
                            x0 = x if t == 1 else 0
                            tp.append(act(S.activation, pt[:, x0 * 512:x0 * 512 + 512], PS[:, b, :], ACT.Copy, w=t1))
                            drop(b, tp[-1])
                    yield
                    nc_, tc = ptc[t, par]
                    b, bw = bank()
                    for n, h in enumerate(hs):
                        o_ = PS[r, b, n * P:n * P + P]
                        g = h // 4
                        for x in range(2):
                            for kt in range(t + 1):
                                c0 = (x * 2 * (t + 1) + n * (t + 1) + kt) * P
                                pe(E.matmul, o_, VV[:, x, kt, 64 * g:64 * g + 64], pt[:, c0:c0 + P],
                                   start=x == 0 and kt == 0, stop=False, w=[tp, vt[0], vt[1], bw])
                        i = h // 2
                        t1 = pe(E.matmul, o_, VCB[:, i, g, :], PTC[:, nc_, :],
                                start=False, stop=True, w=[tc, vcc], sig=True)
                    ot[t].append(split_out(b, 64 * par, 64, 2, hs[0] // 2, t, OTH, OTL, t1))
                    yield

                items = [(t, hs) for t in range(2) for hs in ([0, 2], [4, 6], [1, 3], [5, 7])]
                small_ = [compressed(n, t, par) for n, (t, par) in enumerate(((0, 0), (0, 1), (1, 0), (1, 1)))]
                big_ = [item(t, hs, k) for k, (t, hs) in enumerate(items)]
                cf = {}

                def conformer(t):
                    if t == 0:
                        taps(31)
                        run(cpe)
                    b, bw = bank()
                    for j in range(4):
                        t1 = pe(E.transpose, PS[:, b, j * P:j * P + P], ZA[:, j, t * P:t * P + P], ident,
                                w=[zt[j], bw], sig=True)
                    o = 44 + 8 * t
                    t2 = dve(V.bn_stats, ST[:, o:o + 6], PS[:, b, :], w=t1)
                    t2 = dve(V.bn_aggr, ST[:, o + 6:o + 8], ST[:, o:o + 6], w=t2)
                    t3 = power(ST[:, o:o + 1], ST[:, o + 7:o + 8], 1.0, 1e-6, t2, epst)
                    t4 = dve(V.tensor_scalar, ZN[t], PS[:, b, :], ST[:, o + 6:o + 7], ST[:, o:o + 1],
                             ALU.subtract, ALU.mult, w=[t2, t3])
                    drop(b, t4)
                    yield
                    b, bw = bank()
                    for j in range(4):
                        t1 = pe(E.transpose, PS[:, b, j * P:j * P + P], ZN[t][:, j * P:j * P + P], ident,
                                w=[t4, bw], sig=True)
                    for j in range(4):
                        t5 = act(S.activation, ZS[:, j, t * P:t * P + P], PS[:, b, j * P:j * P + P], ACT.Silu,
                                 bias=vec["conf_lb"][:, j:j + 1], scale=vec["conf_lg"][:, j:j + 1], w=[t1, vec_tok])
                    drop(b, t5)
                    ts = slice(t * P, t * P + P)
                    cf[t] = split_sb(ZS[:, :, ts], OTH[:, 4:8, ts], OTL[:, 4:8, ts], t5)
                    yield

                pipeline([small_[0], big_[0], small_[1], big_[1], small_[2], big_[2], small_[3]] + big_[3:7]
                         + [conformer(0), conformer(1)] + big_[7:], fill, 7)
                run(out_rows(a["w_out_odd_2"][0], 8, OTH, OTL, lambda kt, t: ot[t] if kt < 4 else cf[t], 1.0, False,
                             [4, 6, 0, 2]))

            YH = PP = PT = SC = None

            def store():
                toks = [q.dma("sp", "st", out[0, t * P:(t + 1) * P, :], X[:, t, :], s["x"][t]) for t in range(2)]
                q.wait("sp", toks[-1])

            for l in range(2):
                load_gb(a["ln1_g"][l:l + 1, :], a["ln1_b"][l:l + 1, :])
                if l == 0:
                    s["next"] = "x"
                    x_turn(0)
                    x_turn(1)
                s["next"] = "x"
                ffn(a["w_ff1_in"][l], a["w_ff1_in"][l], a["w_ff1_out"][l], 0, 4096, 4096, xtok, 0.5, True, f"a{l}")
                s["next"] = "x"
                mixer1(l)
                load_gb(a["ln3_g"][l:l + 1, :], a["ln3_b"][l:l + 1, :])
                s["next"] = "x" if l == 0 else "rms"
                if l == 1:
                    load_rg(a["norm_mix_2"][0:1, :], 76, s["x"])
                ffn(a["w_ff2_in"][l], a["w_ff2_in"][l], a["w_ff2_out"][l], 0, 4096, 4096, xtok, 0.5, True, f"c{l}")
            for i in range(2):
                s["next"] = "rms"
                if i == 0:
                    load_rg(a["norm_ffn_2"][0:1, :], 76)
                (mixer_even, mixer_odd)[i]()
                s["next"] = "rms" if i == 0 else ""
                if i == 0:
                    load_rg(a["norm_mix_2"][1:2, :], 76)
                ffn(a["ffn_gate_2"][i], a["ffn_up_2"][i], a["ffn_down_2"][i], 0, 0, 2816, xtok, 1.0, False, "g")
            store()
            return q

        trace(None)
        made_units = list(record)
        q = trace(made_units)

        block = ctx.enter_context(nc.Block())

        @block.sync
        def _(e):
            q.play("sp", e)

        @block.gpsimd
        def _(e):
            q.play("pool", e)

        @block.scalar
        def _(e):
            q.play("act", e)

        @block.vector
        def _(e):
            q.play("dve", e)

        @block.tensor
        def _(e):
            q.play("pe", e)


_INS = ['x', 'ln1_g', 'ln1_b', 'w_ff1_in', 'w_ff1_out', 'w_in', 'b_in', 'conv_w', 'a_log', 'dt_bias',
        'gdn_norm_g', 'rel_bias', 'sinks', 'w_gate', 'b_gate', 'w_br_a', 'w_br_b', 'w_br_c', 'w_out',
        'ln2_g', 'ln2_b', 'w_ff2_in', 'w_ff2_out', 'ln3_g', 'ln3_b', 'norm_mix_2', 'norm_ffn_2',
        'ffn_gate_2', 'ffn_up_2', 'ffn_down_2', 'w_in_even_2', 'conv_a_2', 'pool_w_2', 'pool_scale_2',
        'w_out_even_2', 'w_in_odd_2', 'q_norm_2', 'k_norm_2', 'cmp_pos_2', 'cmp_w1_2', 'cmp_w2_2',
        'conf_dw_2', 'conf_dw_b_2', 'conf_ln_g_2', 'conf_ln_b_2', 'w_out_odd_2']


def kernel(**inputs):
    import numpy as _np
    import concourse.bacc as _bacc
    from concourse import mybir as _mybir
    from concourse.bass_utils import run_bass_kernel_spmd as _run

    nc = _bacc.Bacc("TRN2", target_bir_lowering=False, num_devices=1)
    arrays, aps = {}, {}
    for name in _INS + ["consts"]:
        v = shape_constants() if name == "consts" else _np.ascontiguousarray(inputs[name])
        arrays[f"in_{name}"] = v
        aps[name] = nc.dram_tensor(f"in_{name}", v.shape, _mybir.dt.from_np(v.dtype), kind="ExternalInput").ap()
    o = nc.dram_tensor("out_0", (1, T, D), _mybir.dt.float32, kind="ExternalOutput").ap()
    build(nc, aps, o)
    r = _run(nc, [arrays], core_ids=[0])
    return r.results[0]["out_0"]
```
